# Optimizing a Trainium2 kernel written in Bass

```python
import jax, jax.numpy as jnp
from jax import lax
import numpy as np
import math

D_MODEL = 1024
BATCH = 1
SEQ = 256
DEPTH = 2

MEM_LEN = 256
MLA_HEADS = 8
MLA_NOPE = 64
MLA_ROPE = 32
MLA_V = 64
Q_LORA = 384
KV_LORA = 256
ROPE_THETA = 10000.0
Q_BLOCK = 128
HG_HEADS = 4
HG_KDIM = 128
HG_VDIM = 128
HG_CHUNK = 64
MEM_HEADS = 4
MEM_HDIM = 128
D_FF = 2816
N_BRANCH = 3
NORM_EPS = 1e-6

MLA_QK = MLA_NOPE + MLA_ROPE
HG_K = HG_HEADS * HG_KDIM
HG_V = HG_HEADS * HG_VDIM
MEM_W = MEM_HEADS * MEM_HDIM
IN_SPLITS = (Q_LORA, KV_LORA, MLA_ROPE, HG_K, HG_K, HG_V, HG_V, MEM_W, N_BRANCH * D_MODEL)
D_IN = sum(IN_SPLITS)


def rmsnorm(x, g):
    xf = x.astype(jnp.float32)
    y = xf * lax.rsqrt(jnp.mean(xf * xf, axis=-1, keepdims=True) + NORM_EPS)
    return (y * g.astype(jnp.float32)).astype(x.dtype)

def swiglu(x, w_in, w_out):
    a, b = jnp.split(x @ w_in, 2, axis=-1)
    return (jax.nn.silu(a) * b) @ w_out

def split_sizes(z, sizes):
    idx = [int(v) for v in np.cumsum(sizes)[:-1]]
    return jnp.split(z, idx, axis=-1)

def apply_rope(t, cos, sin):
    tf = t.astype(jnp.float32)
    t1, t2 = jnp.split(tf, 2, axis=-1)
    out = jnp.concatenate([t1 * cos - t2 * sin, t2 * cos + t1 * sin], axis=-1)
    return out.astype(t.dtype)

def causal_mla_attention(q_nope, q_rope, k_nope, k_rope, v):
    B, S, H, _ = q_nope.shape
    nb = S // Q_BLOCK
    scale = MLA_QK ** -0.5
    k_pos = jnp.arange(S)

    def to_blocks(t):
        return jnp.moveaxis(t.reshape((B, nb, Q_BLOCK) + t.shape[2:]), 1, 0)

    def block(args):
        i, qn, qr = args
        s = jnp.einsum('bqhd,bkhd->bhqk', qn, k_nope) + jnp.einsum('bqhd,bkd->bhqk', qr, k_rope)
        s = s.astype(jnp.float32) * scale
        q_pos = i * Q_BLOCK + jnp.arange(Q_BLOCK)
        s = jnp.where(q_pos[:, None] >= k_pos[None, :], s, -jnp.inf)
        p = jax.nn.softmax(s, axis=-1).astype(v.dtype)
        return jnp.einsum('bhqk,bkhd->bqhd', p, v)

    o = lax.map(block, (jnp.arange(nb), to_blocks(q_nope), to_blocks(q_rope)))
    return jnp.moveaxis(o, 0, 1).reshape(B, S, H * MLA_V)

def mla_branch(c_q, c_kv, k_r, cos, sin, q_norm_g, kv_norm_g, w_uq, w_uk, w_uv):
    B, S, _ = c_q.shape
    q = (rmsnorm(c_q, q_norm_g) @ w_uq).reshape(B, S, MLA_HEADS, MLA_QK)
    q_nope = q[..., :MLA_NOPE]
    q_rope = apply_rope(q[..., MLA_NOPE:], cos[:, :, None, :], sin[:, :, None, :])
    k_rope = apply_rope(k_r, cos, sin)
    ckv = rmsnorm(c_kv, kv_norm_g)
    k_nope = (ckv @ w_uk).reshape(B, S, MLA_HEADS, MLA_NOPE)
    v = (ckv @ w_uv).reshape(B, S, MLA_HEADS, MLA_V)
    return causal_mla_attention(q_nope, q_rope, k_nope, k_rope, v)

def chunk_gated_recurrence(q, k, v, g):
    B, S, H, K = q.shape
    V = v.shape[-1]
    n = S // HG_CHUNK
    causal = jnp.tril(jnp.ones((HG_CHUNK, HG_CHUNK), dtype=bool))

    def chunks(t):
        return t.reshape(B, n, HG_CHUNK, H, t.shape[-1]).transpose(1, 0, 3, 2, 4)

    def step(state, inp):
        qc, kc, vc, gc = inp
        G = jnp.cumsum(gc, axis=2)
        o_inter = jnp.einsum('bhck,bhkv->bhcv', qc * jnp.exp(G), state)
        diff = G[:, :, :, None, :] - G[:, :, None, :, :]
        decay = jnp.exp(jnp.where(causal[:, :, None], diff, -jnp.inf))
        A = jnp.einsum('bhtsk,bhsk->bhts', qc[:, :, :, None, :] * decay, kc)
        o_intra = jnp.einsum('bhts,bhsv->bhtv', A, vc)
        G_last = G[:, :, -1:, :]
        new_state = jnp.exp(G_last[:, :, 0, :])[..., None] * state + jnp.einsum(
            'bhck,bhcv->bhkv', kc * jnp.exp(G_last - G), vc)
        return new_state, o_inter + o_intra

    s0 = jnp.zeros((B, H, K, V), jnp.float32)
    _, o = lax.scan(step, s0, (chunks(q), chunks(k), chunks(v), chunks(g)))
    return o.transpose(1, 0, 3, 2, 4).reshape(B, S, H, V)

def hgrn2_branch(q, f_logit, i_in, gate, lb, o_norm_g):
    B, S, _ = q.shape
    dt = q.dtype
    qf = jax.nn.silu(q.astype(jnp.float32)).reshape(B, S, HG_HEADS, HG_KDIM)
    z = f_logit.astype(jnp.float32)
    g = jnp.logaddexp(jnp.log(lb), jnp.log1p(-lb) + jax.nn.log_sigmoid(z))
    k = (1.0 - lb) * jax.nn.sigmoid(-z)
    g = g.reshape(B, S, HG_HEADS, HG_KDIM)
    k = k.reshape(B, S, HG_HEADS, HG_KDIM)
    v = i_in.astype(jnp.float32).reshape(B, S, HG_HEADS, HG_VDIM)
    o = chunk_gated_recurrence(qf, k, v, g)
    o = rmsnorm(o, o_norm_g) * jax.nn.silu(gate.astype(jnp.float32).reshape(B, S, HG_HEADS, HG_VDIM))
    return o.reshape(B, S, HG_V).astype(dt)

def memory_branch(q, mem_n, w_mem_kv):
    B, S, _ = q.shape
    M = mem_n.shape[1]
    qh = q.reshape(B, S, MEM_HEADS, MEM_HDIM)
    k, v = jnp.split(mem_n @ w_mem_kv, 2, axis=-1)
    k = k.reshape(B, M, MEM_HEADS, MEM_HDIM)
    v = v.reshape(B, M, MEM_HEADS, MEM_HDIM)
    s = jnp.einsum('bqhd,bmhd->bhqm', qh, k).astype(jnp.float32) * (MEM_HDIM ** -0.5)
    p = jax.nn.softmax(s, axis=-1).astype(v.dtype)
    return jnp.einsum('bhqm,bmhd->bqhd', p, v).reshape(B, S, MEM_W)

def first_inputs(seed: int = 0) -> dict:
    key = jax.random.key(seed)
    ks = jax.random.split(key, 32)
    f32 = jnp.float32

    def w(k, shape, fan_in):
        return jax.random.normal(k, shape, f32) * (fan_in ** -0.5)

    def gain(k, shape):
        return 1.0 + 0.02 * jax.random.normal(k, shape, f32)

    x = jax.random.normal(ks[0], (BATCH, SEQ, D_MODEL), f32)
    mem = jax.random.normal(ks[1], (BATCH, MEM_LEN, D_MODEL), f32)
    offsets = jax.random.randint(ks[2], (BATCH, 1), 0, 1024, dtype=jnp.int32)
    positions = offsets + jnp.arange(SEQ, dtype=jnp.int32)[None, :]
    return {
        "x": x,
        "mem": mem,
        "positions": positions,
        "ffn1_norm": gain(ks[3], (DEPTH, D_MODEL)),
        "w_ffn1_in": w(ks[4], (DEPTH, D_MODEL, 2 * D_FF), D_MODEL),
        "w_ffn1_out": w(ks[5], (DEPTH, D_FF, D_MODEL), D_FF),
        "mix_norm": gain(ks[6], (DEPTH, D_MODEL)),
        "w_in": w(ks[7], (DEPTH, D_MODEL, D_IN), D_MODEL),
        "q_lat_norm": gain(ks[8], (DEPTH, Q_LORA)),
        "kv_lat_norm": gain(ks[9], (DEPTH, KV_LORA)),
        "w_uq": w(ks[10], (DEPTH, Q_LORA, MLA_HEADS * MLA_QK), Q_LORA),
        "w_uk": w(ks[11], (DEPTH, KV_LORA, MLA_HEADS * MLA_NOPE), KV_LORA),
        "w_uv": w(ks[12], (DEPTH, KV_LORA, MLA_HEADS * MLA_V), KV_LORA),
        "w_o_mla": w(ks[13], (DEPTH, MLA_HEADS * MLA_V, D_MODEL), MLA_HEADS * MLA_V),
        "hg_lower_bounds": jax.random.normal(ks[14], (DEPTH, HG_K), f32),
        "hg_out_norm": gain(ks[15], (DEPTH, HG_VDIM)),
        "w_o_hg": w(ks[16], (DEPTH, HG_V, D_MODEL), HG_V),
        "mem_norm": gain(ks[17], (DEPTH, D_MODEL)),
        "w_mem_kv": w(ks[18], (DEPTH, D_MODEL, 2 * MEM_W), D_MODEL),
        "w_o_mem": w(ks[19], (DEPTH, MEM_W, D_MODEL), MEM_W),
        "w_out": w(ks[20], (DEPTH, D_MODEL, D_MODEL), D_MODEL),
        "ffn2_norm": gain(ks[21], (DEPTH, D_MODEL)),
        "w_ffn2_in": w(ks[22], (DEPTH, D_MODEL, 2 * D_FF), D_MODEL),
        "w_ffn2_out": w(ks[23], (DEPTH, D_FF, D_MODEL), D_FF),
        "final_norm": gain(ks[24], (D_MODEL,)),
    }

def first_block(x, mem, positions, ffn1_norm, w_ffn1_in, w_ffn1_out, mix_norm, w_in,
              q_lat_norm, kv_lat_norm, w_uq, w_uk, w_uv, w_o_mla, hg_lower_bounds,
              hg_out_norm, w_o_hg, mem_norm, w_mem_kv, w_o_mem, w_out, ffn2_norm,
              w_ffn2_in, w_ffn2_out, final_norm):
    B, S, D = x.shape
    inv_freq = ROPE_THETA ** (-jnp.arange(0, MLA_ROPE, 2, dtype=jnp.float32) / MLA_ROPE)
    ang = positions.astype(jnp.float32)[..., None] * inv_freq
    cos, sin = jnp.cos(ang), jnp.sin(ang)
    lbs = jnp.cumsum(jax.nn.softmax(hg_lower_bounds.astype(jnp.float32), axis=0), axis=0)
    lbs = lbs - lbs[0:1]

    for l in range(DEPTH):
        x = x + 0.5 * swiglu(rmsnorm(x, ffn1_norm[l]), w_ffn1_in[l], w_ffn1_out[l])
        u = rmsnorm(x, mix_norm[l])
        c_q, c_kv, k_r, hq, hf, hi, hgate, mq, gate_logits = split_sizes(u @ w_in[l], IN_SPLITS)
        y_mla = mla_branch(c_q, c_kv, k_r, cos, sin, q_lat_norm[l], kv_lat_norm[l],
                           w_uq[l], w_uk[l], w_uv[l]) @ w_o_mla[l]
        y_hg = hgrn2_branch(hq, hf, hi, hgate, lbs[l], hg_out_norm[l]) @ w_o_hg[l]
        mem_n = rmsnorm(mem, mem_norm[l])
        y_mem = memory_branch(mq, mem_n, w_mem_kv[l]) @ w_o_mem[l]
        gates = jax.nn.sigmoid(gate_logits.reshape(B, S, N_BRANCH, D))
        merged = gates[:, :, 0] * y_mla + gates[:, :, 1] * y_hg + gates[:, :, 2] * y_mem
        x = x + merged @ w_out[l]
        x = x + 0.5 * swiglu(rmsnorm(x, ffn2_norm[l]), w_ffn2_in[l], w_ffn2_out[l])

    return rmsnorm(x, final_norm)


HEAD_DIM = 64
NSA_HEADS = 8
NSA_GROUPS = 2
CMP_BLOCK = 32
CMP_STRIDE = 16
CMP_HIDDEN = 256
SEL_BLOCK = 64
SEL_TOPK = 8
NSA_WINDOW = 512
SWA_HEADS = 8
SWA_GROUPS = 2
SWA_WINDOW = 128
FOX_HEADS = 8
FOX_GATE_BIAS = 3.0
REL_BUCKETS = 32
REL_MAX_DIST = 128
LN_EPS = 1e-5
DN_ALPHA = (2 * DEPTH) ** 0.25
DN_BETA = (8 * DEPTH) ** -0.25

W_A = NSA_HEADS * HEAD_DIM
KV_A = NSA_GROUPS * HEAD_DIM
W_B = SWA_HEADS * HEAD_DIM
KV_B = SWA_GROUPS * HEAD_DIM
W_C = FOX_HEADS * HEAD_DIM
D_IN_2 = W_A + 6 * KV_A + 3 * NSA_HEADS + W_B + 2 * KV_B + 3 * W_C + FOX_HEADS


def _layer_norm(x, g, b):
    xf = x.astype(jnp.float32)
    mu = jnp.mean(xf, axis=-1, keepdims=True)
    var = jnp.mean(jnp.square(xf - mu), axis=-1, keepdims=True)
    return ((xf - mu) * lax.rsqrt(var + LN_EPS) * g + b).astype(x.dtype)

def _swiglu(x, w1, w2):
    gt, up = jnp.split(x @ w1, 2, axis=-1)
    return (jax.nn.silu(gt) * up) @ w2

def _t5_bucket(dist):
    n = jnp.maximum(dist, 0)
    exact = REL_BUCKETS // 2
    log_ratio = jnp.log(jnp.maximum(n, 1).astype(jnp.float32) / exact) / math.log(REL_MAX_DIST / exact)
    large = exact + (log_ratio * (REL_BUCKETS - exact)).astype(jnp.int32)
    return jnp.where(n < exact, n, jnp.minimum(large, REL_BUCKETS - 1))

def _masked_softmax(logits, mask):
    logits = jnp.where(mask, logits.astype(jnp.float32), -jnp.inf)
    m = jnp.max(logits, axis=-1, keepdims=True)
    m = jnp.where(jnp.isfinite(m), m, 0.0)
    p = jnp.exp(logits - m)
    return p / jnp.maximum(jnp.sum(p, axis=-1, keepdims=True), 1e-30)

def _split_cols(z):
    sizes = [W_A, 6 * KV_A, 3 * NSA_HEADS, W_B, KV_B, KV_B, W_C, W_C, W_C, FOX_HEADS]
    return jnp.split(z, np.cumsum(sizes)[:-1].tolist(), axis=-1)

def _compress(z, pe, w1, w2):
    B, S, G, dh = z.shape
    r = CMP_BLOCK // CMP_STRIDE
    n_chunk = S // CMP_STRIDE
    nc = n_chunk - r + 1
    zr = z.reshape(B, n_chunk, CMP_STRIDE, G, dh)
    blocks = jnp.concatenate([zr[:, j:j + nc] for j in range(r)], axis=2)
    blocks = blocks + pe[:, None, :]
    flat = blocks.transpose(0, 3, 1, 2, 4).reshape(B, G, nc, CMP_BLOCK * dh)
    return jax.nn.gelu(flat @ w1) @ w2

def _nsa(q_a, kv_a, g_a, pe_k, pe_v, ck_w1, ck_w2, cv_w1, cv_w2, rel_a):
    B, S, _ = q_a.shape
    G, HPG, dh = NSA_GROUPS, NSA_HEADS // NSA_GROUPS, HEAD_DIM
    nb = S // Q_BLOCK
    scale = HEAD_DIM ** -0.5
    q = q_a.reshape(B, S, G, HPG, dh).transpose(0, 2, 3, 1, 4)
    k_cmp, v_cmp, k_slc, v_slc, k_win, v_win = [z.reshape(B, S, G, dh) for z in jnp.split(kv_a, 6, axis=-1)]
    kc = _compress(k_cmp, pe_k, ck_w1, ck_w2)
    vc = _compress(v_cmp, pe_v, cv_w1, cv_w2)
    nc = kc.shape[2]
    ns = S // SEL_BLOCK
    n_sel = min(SEL_TOPK, ns)
    ks = k_slc.reshape(B, ns, SEL_BLOCK, G, dh).transpose(0, 3, 1, 2, 4)
    vs = v_slc.reshape(B, ns, SEL_BLOCK, G, dh).transpose(0, 3, 1, 2, 4)
    pad = ((0, 0), (0, 0), (NSA_WINDOW, 0), (0, 0))
    kw = jnp.pad(k_win.transpose(0, 2, 1, 3), pad)
    vw = jnp.pad(v_win.transpose(0, 2, 1, 3), pad)
    gates = jax.nn.sigmoid(g_a.astype(jnp.float32)).reshape(B, S, G, HPG, 3).transpose(0, 2, 3, 1, 4)
    rel_g = rel_a.reshape(G, HPG, REL_BUCKETS)
    c_start = jnp.arange(nc) * CMP_STRIDE
    c_end = c_start + (CMP_BLOCK - 1)
    s_start = jnp.arange(ns) * SEL_BLOCK
    overlap = ((c_start[:, None] < s_start[None] + SEL_BLOCK) & (c_end[:, None] >= s_start[None])).astype(jnp.float32)
    i_w = jnp.arange(Q_BLOCK)
    j_w = jnp.arange(Q_BLOCK + NSA_WINDOW)
    dist_w = NSA_WINDOW + i_w[:, None] - j_w[None]
    band_w = (dist_w >= 0) & (dist_w < NSA_WINDOW)
    bias_w = rel_g[:, :, _t5_bucket(dist_w)]
    blk = jnp.arange(ns)
    sel_off = jnp.arange(SEL_BLOCK)
    gather = jax.vmap(jax.vmap(lambda kb, ix: kb[ix]))
    lookup = jax.vmap(lambda tab, bk: jnp.moveaxis(tab[:, bk], 0, 1), in_axes=(0, 1), out_axes=1)

    def block(qb):
        q0 = qb * Q_BLOCK
        t = q0 + jnp.arange(Q_BLOCK)
        qq = lax.dynamic_slice_in_dim(q, q0, Q_BLOCK, axis=3)
        gg = lax.dynamic_slice_in_dim(gates, q0, Q_BLOCK, axis=3)
        s_c = jnp.einsum('bghqd,bgkd->bghqk', qq, kc, preferred_element_type=jnp.float32) * scale
        s_c = s_c + rel_g[:, :, _t5_bucket(t[:, None] - c_end[None])]
        p_c = _masked_softmax(s_c, c_end[None] <= t[:, None])
        o_c = jnp.einsum('bghqk,bgkd->bghqd', p_c.astype(vc.dtype), vc)
        imp = jnp.einsum('bghqk,kj->bgqj', p_c, overlap)
        cur = (t // SEL_BLOCK)[:, None]
        forced = (blk[None] == 0) | (blk[None] == cur) | (blk[None] == cur - 1)
        valid = blk[None] * SEL_BLOCK <= t[:, None]
        score = jnp.where(forced, jnp.inf, jnp.where(valid, imp, -jnp.inf))
        _, idx = lax.top_k(score, n_sel)
        k_sel = gather(ks, idx).reshape(B, G, Q_BLOCK, n_sel * SEL_BLOCK, dh)
        v_sel = gather(vs, idx).reshape(B, G, Q_BLOCK, n_sel * SEL_BLOCK, dh)
        pos = (idx[..., None] * SEL_BLOCK + sel_off).reshape(B, G, Q_BLOCK, n_sel * SEL_BLOCK)
        dist = t[:, None] - pos
        s_s = jnp.einsum('bghqd,bgqkd->bghqk', qq, k_sel, preferred_element_type=jnp.float32) * scale
        s_s = s_s + lookup(rel_g, _t5_bucket(dist))
        p_s = _masked_softmax(s_s, (dist >= 0)[:, :, None])
        o_s = jnp.einsum('bghqk,bgqkd->bghqd', p_s.astype(v_sel.dtype), v_sel)
        kwb = lax.dynamic_slice_in_dim(kw, q0, Q_BLOCK + NSA_WINDOW, axis=2)
        vwb = lax.dynamic_slice_in_dim(vw, q0, Q_BLOCK + NSA_WINDOW, axis=2)
        s_w = jnp.einsum('bghqd,bgkd->bghqk', qq, kwb, preferred_element_type=jnp.float32) * scale + bias_w
        mask_w = band_w & ((q0 - NSA_WINDOW + j_w) >= 0)[None]
        p_w = _masked_softmax(s_w, mask_w)
        o_w = jnp.einsum('bghqk,bgkd->bghqd', p_w.astype(vwb.dtype), vwb)
        return gg[..., 0:1] * o_c + gg[..., 1:2] * o_s + gg[..., 2:3] * o_w

    out = lax.map(block, jnp.arange(nb))
    return out.transpose(1, 0, 4, 2, 3, 5).reshape(B, S, W_A).astype(q_a.dtype)

def _swa_sink(q_b, k_b, v_b, sinks, rel_b):
    B, S, _ = q_b.shape
    G, HPG, dh, W = SWA_GROUPS, SWA_HEADS // SWA_GROUPS, HEAD_DIM, SWA_WINDOW
    nb = S // W
    scale = HEAD_DIM ** -0.5
    q = q_b.reshape(B, nb, W, G, HPG, dh)
    k = k_b.reshape(B, nb, W, G, dh)
    v = v_b.reshape(B, nb, W, G, dh)

    def with_prev(z):
        prev = jnp.pad(z[:, :-1], ((0, 0), (1, 0), (0, 0), (0, 0), (0, 0)))
        return jnp.concatenate([prev, z], axis=2)

    kk, vv = with_prev(k), with_prev(v)
    i = jnp.arange(W)
    j = jnp.arange(2 * W)
    dist = W + i[:, None] - j[None]
    band = (dist >= 0) & (dist < W)
    first = (jnp.arange(nb)[:, None] * W - W + j[None]) >= 0
    mask = band[None] & first[:, None, :]
    bias = rel_b.reshape(G, HPG, REL_BUCKETS)[:, :, _t5_bucket(dist)]
    logits = jnp.einsum('bnqghd,bnkgd->bghnqk', q, kk, preferred_element_type=jnp.float32) * scale
    logits = jnp.where(mask, logits + bias[:, :, None], -jnp.inf)
    sink = jnp.broadcast_to(sinks.astype(jnp.float32).reshape(1, G, HPG, 1, 1, 1), logits.shape[:-1] + (1,))
    p = jax.nn.softmax(jnp.concatenate([logits, sink], axis=-1), axis=-1)[..., :-1]
    o = jnp.einsum('bghnqk,bnkgd->bnqghd', p.astype(vv.dtype), vv)
    return o.reshape(B, S, W_B)

def _fox(q_c, k_c, v_c, f_c, b_f):
    B, S, _ = q_c.shape
    H, dh = FOX_HEADS, HEAD_DIM
    nb = S // Q_BLOCK
    scale = HEAD_DIM ** -0.5
    q = q_c.reshape(B, S, H, dh).transpose(0, 2, 1, 3)
    k = k_c.reshape(B, S, H, dh).transpose(0, 2, 1, 3)
    v = v_c.reshape(B, S, H, dh).transpose(0, 2, 1, 3)
    log_f = jax.nn.log_sigmoid((f_c + b_f).astype(jnp.float32))
    c = jnp.cumsum(log_f, axis=1).transpose(0, 2, 1)
    s_idx = jnp.arange(S)

    def block(qb):
        q0 = qb * Q_BLOCK
        t = q0 + jnp.arange(Q_BLOCK)
        qq = lax.dynamic_slice_in_dim(q, q0, Q_BLOCK, axis=2)
        cq = lax.dynamic_slice_in_dim(c, q0, Q_BLOCK, axis=2)
        logits = jnp.einsum('bhqd,bhkd->bhqk', qq, k, preferred_element_type=jnp.float32) * scale
        logits = logits + cq[..., None] - c[:, :, None, :]
        logits = jnp.where(s_idx[None] <= t[:, None], logits, -jnp.inf)
        p = jax.nn.softmax(logits, axis=-1)
        return jnp.einsum('bhqk,bhkd->bhqd', p.astype(v.dtype), v)

    out = lax.map(block, jnp.arange(nb))
    return out.transpose(1, 0, 3, 2, 4).reshape(B, S, W_C)

def _token_mix(h, w_in, pe_k, pe_v, ck_w1, ck_w2, cv_w1, cv_w2, sinks, b_f, rel_bias,
               w_br_a, w_br_b, w_br_c, w_gate, b_gate, w_out):
    B, S, D = h.shape
    q_a, kv_a, g_a, q_b, k_b, v_b, q_c, k_c, v_c, f_c = _split_cols(h @ w_in)
    rel_t = rel_bias.T
    o_a = _nsa(q_a, kv_a, g_a, pe_k, pe_v, ck_w1, ck_w2, cv_w1, cv_w2, rel_t[:NSA_HEADS])
    o_b = _swa_sink(q_b, k_b, v_b, sinks, rel_t[NSA_HEADS:])
    o_c = _fox(q_c, k_c, v_c, f_c, b_f)
    g = jax.nn.sigmoid(h @ w_gate + b_gate).reshape(B, S, N_BRANCH, D)
    merged = g[:, :, 0] * (o_a @ w_br_a) + g[:, :, 1] * (o_b @ w_br_b) + g[:, :, 2] * (o_c @ w_br_c)
    return merged @ w_out

def second_inputs(seed: int = 0) -> dict:
    key = jax.random.key(seed)
    keys = iter(jax.random.split(key, 32))
    L, D, F = DEPTH, D_MODEL, D_FF

    def nrm(shape, scale):
        return jax.random.normal(next(keys), shape, jnp.float32) * scale

    return {
        'x': nrm((BATCH, SEQ, D), 1.0),
        'rel_bias': nrm((REL_BUCKETS, NSA_HEADS + SWA_HEADS), 0.5),
        'ln1_g': 1.0 + nrm((L, D), 0.02),
        'ln1_b': nrm((L, D), 0.02),
        'ffn1_w1': nrm((L, D, 2 * F), D ** -0.5),
        'ffn1_w2': nrm((L, F, D), DN_BETA * F ** -0.5),
        'w_in': nrm((L, D, D_IN_2), D ** -0.5),
        'cmp_pe_k': nrm((L, CMP_BLOCK, HEAD_DIM), 0.1),
        'cmp_pe_v': nrm((L, CMP_BLOCK, HEAD_DIM), 0.1),
        'cmp_k_w1': nrm((L, CMP_BLOCK * HEAD_DIM, CMP_HIDDEN), (CMP_BLOCK * HEAD_DIM) ** -0.5),
        'cmp_k_w2': nrm((L, CMP_HIDDEN, HEAD_DIM), CMP_HIDDEN ** -0.5),
        'cmp_v_w1': nrm((L, CMP_BLOCK * HEAD_DIM, CMP_HIDDEN), (CMP_BLOCK * HEAD_DIM) ** -0.5),
        'cmp_v_w2': nrm((L, CMP_HIDDEN, HEAD_DIM), CMP_HIDDEN ** -0.5),
        'swa_sinks': nrm((L, SWA_HEADS), 1.0),
        'fox_b_f': FOX_GATE_BIAS + nrm((L, FOX_HEADS), 0.1),
        'w_br_a': nrm((L, W_A, D), W_A ** -0.5),
        'w_br_b': nrm((L, W_B, D), W_B ** -0.5),
        'w_br_c': nrm((L, W_C, D), W_C ** -0.5),
        'w_gate': nrm((L, D, N_BRANCH * D), D ** -0.5),
        'b_gate': nrm((L, N_BRANCH * D), 0.01),
        'w_out': nrm((L, D, D), DN_BETA * D ** -0.5),
        'ln2_g': 1.0 + nrm((L, D), 0.02),
        'ln2_b': nrm((L, D), 0.02),
        'ffn2_w1': nrm((L, D, 2 * F), D ** -0.5),
        'ffn2_w2': nrm((L, F, D), DN_BETA * F ** -0.5),
        'ln3_g': 1.0 + nrm((L, D), 0.02),
        'ln3_b': nrm((L, D), 0.02),
    }

def second_block(x, rel_bias, ln1_g, ln1_b, ffn1_w1, ffn1_w2, w_in, cmp_pe_k, cmp_pe_v,
              cmp_k_w1, cmp_k_w2, cmp_v_w1, cmp_v_w2, swa_sinks, fox_b_f,
              w_br_a, w_br_b, w_br_c, w_gate, b_gate, w_out, ln2_g, ln2_b,
              ffn2_w1, ffn2_w2, ln3_g, ln3_b):
    for l in range(DEPTH):
        x = _layer_norm(DN_ALPHA * x + 0.5 * _swiglu(x, ffn1_w1[l], ffn1_w2[l]), ln1_g[l], ln1_b[l])
        mix = _token_mix(x, w_in[l], cmp_pe_k[l], cmp_pe_v[l], cmp_k_w1[l], cmp_k_w2[l],
                         cmp_v_w1[l], cmp_v_w2[l], swa_sinks[l], fox_b_f[l], rel_bias,
                         w_br_a[l], w_br_b[l], w_br_c[l], w_gate[l], b_gate[l], w_out[l])
        x = _layer_norm(DN_ALPHA * x + mix, ln2_g[l], ln2_b[l])
        x = _layer_norm(DN_ALPHA * x + 0.5 * _swiglu(x, ffn2_w1[l], ffn2_w2[l]), ln3_g[l], ln3_b[l])
    return x


def setup_inputs(seed=0):
    out = dict(first_inputs(seed))
    for name, value in second_inputs(seed + 1).items():
        if name != "x":
            out[name + "_2"] = value
    return out


def reference(
    x, mem, positions, ffn1_norm, w_ffn1_in, w_ffn1_out, mix_norm, w_in, q_lat_norm,
    kv_lat_norm, w_uq, w_uk, w_uv, w_o_mla, hg_lower_bounds, hg_out_norm, w_o_hg, mem_norm,
    w_mem_kv, w_o_mem, w_out, ffn2_norm, w_ffn2_in, w_ffn2_out, final_norm, rel_bias_2, ln1_g_2,
    ln1_b_2, ffn1_w1_2, ffn1_w2_2, w_in_2, cmp_pe_k_2, cmp_pe_v_2, cmp_k_w1_2, cmp_k_w2_2,
    cmp_v_w1_2, cmp_v_w2_2, swa_sinks_2, fox_b_f_2, w_br_a_2, w_br_b_2, w_br_c_2, w_gate_2,
    b_gate_2, w_out_2, ln2_g_2, ln2_b_2, ffn2_w1_2, ffn2_w2_2, ln3_g_2, ln3_b_2,
):
    x = first_block(
        x, mem, positions, ffn1_norm, w_ffn1_in, w_ffn1_out, mix_norm, w_in, q_lat_norm,
        kv_lat_norm, w_uq, w_uk, w_uv, w_o_mla, hg_lower_bounds, hg_out_norm, w_o_hg, mem_norm,
        w_mem_kv, w_o_mem, w_out, ffn2_norm, w_ffn2_in, w_ffn2_out, final_norm,
    )
    return second_block(
        x, rel_bias_2, ln1_g_2, ln1_b_2, ffn1_w1_2, ffn1_w2_2, w_in_2, cmp_pe_k_2, cmp_pe_v_2,
        cmp_k_w1_2, cmp_k_w2_2, cmp_v_w1_2, cmp_v_w2_2, swa_sinks_2, fox_b_f_2, w_br_a_2,
        w_br_b_2, w_br_c_2, w_gate_2, b_gate_2, w_out_2, ln2_g_2, ln2_b_2, ffn2_w1_2, ffn2_w2_2,
        ln3_g_2, ln3_b_2,
    )


_drawn_inputs = setup_inputs


def setup_inputs(seed=0):
    import zlib

    import numpy as np

    out = dict(_drawn_inputs(seed))
    spreads = {}
    factors = {'ffn1_norm': 4.455,
     'mix_norm': 3.771,
     'q_lat_norm': 8.0,
     'kv_lat_norm': 8.0,
     'hg_out_norm': 6.675,
     'mem_norm': 8.0,
     'ffn2_norm': 4.956,
     'final_norm': 2.764,
     'cmp_pe_k_2': 8.0,
     'cmp_pe_v_2': 7.47,
     'cmp_k_w1_2': 3.446,
     'cmp_k_w2_2': 3.462,
     'swa_sinks_2': 8.0,
     'fox_b_f_2': 64.0,
     'b_gate_2': 64.0}
    for name, (base, spread) in spreads.items():
        noise = np.random.default_rng([zlib.crc32(name.encode()), seed]).standard_normal(out[name].shape)
        drawn = base * np.exp(spread * noise) if base else spread * noise
        out[name] = __import__('jax').numpy.asarray(drawn.astype(out[name].dtype))
    for name, factor in factors.items():
        out[name] = (out[name] * factor).astype(out[name].dtype)
    return out
```

```python
from contextlib import ExitStack, contextmanager

import numpy as np

import concourse.bass as bass
from concourse import mybir

F32 = mybir.dt.float32
I32 = mybir.dt.int32
ALU = mybir.AluOpType
ACT = mybir.ActivationFunctionType
AX = mybir.AxisListType.X

P = 128
S = 256
TT = S // P
D = 1024
KD = D // P
DEPTH = 2
F = 2816
FT = F // P
NEG = -1.0e30
LOW = -1.0e29

SLOT = 2048
R = 5
SLOTS = 109
PASSES = (SLOTS + 1) // R
assert (SLOTS + 1) % R == 0

NC_COLS = 128 + 256 + 256 + 40 + 32 + 128
NP_COLS = 512


class Signal:

    def __init__(self, name, sem, book, places):
        self.name, self.sem, self.book, self.places = name, sem, book, places
        self.count = [0] * len(ITERATIONS)
        self.labels = {}

    def up(self, label=None, by=1):
        r = self.places["made in"]
        self.count[r] += by
        if label is not None:
            assert (r, label) not in self.labels, (self.name, label)
            self.labels[r, label] = self.count[r]
        return self.sem, by

    def value(self, v):
        old = self.book.get(self.name)
        r, it = self.places["made in"], self.places["iteration"]
        if old is None:
            return self.sem, 1
        count = old[0]
        base = sum(n * c for n, c in zip(ITERATIONS[:r], count[:r])) + v
        if isinstance(it, int) or not count[r]:
            return self.sem, base
        return self.sem, it * count[r] + base

    def after(self, label):
        old = self.book.get(self.name)
        if old is None:
            return self.sem, 1
        return self.value(old[1][self.places["made in"], label])

    def value_at_end(self):
        old = self.book.get(self.name)
        return (self.sem, 1) if old is None else (self.sem, sum(n * c for n, c in zip(ITERATIONS, old[0])))

    def after_in(self, region, label):
        old = self.book.get(self.name)
        if old is None:
            return self.sem, 1
        assert ITERATIONS[region] == 1
        return self.sem, sum(n * c for n, c in zip(ITERATIONS[:region], old[0][:region])) + old[1][region, label]


PREP, BLOCK1, BETWEEN, BLOCK2, END = range(5)
ITERATIONS = [1, DEPTH, 1, DEPTH, 1]


class Signals(dict):
    def __init__(self, nc, ctx, book, places):
        super().__init__()
        self.nc, self.ctx, self.book, self.places = nc, ctx, book, places

    def __missing__(self, name):
        sem = self.ctx.enter_context(self.nc.semaphore("s_" + name.replace(" ", "_")))
        self[name] = Signal(name, sem, self.book, self.places)
        return self[name]

    def counts(self):
        return {n: (s.count, s.labels) for n, s in self.items()}


def build(nc, a, new):
    dry = new()
    emit(nc, a, emit(dry, declare(dry), {}))


INPUTS = {
    "x": ((S, D), F32), "mem": ((S, D), F32), "pos": ((1, S), I32),
    "weights": ((2 * DEPTH * SLOTS, P, SLOT), F32), "params": ((2 * DEPTH, P, NP_COLS), F32),
    "rows": ((1 + 3 * DEPTH, 2, D), F32), "consts": ((P, NC_COLS), F32), "masks": ((P, 7 * P), I32),
    "onehots": ((32, 2 * 512), F32), "relb": ((32, 16), F32), "relmask": ((16, 512), F32),
}


def declare(nc):
    a = {n: nc.dram_tensor("in_" + n, s, t, kind="ExternalInput").ap() for n, (s, t) in INPUTS.items()}
    a["out"] = nc.dram_tensor("out_x", (S, D), F32, kind="ExternalOutput").ap()
    return a


def emit(nc, a, book):
    places = {"made in": PREP, "iteration": 0}
    nc.disable_value_cache = True
    rel_dram = nc.dram_tensor("rel_by_distance", (16, 512), F32).ap()
    with ExitStack() as ctx:
        sig = Signals(nc, ctx, book, places)

        def sb(name, shape, dt=F32):
            return ctx.enter_context(nc.sbuf_tensor(name, shape, dt))

        psA = ctx.enter_context(nc.psum_tensor("psA", [P, 2, 512], F32))
        psY = ctx.enter_context(nc.psum_tensor("psY", [P, 4, 512], F32))
        psT = ctx.enter_context(nc.psum_tensor("psT", [P, 2, 512], F32))
        BANK = {f"A{i}": psA[:, i, :] for i in range(2)}
        BANK |= {f"Y{i}": psY[:, i, :] for i in range(4)}
        BANK |= {f"T{i}": psT[:, i, :] for i in range(2)}
        bank_of = {}

        ring = sb("ring", [P, R, SLOT])
        x = sb("x", [P, TT, D])
        xn = sb("xn", [P, TT, D])
        xT = sb("xT", [P, KD, S])
        G = sb("G", [P, 24, S])
        Sc = sb("Sc", [P, 2, 4, S])
        PT = sb("PT", [P, 2, 2, 4, P])
        O = sb("O", [P, TT, 512])
        OT = sb("OT", [P, 3, 4, S])
        par = sb("par", [P, NP_COLS])
        sil = sb("sil", [P, 2, S])
        hT = sb("hT", [P, 2, S])
        cst = sb("cst", [P, NC_COLS])
        st = sb("st", [P, 148])
        ident, CM, ones = cst[:, 0:128], cst[:, 128:384], cst[:, 384:640]
        invf, sgn, half = cst[:, 640:641], cst[:, 641:642], cst[:, 642:650]
        cmask, flip = cst[:, 680:710], cst[:, 712:840]
        lnr = G[:, 0:8, :].rearrange("p a b -> p (a b)").rearrange("p (a b) -> p a b", a=2)
        memraw = lnr
        xf = xn[:, :, :].rearrange("p a b -> p (a b)")
        memTg = xf.rearrange("p (k t) -> p k t", k=KD)
        cn = xf[:, 0:1280].rearrange("p (t n) -> p t n", t=2)
        ARENA = 19904
        arena = sb("arena", [P, ARENA])
        used = [0]

        def take(*shape):
            n = int(np.prod(shape))
            v = arena[:, used[0]:used[0] + n]
            used[0] += n
            assert used[0] <= ARENA, used[0]
            if len(shape) == 2:
                v = v.rearrange("p (a b) -> p a b", a=shape[0])
            if len(shape) == 3:
                v = v.rearrange("p (a b c) -> p a b c", a=shape[0], b=shape[1])
            return v

        memT = take(KD, S)
        KT = take(8, S)
        QT = take(8, S)
        QM = take(4, S)
        KM = take(4, S)
        QH = take(4, S)
        KH = take(4, S)
        GC = take(4, S)
        Am = take(2, 4, P)
        Aoff = take(4, P)
        VM = take(TT, 512)
        VH = take(TT, 512)
        VX = take(TT, 512)
        GH = take(TT, 512)
        cT = take(5, S)
        MASK = take(7, P).bitcast(I32)
        CS = take(S)
        CK = take(2, S)
        lbt = take(64)
        posi = KT[:, 5, :].bitcast(I32)
        flatten = lambda t: t.rearrange("p a b -> p (a b)")
        mergedA = QT
        EB = [Sc[:, i, :, :] for i in range(2)]
        TL = [PT[:, i, :, :, :].rearrange("p a b c -> p (a b c)").rearrange("p (h t) -> p h t", h=4)
              for i in range(2)]
        used[0] = 0
        BIAS = take(16, S)
        QA = take(4, S)
        QB = take(4, S)
        QF = take(4, S)
        KS = take(2, 2, S)
        KW = take(2, 2, S)
        KB = take(2, 2, S)
        KF = take(4, 2, S)
        KC = take(2, 30)
        VC = take(2, 64)
        VT = take(TT, 416)
        VF = take(TT, 512)
        mergedB = take(KD, S)
        Z2 = take(2, S)
        ZB = take(16, 30)
        HC = take(2, 30)
        CB = take(TT, 8, 15)
        CF = take(2, S)
        gg = take(TT, 24)

        FS = take(3, S)
        scf = Sc[:, :, :, :].rearrange("p a b c -> p (a b c)")
        onehot_f, onehot_r, relb = scf[0:32, 0:512], scf[0:32, 512:1024], scf[0:32, 1024:1040]
        relmask = scf[0:16, 1040:1552]
        relsum = O[0:16, 0, :]
        BR = G[:, 8:24, :]
        BRANCH = {BLOCK1: ["mla", "hg", "mem"], BLOCK2: ["nsa", "swa", "fox"]}

        def spread(ap, shape):
            return ap.broadcast_to(shape)

        def fill(eng, bank, label):
            bank_of[places["made in"], label] = bank
            sem, v = sig[bank + " read"].value(sig[bank + " full"].count[places["made in"]])
            if not (isinstance(v, int) and v <= 0):
                eng.wait_ge(sem, v)
            return BANK[bank]

        def full(label):
            return sig[bank_of[places["made in"], label] + " full"].after(label)

        def filled(label):
            return sig[bank_of[places["made in"], label] + " full"].up(label)

        def at(label):
            return BANK[bank_of[places["made in"], label]]

        def read(label):
            return sig[bank_of[places["made in"], label] + " read"].up(label)

        def taken(label):
            bank, old = bank_of[places["made in"], label], book.get(bank_of[places["made in"], label] + " full")
            return sig[bank + " read"].value(old[1][places["made in"], label] if old else 1)

        @contextmanager
        def region(eng, r):
            places["made in"] = r
            if ITERATIONS[r] == 1:
                places["iteration"] = 0
                yield 0
            else:
                with eng.Fori(0, ITERATIONS[r]) as it:
                    places["iteration"] = it
                    yield it
            places["iteration"] = 0

        def x_is_done(eng, label):
            for b in range(4):
                eng.wait_ge(*(sig[f"Y{b} read"].value(0) if label is None else taken(label + (b,))))

        block = ctx.enter_context(nc.Block())

        BEFORE = [None, ("y", 0), ("y", "mix")]

        @block.tensor
        def _(pe):
            state = {"slot": 0, "freed": 1, "A": 0}

            def mm(out, lhsT, rhs, start, stop, up=None):
                i = pe.matmul(out, lhsT, rhs, start=start, stop=stop)
                if up is not None:
                    i.then_inc(*up)
                elif state["freed"]:
                    i.then_inc(*sig["slot free"].up(by=state["freed"]))
                    state["freed"] = 0

            def slot():
                c, r = state["slot"], state["slot"] % R
                state["slot"] += 1
                per = PASSES - (r == R - 1)
                layer = places["iteration"] + (0 if places["made in"] == BLOCK1 else DEPTH)
                pe.wait_ge(sig[f"slot {r} loaded"].sem, layer * (16 * per) + 16 * (c // R + 1))
                return ring[:, r, :]

            def free(n=1):
                state["freed"] += n

            def next_a():
                state["A"] ^= 1
                return f"A{state['A'] ^ 1}"

            def turn(bank, label, tiles, src_ready=None):
                if src_ready is not None:
                    pe.wait_ge(*src_ready)
                out = fill(pe, bank, label)
                at_col = 0
                for n, t in enumerate(tiles):
                    i = pe.transpose(out[0:t.shape[1], at_col:at_col + P], t, ident)
                    at_col += P
                i.then_inc(*filled(label))

            def turn_x(src, label, ready):
                for tt in range(TT):
                    pe.wait_ge(*ready(tt))
                    for h in range(2):
                        turn(f"T{h}", label + (tt, h),
                             [src[:, tt, (4 * h + q) * P:(4 * h + q + 1) * P] for q in range(4)])

            def wait_xT(label):
                for h in range(2):
                    pe.wait_ge(*taken(label + (1, h)))

            def features(label, n_tiles, rhs, kt, w, m=P, ready=None):
                if ready is not None:
                    pe.wait_ge(*ready)
                for n in range(0, n_tiles, 2):
                    lab = (label, n // 2)
                    out = fill(pe, next_a(), lab)
                    for j in range(2):
                        for k in range(kt):
                            mm(out[0:m, j * S:(j + 1) * S], w(n + j, k), rhs(k), k == 0, k == kt - 1,
                               filled(lab) if j == 1 and k == kt - 1 else None)

            def slot_features(label, n_slots, rhs=None):
                for n in range(n_slots):
                    s = slot().rearrange("p (k c) -> p k c", k=KD)
                    lab = (label, n)
                    out = fill(pe, next_a(), lab)
                    for j in range(2):
                        for k in range(KD):
                            mm(out[:, j * S:(j + 1) * S], s[:, k, j * P:(j + 1) * P],
                               (xT if rhs is None else rhs)[:, k, :], k == 0, k == KD - 1,
                               filled(lab) if j == 1 and k == KD - 1 else None)
                    free()

            def slot_tokens(label, width, lhs=None):
                lhs = xT if lhs is None else lhs
                banks = [next_a(), next_a()]
                outs = [fill(pe, banks[t], (label, t)) for t in range(TT)]
                for h in range(2):
                    s = slot()[:, 0:4 * width].rearrange("p (k c) -> p k c", k=4)
                    for q in range(4):
                        k = 4 * h + q
                        for t in range(TT):
                            mm(outs[t][:, 0:width], lhs[:, k, t * P:(t + 1) * P], s[:, q, :], k == 0, k == KD - 1,
                               filled((label, t)) if k == KD - 1 else None)
                    free()

            def ffn(f, xlabel):
                if xlabel is None:
                    for h in range(2):
                        pe.wait_ge(*sig[f"T{h} read"].value(0))
                else:
                    wait_xT(xlabel)

                def up(j, sa, sbb):
                    lab = ("ab", f, j)
                    out = fill(pe, f"A{j % 2}", lab)
                    for v, s in enumerate((sa, sbb)):
                        for k in range(KD):
                            mm(out[:, v * S:(v + 1) * S], s[:, k, (j % 2) * P:(j % 2 + 1) * P], xT[:, k, :],
                               k == 0, k == KD - 1, filled(lab) if v == 1 and k == KD - 1 else None)

                ys = []

                def down(j, s):
                    pe.wait_ge(*taken(("ab", f, j)))
                    if j == 0:
                        ys.extend(fill(pe, f"Y{b}", ("y", f, b)) for b in range(4))
                    for t in range(TT):
                        for n in range(2):
                            mm(ys[2 * t + n], hT[:, j % 2, t * P:(t + 1) * P], s[:, j % 2, n * 512:(n + 1) * 512],
                               j == 0, j == FT - 1, filled(("y", f, 2 * t + n)) if j == FT - 1 else None)

                w2 = [None] * (FT // 2)
                for j in range(FT):
                    if j % 2 == 0:
                        sa = slot().rearrange("p (k c) -> p k c", k=KD)
                        sbb = slot().rearrange("p (k c) -> p k c", k=KD)
                    up(j, sa, sbb)
                    if j % 2 == 1:
                        free(2)
                    else:
                        w2[j // 2] = None
                    if j >= 1:
                        g = (j - 1) // 2
                        if w2[g] is None:
                            w2[g] = slot().rearrange("p (k c) -> p k c", k=2)
                        down(j - 1, w2[g])
                        if (j - 1) % 2 == 1:
                            free()
                down(FT - 1, w2[FT // 2 - 1])
                free()
                state["A"] = 0

            def attention(name, hbs, q, k, v, dv, causal, extra=None):
                todo = [(hb, qt) for hb in range(hbs) for qt in range(TT)]
                keys = lambda qt: TT if (qt or not causal) else 1

                def scores(hb, qt):
                    w = keys(qt) * P
                    for b in range(2):
                        lab = ("s", name, hb, qt, b)
                        out = fill(pe, f"A{b}", lab)
                        for j in range(2):
                            h = 4 * hb + 2 * b + j
                            o = out[:, j * S:j * S + w]
                            last = filled(lab) if j == 1 else None
                            mm(o, q(h, qt), k(h, w), True, extra is None, None if extra else last)
                            if extra:
                                c1, c2 = extra(h, qt, w)
                                mm(o, *c1, False, False)
                                mm(o, *c2, False, True, last)

                def rest(n):
                    hb, qt = todo[n]
                    for kt in range(keys(qt)):
                        turn(f"T{kt}", ("pt", name, hb, qt, kt),
                             [Sc[:, n % 2, j, kt * P:(kt + 1) * P] for j in range(4)],
                             sig["weights"].after((name, hb, qt)))
                    lab = ("o", name, hb, qt)
                    out = fill(pe, f"Y{n % 2}", lab)
                    for kt in range(keys(qt)):
                        pe.wait_ge(*taken(("pt", name, hb, qt, kt)))
                    for j in range(4):
                        for kt in range(keys(qt)):
                            mm(out[:, j * dv:(j + 1) * dv], PT[:, n % 2, kt, j, :], v(4 * hb + j, kt),
                               kt == 0, kt == keys(qt) - 1,
                               filled(lab) if j == 3 and kt == keys(qt) - 1 else None)

                scores(*todo[0])
                for n in range(len(todo)):
                    if n + 1 < len(todo):
                        scores(*todo[n + 1])
                    rest(n)

            def turn_o(name, ready):
                for qt in range(TT):
                    turn(f"T{qt}", ("ot", name, qt), [O[:, qt, j * P:(j + 1) * P] for j in range(4)], ready(qt))

            def merge(merged):
                for br in range(3):
                    for t in range(TT):
                        pe.wait_ge(*taken(("ot", BRANCH[places["made in"]][br], t)))
                    for h in range(2):
                        s = slot().rearrange("p (k c) -> p k c", k=4)
                        for n in range(2):
                            lab = ("wo", br, 2 * h + n)
                            out = fill(pe, next_a(), lab)
                            for j in range(2):
                                for k in range(4):
                                    c = (2 * n + j) * P
                                    mm(out[:, j * S:(j + 1) * S], s[:, k, c:c + P], OT[:, br, k, :], k == 0, k == 3,
                                       filled(lab) if j == 1 and k == 3 else None)
                        free()
                pe.wait_ge(*sig["merged"].after("all"))
                ys = [fill(pe, f"Y{b}", ("y", "mix", b)) for b in range(4)]
                for g in range(4):
                    s = slot().rearrange("p (k c) -> p k c", k=2)
                    for q in range(2):
                        k = 2 * g + q
                        for b in range(4):
                            mm(ys[b], merged[:, k, (b // 2) * P:(b // 2 + 1) * P],
                               s[:, q, (b % 2) * 512:(b % 2 + 1) * 512], k == 0, k == KD - 1,
                               filled(("y", "mix", b)) if k == KD - 1 else None)
                    free()

            with region(pe, PREP):
                pe.wait_ge(sig["consts"].sem, 16)
                turn_x(xn, ("mem",), lambda tt: sig["scaled"].after(("mem", tt)))

            with region(pe, BLOCK1):
                state["slot"] = 0
                turn_x(xn, ("norm", 0), lambda tt: sig["scaled"].after((0, tt)))
                ffn(0, ("norm", 0))
                turn_x(xn, ("norm", 1), lambda tt: sig["scaled"].after((1, tt)))
                wait_xT(("norm", 1))
                outs = [fill(pe, f"Y{b}", ("c", b)) for b in range(4)]
                k = 0
                for n in (3, 3, 2):
                    s = slot()[:, 0:n * 640].rearrange("p (k c) -> p k c", k=n)
                    for q in range(n):
                        for t in range(TT):
                            lhsT = xT[:, k, t * P:(t + 1) * P]
                            mm(outs[t][:, 0:384], lhsT, s[:, q, 0:384], k == 0, k == KD - 1,
                               filled(("c", t)) if k == KD - 1 else None)
                            mm(outs[2 + t][:, 0:256], lhsT, s[:, q, 384:640], k == 0, k == KD - 1,
                               filled(("c", 2 + t)) if k == KD - 1 else None)
                        k += 1
                    free()
                s = slot().rearrange("p (n k c) -> p n k c", n=2, k=KD)
                features("kr", 2, lambda k: xT[:, k, :], KD, lambda n, k: s[:, n, k, :])
                free()
                slot_features("mq", 2)
                slot_features("hq", 2)
                slot_features("hf", 2)
                slot_tokens("hi", 512)
                slot_tokens("hgate", 512)
                slot_features("gate", 12)
                for t in range(TT):
                    pe.wait_ge(*taken(("c", t)))
                    pe.wait_ge(*taken(("c", 2 + t)))
                    turn("T0", ("cT", t, 0), [cn[:, t, j * P:(j + 1) * P] for j in range(3)])
                    turn("T1", ("cT", t, 1), [cn[:, t, j * P:(j + 1) * P] for j in range(3, 5)])
                for h in range(2):
                    pe.wait_ge(*taken(("cT", 1, h)))
                for h in range(2):
                    s = slot()[:, 0:3 * 512].rearrange("p (k c) -> p k c", k=3)
                    features(("uq", h), 4, lambda k: cT[:, k, :], 3, lambda n, k: s[:, k, n * P:(n + 1) * P])
                    free()
                s = slot().rearrange("p (v k c) -> p v k c", v=2, k=2)
                features("uk", 8, lambda k: cT[:, 3 + k, :], 2, lambda n, k: s[:, 0, k, n * 64:(n + 1) * 64], m=64)
                for t in range(TT):
                    out = fill(pe, next_a(), ("uv", t))
                    for k in range(2):
                        mm(out, cT[:, 3 + k, t * P:(t + 1) * P], s[:, 1, k, :], k == 0, k == 1,
                           filled(("uv", t)) if k == 1 else None)
                free()
                pe.wait_ge(*sig["memory scaled"].after(0))
                slot_features("mk", 2, rhs=memTg)
                slot_tokens("mv", 512, lhs=memTg)
                pe.wait_ge(*sig["recurrence keys"].after(0))
                for i in range(2):
                    pe.wait_ge(*taken(("hq", i)))
                for t in range(TT):
                    lab = ("diag", t)
                    out = fill(pe, next_a(), lab)
                    for h in range(4):
                        c = slice(t * P, (t + 1) * P)
                        mm(out[:, h * P:(h + 1) * P], KH[:, h, c], QH[:, h, c], True, True,
                           filled(lab) if h == 3 else None)
                for i in range(8):
                    pe.wait_ge(*sig["decayed"].after(i))
                    tl = TL[i % 2]
                    if i < 7:
                        for t in range(TT):
                            lab = ("level", i, t)
                            out = fill(pe, next_a(), lab)
                            for h in range(4):
                                c = tl[:, h, t * P:(t + 1) * P]
                                mm(out[:, h * P:(h + 1) * P], c, c, True, True, filled(lab) if h == 3 else None)
                    else:
                        lab = ("level", i, 0)
                        out = fill(pe, next_a(), lab)
                        for h in range(4):
                            mm(out[:, h * P:(h + 1) * P], tl[:, h, 0:P], tl[:, h, P:S], True, True,
                               filled(lab) if h == 3 else None)
                if state["A"]:
                    state["A"] = 0
                pe.wait_ge(*taken(("level", 7, 0)))
                for t in range(TT):
                    pe.wait_ge(*taken(("hi", t)))
                for t in range(TT):
                    lab = ("ho", t)
                    out = fill(pe, f"Y{2 + t}", lab)
                    for h in range(4):
                        o = out[:, h * P:(h + 1) * P]
                        v = lambda s: VH[:, s, h * P:(h + 1) * P]
                        last = filled(lab) if h == 3 else None
                        if t == 0:
                            mm(o, Am[:, 0, h, :], v(0), True, True, last)
                        else:
                            mm(o, Aoff[:, h, :], v(0), True, False)
                            mm(o, Am[:, 1, h, :], v(1), False, True, last)
                for h in range(2):
                    for n in range(2):
                        pe.wait_ge(*taken((("uq", h), n)))
                for n in range(4):
                    pe.wait_ge(*taken(("uk", n)))
                for t in range(TT):
                    pe.wait_ge(*taken(("uv", t)))
                pe.wait_ge(*sig["rotary keys"].after(0))
                attention("mla", 2, lambda h, qt: QT[:, h, qt * P:(qt + 1) * P], lambda h, w: KT[:, h, 0:w],
                          lambda h, kt: VM[:, kt, h * 64:(h + 1) * 64], 64, True)
                turn_o("mla", lambda qt: taken(("o", "mla", 1, qt)))
                for t in range(TT):
                    turn(f"T{t}", ("ot", "hg", t), [GH[:, t, j * P:(j + 1) * P] for j in range(4)],
                         sig["recurrence out"].after(t))
                for n in range(2):
                    pe.wait_ge(*taken(("mq", n)))
                    pe.wait_ge(*taken(("mk", n)))
                    pe.wait_ge(*taken(("mv", n)))
                attention("mem", 1, lambda h, qt: QM[:, h, qt * P:(qt + 1) * P], lambda h, w: KM[:, h, 0:w],
                          lambda h, kt: VX[:, kt, h * P:(h + 1) * P], P, False)
                turn_o("mem", lambda qt: taken(("o", "mem", 0, qt)))
                merge(mergedA)
                turn_x(xn, ("norm", 2), lambda tt: sig["scaled"].after((2, tt)))
                ffn(1, ("norm", 2))

            with region(pe, BETWEEN):
                pe.wait_ge(*sig["rel tables"].value(16 * 3))
                mm(fill(pe, "A0", "rel")[0:16, :], relb, onehot_r, True, True, filled("rel"))
                out = fill(pe, "A1", "rel cmp")
                for qt in range(TT):
                    for c in range(15):
                        i = 256 + qt * P - 31 - 16 * c
                        n = (qt * 15 + c) * 8
                        mm(out[:, n:n + 8], onehot_f[:, i:i + P], relb[:, 0:8], True, True,
                           filled("rel cmp") if (qt, c) == (1, 14) else None)
                turn_x(x, ("norm", "final"), lambda tt: sig["x normed"].after(("final", tt)))
                pe.wait_ge(*sig["bias"].value(16))
                for n in range(8):
                    mm(fill(pe, f"A{n % 2}", ("flip", n)), flip, BR[:, 2 * n:2 * n + 2, :], True, True, filled(("flip", n)))

            with region(pe, BLOCK2):
                state["slot"] = 0
                ffn(0, None)
                turn_x(x, ("norm", 0), lambda tt: sig["x normed"].after((0, tt)))
                wait_xT(("norm", 0))
                slot_features("qa", 2)
                for n in ("ks", "kw", "kc", "vc"):
                    slot_features(n, 1)
                slot_features("qb", 2)
                slot_features("kb", 1)
                banks = [next_a(), next_a()]
                outs = [fill(pe, banks[t], ("vt", t)) for t in range(TT)]
                fout = fill(pe, "Y0", "f")
                for h in range(2):
                    s = slot()[:, 0:4 * 416].rearrange("p (k c) -> p k c", k=4)
                    for q in range(4):
                        k = 4 * h + q
                        for t in range(TT):
                            mm(outs[t][:, 0:416], xT[:, k, t * P:(t + 1) * P], s[:, q, :], k == 0, k == KD - 1,
                               filled(("vt", t)) if k == KD - 1 else None)
                        mm(fout[0:8, 0:S], s[:, q, 408:416], xT[:, k, :], k == 0, k == KD - 1,
                           filled("f") if k == KD - 1 else None)
                    free()
                slot_features("qf", 2)
                slot_features("kf", 2)
                slot_tokens("vf", 512)
                for z in ("k", "v"):
                    pe.wait_ge(*sig["blocks"].after(z))
                    for m in range(2):
                        s = slot().rearrange("p (l c) -> p l c", l=16)
                        out = fill(pe, next_a(), ("cmp", z, m))
                        for lp in range(16):
                            mm(out[:, 0:30], s[:, lp, :], ZB[:, lp, :], lp == 0, lp == 15,
                               filled(("cmp", z, m)) if lp == 15 else None)
                        free()
                    for m in range(2):
                        pe.wait_ge(*taken(("cmp", z, m)))
                    out = fill(pe, "Y1", ("cmp out", z))
                    if z == "k":
                        for m in range(2):
                            mm(out[:, 0:30], par[:, 56 + m * P:56 + (m + 1) * P], HC[:, m, :], m == 0, m == 1,
                               filled(("cmp out", z)) if m == 1 else None)
                    else:
                        for g in range(2):
                            for m in range(2):
                                mm(out[0:15, g * 64:(g + 1) * 64], HC[:, m, g * 15:(g + 1) * 15],
                                   par[:, 312 + m * 64:312 + (m + 1) * 64], m == 0, m == 1,
                                   filled(("cmp out", z)) if g == 1 and m == 1 else None)
                slot_features("gate", 12)
                state["A"] = 0
                for n in (("qa", 0), ("qa", 1), ("cmp out", "k"), ("cmp out", "v")):
                    pe.wait_ge(*taken(n))
                for qt in range(TT):
                    lab = ("sc", qt)
                    out = fill(pe, f"A{qt}", lab)
                    for h in range(8):
                        g = h // 4
                        mm(out[:, h * 15:(h + 1) * 15], QA[:, h // 2, qt * P:(qt + 1) * P],
                           KC[:, h % 2, g * 15:(g + 1) * 15], True, True, filled(lab) if h == 7 else None)
                for qt in range(TT):
                    pe.wait_ge(*sig["weights"].after(("cmp", qt)))
                    sc = scf[:, qt * 1024:qt * 1024 + 120]
                    for b in range(2):
                        turn(f"T{b}", ("ptc", qt, b), [sc[:, (4 * b + j) * 15:(4 * b + j + 1) * 15] for j in range(4)])
                    for b in range(2):
                        pe.wait_ge(*taken(("ptc", qt, b)))
                    lab = ("o", "cmp", 0, qt)
                    out = fill(pe, f"Y{qt}", lab)
                    for h in range(8):
                        mm(out[:, h * 64:(h + 1) * 64], PT[0:15, qt, h // 4, h % 4, :], VC[0:15, h // 4, :], True, True,
                           filled(lab) if h == 7 else None)
                for n in (("ks", 0), ("kw", 0), ("kb", 0), ("vt", 0), ("vt", 1), ("vf", 0), ("vf", 1),
                          ("qb", 0), ("qb", 1), ("qf", 0), ("qf", 1), ("kf", 0), ("kf", 1)):
                    pe.wait_ge(*taken(n))
                qa = lambda h, qt: QA[:, h // 2, qt * P:(qt + 1) * P]
                attention("slc", 2, qa, lambda h, w: KS[:, h // 4, h % 2, 0:w],
                          lambda h, kt: VT[:, kt, (h // 4) * 64:(h // 4 + 1) * 64], 64, True)
                attention("win", 2, qa, lambda h, w: KW[:, h // 4, h % 2, 0:w],
                          lambda h, kt: VT[:, kt, 128 + (h // 4) * 64:128 + (h // 4 + 1) * 64], 64, True)
                turn_o("nsa", lambda qt: taken(("o", "win", 1, qt)))
                attention("swa", 2, lambda h, qt: QB[:, h // 2, qt * P:(qt + 1) * P],
                          lambda h, w: KB[:, h // 4, h % 2, 0:w],
                          lambda h, kt: VT[:, kt, 256 + (h // 4) * 64:256 + (h // 4 + 1) * 64], 64, True)
                turn_o("swa", lambda qt: taken(("o", "swa", 1, qt)))
                pe.wait_ge(*sig["decay sums"].after(0))
                attention("fox", 2, lambda h, qt: QF[:, h // 2, qt * P:(qt + 1) * P],
                          lambda h, w: KF[:, h // 2, h % 2, 0:w],
                          lambda h, kt: VF[:, kt, h * 64:(h + 1) * 64], 64, True,
                          extra=lambda h, qt, w: ((CF[:, 0, qt * P:(qt + 1) * P], ident[:, h:h + 1].broadcast_to([P, w])),
                                                  (ident[:, h:h + 1].broadcast_to([P, P]), CF[:, 1, 0:w])))
                turn_o("fox", lambda qt: taken(("o", "fox", 1, qt)))
                merge(mergedB)
                turn_x(x, ("norm", 1), lambda tt: sig["x normed"].after((1, tt)))
                ffn(1, ("norm", 1))
                turn_x(x, ("norm", 2), lambda tt: sig["x normed"].after((2, tt)))

        @block.sync
        def _(sp):
            sp.dma_start(cst[:, :], a["consts"]).then_inc(sig["consts"].sem, 16)
            sp.dma_start(x[:, :, :], a["x"].rearrange("(t p) d -> p t d", p=P)).then_inc(sig["x loaded"].sem, 16)
            sp.dma_start(memraw, a["mem"].rearrange("(t p) d -> p t d", p=P)).then_inc(sig["mem loaded"].sem, 16)
            sp.nop().then_inc(sig["slot free"].sem, R - 1)

            def load(r, n, free):
                sp.wait_ge(sig["slot free"].sem, free)
                sp.dma_start(ring[:, r, :], a["weights"][bass.ds(n, 1), :, :].rearrange("a p n -> (a p) n"))\
                  .then_inc(sig[f"slot {r} loaded"].sem, 16)

            with sp.Fori(0, 2 * DEPTH) as layer:
                for r in range(R):
                    load(r, layer * SLOTS + r, layer * SLOTS + r + (2 if r < R - 1 else 1))
                with sp.Fori(1, PASSES - 1) as go:
                    for r in range(R):
                        n = layer * SLOTS + go * R + r
                        load(r, n, n + 1)
                for r in range(R - 1):
                    n = layer * SLOTS + (PASSES - 1) * R + r
                    load(r, n, n + 1)
            sp.wait_ge(*sig["x normed"].value_at_end())
            sp.dma_start(a["out"].rearrange("(t p) d -> p t d", p=P), x[:, :, :]).then_inc(sig["out stored"].sem, 16)
            sp.wait_ge(sig["out stored"].sem, 16)

        @block.gpsimd
        def _(pool):
            def power(label, n):
                pool.wait_ge(*sig["variance"].after(label))
                pool.tensor_tensor(st[:, 8:8 + n], st[:, 0:n], half[:, 0:n], ALU.pow).then_inc(*sig["rstd"].up(label))

            def load_params(layer):
                pool.dma_start(par[:, :], a["params"][bass.ds(layer, 1), :, :].rearrange("a p n -> (a p) n"))\
                    .then_inc(*sig["params"].up(by=16))

            def load_rows(q):
                pool.dma_start(lnr, a["rows"][bass.ds(q, 1), :, :].partition_broadcast(P) if 0 else rows_of(q))\
                    .then_inc(*sig["rows"].up(by=16))

            def rows_of(q):
                v = a["rows"][bass.ds(q, 1), :, :]
                return bass.AP(v.tensor, v.offset, [[0, P], [D, 2], [1, D]])

            with region(pool, PREP):
                pool.dma_start(flatten(MASK), a["masks"]).then_inc(sig["masks"].sem, 16)
                p = a["pos"]
                pool.dma_start(posi, bass.AP(p.tensor, p.offset, [[0, P], [1, S]])).then_inc(sig["positions"].sem, 16)
                pool.wait_ge(sig["consts"].sem, 16)
                power("mem", 2)
            with region(pool, BLOCK1) as l:
                for h in range(2):
                    pool.wait_ge(*sig[f"T{h} read"].value(0))
                load_params(l)
                power(0, 2)
                power(1, 2)
                power("latent", 4)
                power("recurrence", 8)
                power(2, 2)
            with region(pool, BETWEEN):
                for h in range(2):
                    pool.wait_ge(*sig[f"T{h} read"].value(0))
                pool.dma_start(scf[0:32, 0:1024], a["onehots"]).then_inc(*sig["rel tables"].up(by=16))
                pool.dma_start(relb, a["relb"]).then_inc(*sig["rel tables"].up(by=16))
                pool.dma_start(relmask, a["relmask"]).then_inc(*sig["rel tables"].up(by=16))
                for z in (KS, KW, KB, KF):
                    v = z.rearrange("p a b c -> p (a b c)")
                    pool.memset(v, 0.0).then_inc(*sig["cleared"].up())
                for z in (KC, CF):
                    pool.memset(z.rearrange("p a b -> p (a b)"), 0.0).then_inc(*sig["cleared"].up())
                load_rows(0)
                power("final", 2)
                pool.wait_ge(*sig["rel summed"].after(0))
                pool.dma_start(rel_dram, relsum).then_inc(*sig["rel stored"].up(by=16))
                pool.wait_ge(*sig["rel stored"].value(16))
                pool.dma_start(BR, bass.AP(rel_dram.tensor, rel_dram.offset + 1, [[1, P], [512, 16], [1, S]]))\
                    .then_inc(*sig["bias"].up(by=16))
            with region(pool, BLOCK2) as l:
                for h in range(2):
                    pool.wait_ge(*sig[f"T{h} read"].value(0))
                load_params(l + DEPTH)
                load_rows(l * 3 + 1)
                power(0, 2)
                pool.wait_ge(*sig["merged"].after("all"))
                load_rows(l * 3 + 2)
                power(1, 2)
                for h in range(2):
                    pool.wait_ge(*taken(("norm", 1, 1, h)))
                load_rows(l * 3 + 3)
                power(2, 2)

        @block.vector
        def _(dve):
            def link(i):
                i.then_inc(*sig["vector step"].up())
                dve.wait_ge(*sig["vector step"].value(sig["vector step"].count[places["made in"]]))

            def own():
                dve.wait_ge(*sig["vector step"].value(sig["vector step"].count[places["made in"]]))

            tt_, ts_, stt_ = dve.tensor_tensor, dve.tensor_scalar, dve.scalar_tensor_tensor

            def variance(label, parts):
                for n, (src, dst, count) in enumerate(parts):
                    i = ts_(dst, src, 1.0 / count, 1e-6 if places["made in"] != BLOCK2 else 1e-5, ALU.mult, ALU.add)
                i.then_inc(*sig["variance"].up(label))
                dve.wait_ge(*sig["rstd"].after(label))

            def gained(label, gain):
                for tt in range(TT):
                    for h in range(2):
                        lab = label + (tt, h)
                        dve.wait_ge(*full(lab))
                        o = xT[:, 4 * h:4 * h + 4, tt * P:(tt + 1) * P]
                        src = at(lab).rearrange("p (q c) -> p q c", q=4)
                        if gain is None:
                            dve.tensor_copy(o, src).then_inc(*read(lab))
                        else:
                            g = gain[:, 4 * h:4 * h + 4].unsqueeze(2).broadcast_to([P, 4, P])
                            tt_(o, src, g, ALU.mult).then_inc(*read(lab))

            def rms(i, gain):
                dve.wait_ge(*sig["square sum"].after((i, 1)))
                variance(i, [(st[:, 16:18], st[:, 0:2], D)])
                for tt in range(TT):
                    ts_(xn[:, tt, :], x[:, tt, :], st[:, 8 + tt:9 + tt], None, ALU.mult)\
                        .then_inc(*sig["scaled"].up((i, tt)))
                gained(("norm", i), gain)

            def add_sums(f):
                for b in range(4):
                    lab = ("y", f, b)
                    dve.wait_ge(*full(lab))
                    v = x[:, b // 2, (b % 2) * 512:(b % 2 + 1) * 512]
                    stt_(v, at(lab), 0.5, v, ALU.mult, ALU.add).then_inc(*read(lab))

            def layer_norm(i, f):
                for b in range(4):
                    lab = ("y", f, b)
                    dve.wait_ge(*full(lab))
                    v = x[:, b // 2, (b % 2) * 512:(b % 2 + 1) * 512]
                    stt_(v, at(lab), 0.5, v, ALU.mult, ALU.add, accum_out=st[:, 20 + b:21 + b]).then_inc(*read(lab))
                for b in range(4):
                    dve.wait_ge(*taken(("y", f, b)))
                link(tt_(st[:, 24:26], st[:, 20:24:2], st[:, 21:24:2], ALU.add))
                ts_(st[:, 26:28], st[:, 24:26], -1.0 / D, None, ALU.mult).then_inc(*sig["mean"].up(i))
                dve.wait_ge(*sig["square sum"].after((i, 1)))
                variance(i, [(st[:, 16:18], st[:, 0:2], D)])
                link(tt_(st[:, 28:30], st[:, 26:28], st[:, 8:10], ALU.mult))
                dve.wait_ge(*sig["rows"].value(16 * (i + 1)))
                for tt in range(TT):
                    link(ts_(x[:, tt, :], x[:, tt, :], st[:, 8 + tt:9 + tt], st[:, 28 + tt:29 + tt], ALU.mult, ALU.add))
                    link(tt_(x[:, tt, :], x[:, tt, :], lnr[:, 0, :], ALU.mult))
                    tt_(x[:, tt, :], x[:, tt, :], lnr[:, 1, :], ALU.add).then_inc(*sig["x normed"].up((i, tt)))
                gained(("norm", i), None)

            def scale_x():
                link(ts_(x[:, :, :], x[:, :, :], ALPHA, None, ALU.mult))

            def hidden(f):
                for j in range(FT):
                    lab = ("ab", f, j)
                    dve.wait_ge(*sig["silu"].after((f, j)))
                    tt_(hT[:, j % 2, :], sil[:, j % 2, :], at(lab)[:, S:2 * S], ALU.mult).then_inc(*read(lab))

            def soften(name, n, hb, qt, w, scale, bias, sink):
                sc = Sc[:, n % 2, :, 0:w]
                for b in range(2):
                    lab = ("s", name, hb, qt, b)
                    dve.wait_ge(*full(lab))
                    src = at(lab).rearrange("p (j c) -> p j c", j=2)[:, :, 0:w]
                    if bias is None:
                        ts_(sc[:, 2 * b:2 * b + 2, :], src, scale, None, ALU.mult).then_inc(*read(lab))
                    else:
                        stt_(sc[:, 2 * b:2 * b + 2, :], src, scale, bias(hb, b, S - w if qt == 0 else 0, w),
                             ALU.mult, ALU.add).then_inc(*read(lab))
                for b in range(2):
                    dve.wait_ge(*taken(("s", name, hb, qt, b)))
                m = st[:, 32 + 4 * (n % 2):36 + 4 * (n % 2)]
                link(dve.tensor_reduce(m, sc, AX, ALU.max))
                if sink is not None:
                    link(tt_(m, m, sink[:, 4 * hb:4 * hb + 4], ALU.max))
                    sk = st[:, 40 + 4 * (n % 2):44 + 4 * (n % 2)]
                    tt_(sk, sink[:, 4 * hb:4 * hb + 4], m, ALU.subtract).then_inc(*sig["sink shifted"].up((name, hb, qt)))
                tt_(sc, sc, m.unsqueeze(2).broadcast_to([P, 4, w]), ALU.subtract)\
                    .then_inc(*sig["shifted"].up((name, hb, qt)))

            def weigh(name, n, hb, qt, w, dv, sink, gate, first):
                dve.wait_ge(*sig["weights"].after((name, hb, qt)))
                sums, r = st[:, 48:52], st[:, 52:56]
                link(dve.tensor_reduce(sums, Sc[:, n % 2, :, 0:w], AX, ALU.add))
                if sink is not None:
                    link(tt_(sums, sums, st[:, 40 + 4 * (n % 2):44 + 4 * (n % 2)], ALU.add))
                link(dve.reciprocal(r, sums))
                if gate is not None:
                    link(tt_(r, r, gg[:, qt, :].rearrange("p (h b) -> p h b", b=3)[:, 4 * hb:4 * hb + 4, gate], ALU.mult))
                lab = ("o", name, hb, qt)
                dve.wait_ge(*full(lab))
                src = at(lab)[:, 0:4 * dv].rearrange("p (j c) -> p j c", j=4)
                o = O[:, qt, hb * 4 * dv:(hb + 1) * 4 * dv].rearrange("p (j c) -> p j c", j=4)
                rb = r.unsqueeze(2).broadcast_to([P, 4, dv])
                if first:
                    tt_(o, src, rb, ALU.mult).then_inc(*read(lab))
                else:
                    tmp = sil[:, 0, :].rearrange("p (j c) -> p j c", j=4)
                    link(tt_(tmp, src, rb, ALU.mult))
                    tt_(o, o, tmp, ALU.add).then_inc(*read(lab))

            def attention(name, hbs, dv, causal, scale, bias, before, sink=None, gate=None, first=True):
                todo = [(hb, qt) for hb in range(hbs) for qt in range(TT)]
                width = lambda qt: S if (qt or not causal) else P
                if before is not None:
                    for t in range(TT):
                        dve.wait_ge(*full(("ot", before, t)))
                for n, (hb, qt) in enumerate(todo):
                    soften(name, n, hb, qt, width(qt), scale, bias, sink)
                    if n:
                        weigh(name, n - 1, *todo[n - 1], width(todo[n - 1][1]), dv, sink, gate, first)
                n = len(todo)
                weigh(name, n - 1, *todo[n - 1], width(todo[n - 1][1]), dv, sink, gate, first)

            def merge(merged):
                for br in range(3):
                    for n in range(4):
                        lab = ("wo", br, n)
                        dve.wait_ge(*full(lab))
                        src = at(lab).rearrange("p (j c) -> p j c", j=2)
                        g = G[:, 8 * br + 2 * n:8 * br + 2 * n + 2, :]
                        o = merged[:, 2 * n:2 * n + 2, :]
                        if br == 0:
                            stt_(o, g, 1.0, src, ALU.add, ALU.mult).then_inc(*read(lab))
                        else:
                            k = 4 * br + n
                            tmp = (sil, hT)[k % 2][:, :, :]
                            if k >= 6:
                                dve.wait_ge(*sig["merged"].after(k - 2))
                            if k >= 8:
                                dve.wait_ge(*sig["merged"].after(k - 4))
                            stt_(tmp, g, 1.0, src, ALU.add, ALU.mult).then_inc(*read(lab))
                            dve.wait_ge(*taken(lab))
                            tt_(o, o, tmp, ALU.add).then_inc(*sig["merged"].up("all" if k == 11 else k))

            causal_bias = lambda hb, b, c, w: CM[:, c:c + w].unsqueeze(1).broadcast_to([P, 2, w])

            with region(dve, PREP):
                dve.wait_ge(sig["consts"].sem, 16)
                dve.wait_ge(sig["positions"].sem, 16)
                an, kk, sn_, cs_, cm_ = (KT[:, i, :] for i in range(5))
                link(dve.tensor_copy(an, posi))
                link(ts_(an, an, invf, None, ALU.mult))
                link(ts_(kk, an, 1.0 / TWO_PI, ROUND, ALU.mult, ALU.add))
                link(ts_(kk, kk, ROUND, None, ALU.subtract))
                for c in PERIOD:
                    link(stt_(an, kk, -c, an, ALU.mult, ALU.add))
                link(ts_(cs_, an, TWO_PI / 4, None, ALU.add))
                link(ts_(cm_, cs_, TWO_PI / 2, -TWO_PI, ALU.is_gt, ALU.mult))
                link(tt_(cs_, cs_, cm_, ALU.add))
                link(ts_(cs_, cs_, PI_IN, -PI_IN, ALU.min, ALU.max))
                ts_(sn_, an, PI_IN, -PI_IN, ALU.min, ALU.max).then_inc(*sig["angles"].up(0))
                dve.wait_ge(*sig["sines"].after(0))
                link(ts_(sn_, sn_, sgn, None, ALU.mult))
                dve.memset(CS[0:64], 1.0).then_inc(*sig["vector step"].up())
                dve.tensor_copy(CS[64:96], cs_[64:96]).then_inc(*sig["vector step"].up())
                dve.tensor_copy(CS[96:128], sn_[96:128]).then_inc(*sig["vector step"].up())
                dve.tensor_copy(CK[:, 0, :], cs_).then_inc(*sig["vector step"].up())
                link(dve.tensor_copy(CK[:, 1, :], sn_))
                dve.wait_ge(sig["mem loaded"].sem, 16)
                dve.wait_ge(*sig["square sum"].after(("mem", 1)))
                variance("mem", [(st[:, 16:18], st[:, 0:2], D)])
                for tt in range(TT):
                    ts_(xn[:, tt, :], memraw[:, tt, :], st[:, 8 + tt:9 + tt], None, ALU.mult)\
                        .then_inc(*sig["scaled"].up(("mem", tt)))
                for tt in range(TT):
                    for h in range(2):
                        lab = ("mem", tt, h)
                        dve.wait_ge(*full(lab))
                        dve.tensor_copy(memT[:, 4 * h:4 * h + 4, tt * P:(tt + 1) * P],
                                        at(lab).rearrange("p (q c) -> p q c", q=4)).then_inc(*read(lab))
                dve.wait_ge(sig["x loaded"].sem, 16)
                dve.wait_ge(sig["masks"].sem, 16)
                link(dve.memset(st[:, 125:126], 0.0))

            with region(dve, BLOCK1):
                dve.wait_ge(*sig["params"].value(16))
                rms(0, par[:, 0:8])
                b2 = par[:, 38:46]
                m, e, s4, lb, oml = lbt[:, 0:4], lbt[:, 4:12], lbt[:, 12:16], lbt[:, 16:20], lbt[:, 20:24]
                lg, zero = lbt[:, 24:32], lbt[:, 32:40]
                link(tt_(m, b2[:, 0:4], b2[:, 4:8], ALU.max))
                link(tt_(e[:, 0:4], b2[:, 0:4], m, ALU.subtract))
                tt_(e[:, 4:8], b2[:, 4:8], m, ALU.subtract).then_inc(*sig["bounds"].up(0))
                hidden(0)
                dve.wait_ge(*sig["bounds made"].after(0))
                link(tt_(s4, e[:, 0:4], e[:, 4:8], ALU.add))
                link(dve.reciprocal(s4, s4))
                link(tt_(e[:, 0:4], e[:, 0:4], s4, ALU.mult))
                link(tt_(e[:, 4:8], e[:, 4:8], s4, ALU.mult))
                link(tt_(lb, e[:, 0:4], e[:, 4:8], ALU.add))
                link(tt_(lb, lb, e[:, 0:4], ALU.subtract))
                link(ts_(lb, lb, par[:, 46:47], None, ALU.mult))
                link(ts_(oml, lb, -1.0, 1.0, ALU.mult, ALU.add))
                link(ts_(zero, lbt[:, 16:24], 0.0, NEG, ALU.is_equal, ALU.mult))
                ts_(lg, lbt[:, 16:24], 1e-18, None, ALU.max).then_inc(*sig["bounds"].up(1))
                dve.wait_ge(*sig["bounds made"].after(1))
                link(tt_(lg, lg, zero, ALU.add))
                add_sums(0)
                rms(1, par[:, 8:16])
                dve.wait_ge(*sig["latent squares"].after(3))
                variance("latent", [(st[:, 16:18], st[:, 0:2], 384), (st[:, 18:20], st[:, 2:4], 256)])
                for b in range(4):
                    dve.wait_ge(*full(("c", b)))
                    t, lo, hi = b % 2, (0, 384)[b // 2], (384, 640)[b // 2]
                    ts_(cn[:, t, lo:hi], at(("c", b))[:, 0:hi - lo], st[:, 8 + b:9 + b], None, ALU.mult)\
                        .then_inc(*read(("c", b)))
                lab = ("kr", 0)
                dve.wait_ge(*full(lab))
                tt_(sil[64:128, :, :], at(lab)[64:128].rearrange("p (a b) -> p a b", a=2), CK[64:128], ALU.mult)\
                    .then_inc(*read(lab))
                dve.wait_ge(*taken(lab))
                tt_(KT[64:128, :, :], sil[64:128, 0:1, :].broadcast_to([64, 8, S]),
                    sil[64:128, 1:2, :].broadcast_to([64, 8, S]), ALU.add).then_inc(*sig["rotary keys"].up(0))
                for i in range(2):
                    lab = ("hf", i)
                    dve.wait_ge(*sig["forget read"].after(i))
                    ts_(GC[:, 2 * i:2 * i + 2, :], at(lab).rearrange("p (a b) -> p a b", a=2), 0.0, None, ALU.min)\
                        .then_inc(*read(lab))
                for i in range(2):
                    dve.wait_ge(*taken(("hf", i)))
                wide = lambda v: v.unsqueeze(2).broadcast_to([P, 4, S])
                tt_(KH, KH, wide(oml), ALU.mult).then_inc(*sig["recurrence keys"].up(0))
                dve.wait_ge(*sig["forget log"].after(0))
                link(tt_(GC, GC, EB[0], ALU.subtract))
                link(tt_(GC, GC, wide(lg[:, 4:8]), ALU.add))
                link(tt_(EB[1], GC, wide(lg[:, 0:4]), ALU.subtract))
                link(tt_(GC, GC, wide(lg[:, 0:4]), ALU.max))
                stt_(EB[1], EB[1], -1.0, EB[1], ALU.mult, ALU.min).then_inc(*sig["forget gap"].up(0))
                dve.wait_ge(*sig["forget log"].after(1))
                link(tt_(EB[0], GC, EB[1], ALU.add))
                for h in range(4):
                    i = dve.tensor_tensor_scan(GC[:, h, :], ones, EB[0][:, h, :], 0.0, ALU.mult, ALU.add)
                    i.then_inc(*sig["vector step"].up())
                dve.wait_ge(*sig["vector step"].value(sig["vector step"].count[places["made in"]]))
                for t in range(TT):
                    for h, (lo, n) in enumerate(((0, 3), (3, 2))):
                        lab = ("cT", t, h)
                        dve.wait_ge(*full(lab))
                        tt_(cT[:, lo:lo + n, t * P:(t + 1) * P], at(lab)[:, 0:n * P].rearrange("p (q c) -> p q c", q=n),
                            par[:, 32 + lo:32 + lo + n].unsqueeze(2).broadcast_to([P, n, P]), ALU.mult)\
                            .then_inc(*read(lab))
                tt_(memTg, memT, par[:, 24:32].unsqueeze(2).broadcast_to([P, KD, S]), ALU.mult)\
                    .then_inc(*sig["memory scaled"].up(0))
                for h in range(2):
                    for n in range(2):
                        lab = (("uq", h), n)
                        dve.wait_ge(*full(lab))
                        tt_(QT[:, 4 * h + 2 * n:4 * h + 2 * n + 2, :], at(lab).rearrange("p (a b) -> p a b", a=2),
                            CS.unsqueeze(1).broadcast_to([P, 2, S]), ALU.mult).then_inc(*read(lab))

                def halves(t, i):
                    v = t.rearrange("p h t -> p (h t)").rearrange("p (n w) -> p n w", w=2 << i)
                    return v[:, :, 0:1 << i], v[:, :, 1 << i:2 << i]

                def gaps(i):
                    g0, g1 = halves(GC, i)
                    e0, e1 = halves(EB[i % 2], i)
                    if i >= 2:
                        dve.wait_ge(*sig["decayed"].after(i - 2))
                        own()
                    mid = g0[:, :, (1 << i) - 1:1 << i].broadcast_to(list(g0.shape))
                    tt_(e0, mid, g0, ALU.subtract).then_inc(*sig["gaps"].up((i, 0)))
                    tt_(e1, g1, mid, ALU.subtract).then_inc(*sig["gaps"].up((i, 1)))

                def decayed(i):
                    dve.wait_ge(*sig["decays"].after(i))
                    if i >= 2:
                        dve.wait_ge(*full(("level", i - 2, 1)))
                    e0, e1 = halves(EB[i % 2], i)
                    t0, t1 = halves(TL[i % 2], i)
                    tt_(t0, e0, halves(KH, i)[0], ALU.mult).then_inc(*sig["vector step"].up())
                    tt_(t1, e1, halves(QH, i)[1], ALU.mult).then_inc(*sig["decayed"].up(i))

                def chosen(i):
                    for t in range(2 if i < 7 else 1):
                        lab = ("level", i, t)
                        dve.wait_ge(*full(lab))
                        src = at(lab).rearrange("p (h c) -> p h c", h=4)
                        if i < 7:
                            dve.wait_ge(*taken(("diag", t) if i == 0 else ("level", i - 1, t)))
                            c = 128 + 2 * i + t
                            dve.tensor_copy(st[:, c:c + 1], st[:, 125:126])
                            dve.copy_predicated(Am[:, t], MASK[:, i:i + 1, :].broadcast_to([P, 4, P]), src)\
                                .then_inc(*read(lab))
                        else:
                            dve.tensor_copy(Aoff, src).then_inc(*read(lab))

                dve.wait_ge(*sig["recurrence keys"].after(0))
                for i in range(2):
                    dve.wait_ge(*taken(("hq", i)))
                gaps(0)
                for t in range(TT):
                    lab = ("diag", t)
                    dve.wait_ge(*full(lab))
                    tt_(Am[:, t], at(lab).rearrange("p (h c) -> p h c", h=4),
                        ident.unsqueeze(1).broadcast_to([P, 4, P]), ALU.mult).then_inc(*read(lab))
                    dve.wait_ge(*taken(lab))
                for i in range(1, 10):
                    if i < 8:
                        gaps(i)
                    if i <= 8:
                        decayed(i - 1)
                    if i >= 2:
                        chosen(i - 2)
                for t in range(TT):
                    dve.wait_ge(*sig["out squares"].after(t))
                    link(dve.tensor_reduce(st[:, 64 + 4 * t:68 + 4 * t], O[:, t, :].rearrange("p (h c) -> p h c", h=4),
                                           AX, ALU.add))
                variance("recurrence", [(st[:, 64:72], st[:, 0:8], P)])
                for t in range(TT):
                    lab = ("ho", t)
                    tt_(O[:, t, :].rearrange("p (h c) -> p h c", h=4), at(lab).rearrange("p (h c) -> p h c", h=4),
                        st[:, 8 + 4 * t:12 + 4 * t].unsqueeze(2).broadcast_to([P, 4, P]), ALU.mult).then_inc(*read(lab))
                    dve.wait_ge(*taken(lab))
                    dve.wait_ge(*taken(("hgate", t)))
                    tt_(GH[:, t, :], O[:, t, :], GH[:, t, :], ALU.mult).then_inc(*sig["recurrence out"].up(t))
                attention("mla", 2, 64, True, 96.0 ** -0.5, causal_bias, None)
                for t in range(TT):
                    lab = ("ot", "hg", t)
                    dve.wait_ge(*full(lab))
                    ts_(OT[:, 1, :, t * P:(t + 1) * P], at(lab).rearrange("p (q c) -> p q c", q=4), par[:, 37:38], None,
                        ALU.mult).then_inc(*read(lab))
                attention("mem", 1, P, False, 128.0 ** -0.5, None, "mla")
                merge(mergedA)
                add_sums("mix")
                rms(2, par[:, 16:24])
                hidden(1)
                add_sums(1)

            with region(dve, BETWEEN):
                dve.wait_ge(*sig["square sum"].after(("final", 1)))
                variance("final", [(st[:, 16:18], st[:, 0:2], D)])
                dve.wait_ge(*sig["rows"].value(16))
                for tt in range(TT):
                    stt_(x[:, tt, :], x[:, tt, :], st[:, 8 + tt:9 + tt], lnr[:, 0, :], ALU.mult, ALU.mult)\
                        .then_inc(*sig["x normed"].up(("final", tt)))
                dve.wait_ge(*sig["rel tables"].value(48))
                dve.wait_ge(*full("rel"))
                tt_(relsum, at("rel")[0:16, :], relmask, ALU.add).then_inc(*read("rel"))
                dve.wait_ge(*taken("rel"))
                ts_(relsum, relsum, 0.0, None, ALU.add).then_inc(*sig["rel summed"].up(0))
                dve.wait_ge(*full("rel cmp"))
                src = at("rel cmp")[:, 0:240].rearrange("p (q c h) -> p q h c", q=2, c=15)
                for qt in range(TT):
                    i = tt_(CB[:, qt], src[:, qt], cmask[:, 15 * qt:15 * qt + 15].unsqueeze(1).broadcast_to([P, 8, 15]),
                            ALU.add)
                    i.then_inc(*(read("rel cmp") if qt else sig["vector step"].up()))
                gained(("norm", "final"), None)

            with region(dve, BLOCK2):
                dve.wait_ge(*sig["params"].value(16))
                dve.wait_ge(*sig["x normed"].value(0))
                for b in range(2):
                    dve.wait_ge(*sig[f"A{b} read"].value(0))
                for h in range(2):
                    dve.wait_ge(*sig[f"T{h} read"].value(0))
                scale_x()
                hidden(0)
                layer_norm(0, 0)
                scale_x()
                hb = st[:, 96:120]
                ts_(hb, par[:, 0:24], 0.5, None, ALU.mult).then_inc(*sig["half gate bias"].up(0))
                dve.wait_ge(sig["cleared"].sem, 6)
                two = lambda lab: at(lab).rearrange("p (a b) -> p a b", a=2)

                def both_halves(lab, lo, hi):
                    dve.wait_ge(*full(lab))
                    dve.tensor_copy(lo[0:64], two(lab)[0:64]).then_inc(*sig["vector step"].up())
                    dve.tensor_copy(hi[64:128], two(lab)[64:128]).then_inc(*read(lab))

                def compress_blocks(z, lab, pe_cols):
                    dve.wait_ge(*full(lab))
                    link(dve.tensor_copy(Z2[0:64, :, :], two(lab)[0:64]))
                    dve.tensor_copy(Z2[64:128, :, 0:S - 1], two(lab)[64:128, :, 1:S]).then_inc(*read(lab))
                    dve.wait_ge(*taken(lab))
                    if z == "v":
                        dve.wait_ge(*full(("cmp", "k", 1)))
                    for g in range(2):
                        zz = Z2[:, g, :]
                        src = bass.AP(zz.tensor, zz.offset, [zz.ap[0], (2, 16), (16, 15)])
                        i = tt_(ZB[:, :, 15 * g:15 * g + 15], src, pe_cols.unsqueeze(2).broadcast_to([P, 16, 15]), ALU.add)
                        i.then_inc(*(sig["blocks"].up(z) if g else sig["vector step"].up()))

                both_halves(("ks", 0), KS[:, :, 0, :], KS[:, :, 1, :])
                both_halves(("kw", 0), KW[:, :, 0, :], KW[:, :, 1, :])
                compress_blocks("k", ("kc", 0), par[:, 24:40])
                lab = ("vc", 0)
                dve.wait_ge(*full(lab))
                dve.wait_ge(*sig["blocks"].after("k"))
                link(dve.tensor_copy(Z2[0:64, :, :], two(lab)[0:64]))
                dve.tensor_copy(Z2[64:128, :, 0:S - 1], two(lab)[64:128, :, 1:S]).then_inc(*read(lab))
                dve.wait_ge(*taken(lab))
                both_halves(("kb", 0), KB[:, :, 0, :], KB[:, :, 1, :])
                fz, fm, fc = (FS[0:8, i, :] for i in range(3))
                dve.wait_ge(*full("f"))
                ts_(fz, at("f")[0:8, 0:S], par[0:8, 440:441], None, ALU.add).then_inc(*read("f"))
                dve.wait_ge(*taken("f"))
                link(ts_(fm, fz, 0.0, None, ALU.min))
                stt_(fz, fz, -1.0, fz, ALU.mult, ALU.min).then_inc(*sig["fox gap"].up(0))
                dve.wait_ge(*sig["fox log"].after(0))
                link(tt_(fm, fm, fz, ALU.subtract))
                link(dve.tensor_tensor_scan(fc, ones[0:8], fm, 0.0, ALU.mult, ALU.add))
                link(ts_(CF[0:8, 0, :], fc, 8.0, None, ALU.mult))
                ts_(CF[0:8, 1, :], fc, -8.0, None, ALU.mult).then_inc(*sig["decay sums"].up(0))
                for n in range(2):
                    both_halves(("kf", n), KF[:, 2 * n:2 * n + 2, 0, :], KF[:, 2 * n:2 * n + 2, 1, :])
                dve.wait_ge(*full(("cmp", "k", 1)))
                for g in range(2):
                    zz = Z2[:, g, :]
                    src = bass.AP(zz.tensor, zz.offset, [zz.ap[0], (2, 16), (16, 15)])
                    i = tt_(ZB[:, :, 15 * g:15 * g + 15], src, par[:, 40:56].unsqueeze(2).broadcast_to([P, 16, 15]), ALU.add)
                    i.then_inc(*(sig["blocks"].up("v") if g else sig["vector step"].up()))
                lab = ("cmp out", "k")
                dve.wait_ge(*full(lab))
                dve.tensor_copy(KC[0:64, 0, :], at(lab)[0:64, 0:30]).then_inc(*sig["vector step"].up())
                dve.tensor_copy(KC[64:128, 1, :], at(lab)[64:128, 0:30]).then_inc(*read(lab))
                lab = ("cmp out", "v")
                dve.wait_ge(*full(lab))
                dve.tensor_copy(VC[0:15, :, :], at(lab)[0:15, 0:128].rearrange("p (g c) -> p g c", g=2))\
                    .then_inc(*read(lab))
                dve.wait_ge(*sig["small gates"].after(1))
                link(ts_(gg, gg, 0.5, 0.5, ALU.mult, ALU.add))
                for qt in range(TT):
                    lab = ("sc", qt)
                    sc = scf[:, qt * 1024:qt * 1024 + 120].rearrange("p (h c) -> p h c", h=8)
                    dve.wait_ge(*full(lab))
                    stt_(sc, at(lab)[:, 0:120].rearrange("p (h c) -> p h c", h=8), 0.125, CB[:, qt], ALU.mult, ALU.add)\
                        .then_inc(*read(lab))
                    dve.wait_ge(*taken(lab))
                    m = st[:, 56 + 32 * qt:64 + 32 * qt]
                    link(dve.tensor_reduce(m, sc, AX, ALU.max))
                    link(ts_(m, m, LOW, None, ALU.max))
                    tt_(sc, sc, m.unsqueeze(2).broadcast_to([P, 8, 15]), ALU.subtract)\
                        .then_inc(*sig["shifted"].up(("cmp", qt)))
                for qt in range(TT):
                    dve.wait_ge(*sig["weights"].after(("cmp", qt)))
                    sc = scf[:, qt * 1024:qt * 1024 + 120].rearrange("p (h c) -> p h c", h=8)
                    r = st[:, 72 + 8 * qt:80 + 8 * qt]
                    link(dve.tensor_reduce(r, sc, AX, ALU.add))
                    link(ts_(r, r, 1e-30, None, ALU.max))
                    link(dve.reciprocal(r, r))
                    link(tt_(r, r, gg[:, qt, :].rearrange("p (h b) -> p h b", b=3)[:, :, 0], ALU.mult))
                    lab = ("o", "cmp", 0, qt)
                    dve.wait_ge(*full(lab))
                    tt_(O[:, qt, :].rearrange("p (h c) -> p h c", h=8), at(lab).rearrange("p (h c) -> p h c", h=8),
                        r.unsqueeze(2).broadcast_to([P, 8, 64]), ALU.mult).then_inc(*read(lab))
                    dve.wait_ge(*taken(lab))
                dve.wait_ge(*sig["A1 read"].value(0))
                table = lambda h0: (lambda hb, b, c, w: BIAS[:, h0 + 4 * hb + 2 * b:h0 + 4 * hb + 2 * b + 2, c:c + w])
                attention("slc", 2, 64, True, 0.125, table(0), None, gate=1, first=False)
                attention("win", 2, 64, True, 0.125, table(0), None, gate=2, first=False)
                attention("swa", 2, 64, True, 0.125, table(8), "nsa", sink=par[:, 441:449])
                attention("fox", 2, 64, True, 0.125, causal_bias, "swa")
                merge(mergedB)
                layer_norm(1, "mix")
                scale_x()
                hidden(1)
                layer_norm(2, 1)

        @block.scalar
        def _(act):
            def go(out, in_, func, up, **kw):
                act.activation(out, in_, func, **kw).then_inc(*up)

            def step():
                return sig["scalar step"].up()

            def linked():
                act.wait_ge(*sig["scalar step"].value(sig["scalar step"].count[places["made in"]]))

            def squares(i, src, bias=None):
                for tt in range(TT):
                    kw = {} if bias is None else {"bias": bias[:, tt:tt + 1]}
                    act.activation(xn[:, tt, :], src[:, tt, :], ACT.Square, accum_out=st[:, 16 + tt:17 + tt], **kw)\
                        .then_inc(*sig["square sum"].up((i, tt)))

            def hidden(f):
                for j in range(FT):
                    lab = ("ab", f, j)
                    act.wait_ge(*full(lab))
                    go(sil[:, j % 2, :], at(lab)[:, 0:S], ACT.Silu, sig["silu"].up((f, j)))

            def copy(lab, out, n=None, func=ACT.Copy, **kw):
                act.wait_ge(*full(lab))
                src = at(lab)
                if len(out.shape) == 3:
                    src = src[0:out.shape[0], 0:out.shape[1] * out.shape[2]].rearrange("p (a b) -> p a b", a=out.shape[1])
                else:
                    src = src[0:out.shape[0], 0:out.shape[1]]
                go(out, src, func, read(lab), **kw)

            def attention(name, hbs, causal, sink=False):
                todo = [(hb, qt) for hb in range(hbs) for qt in range(TT)]
                for n, (hb, qt) in enumerate(todo):
                    kts = TT if (qt or not causal) else 1
                    if sink:
                        act.wait_ge(*sig["sink shifted"].after((name, hb, qt)))
                        sk = st[:, 40 + 4 * (n % 2):44 + 4 * (n % 2)]
                        go(sk, sk, ACT.Exp, step())
                    act.wait_ge(*sig["shifted"].after((name, hb, qt)))
                    sc = Sc[:, n % 2, :, 0:kts * P]
                    if sink:
                        linked()
                    go(sc, sc, ACT.Exp, sig["weights"].up((name, hb, qt)))
                    for kt in range(kts):
                        copy(("pt", name, hb, qt, kt), PT[:, n % 2, kt, :, :])

            def turned(name, br):
                for qt in range(TT):
                    copy(("ot", name, qt), OT[:, br, :, qt * P:(qt + 1) * P])

            with region(act, PREP):
                act.wait_ge(sig["mem loaded"].sem, 16)
                squares("mem", memraw)
                act.wait_ge(*sig["angles"].after(0))
                go(KT[:, 2, :], KT[:, 2, :], ACT.Sin, step())
                go(KT[:, 3, :], KT[:, 3, :], ACT.Sin, sig["sines"].up(0))
                act.wait_ge(sig["x loaded"].sem, 16)
                for h in range(2):
                    act.wait_ge(*full(("mem", 1, h)))

            with region(act, BLOCK1):
                x_is_done(act, None)
                squares(0, x)
                lb_e, lb_g = lbt[:, 4:12], lbt[:, 24:32]
                act.wait_ge(*sig["bounds"].after(0))
                go(lb_e, lb_e, ACT.Exp, sig["bounds made"].up(0))
                hidden(0)
                act.wait_ge(*sig["bounds"].after(1))
                go(lb_g, lb_g, ACT.Ln, sig["bounds made"].up(1))
                x_is_done(act, BEFORE[1])
                squares(1, x)
                for b in range(4):
                    act.wait_ge(*full(("c", b)))
                    t, lo, hi = b % 2, (0, 384)[b // 2], (384, 640)[b // 2]
                    if b == 0:
                        for h in range(2):
                            act.wait_ge(*taken(("norm", 1, 1, h)))
                    act.activation(cn[:, t, lo:hi], at(("c", b))[:, 0:hi - lo], ACT.Square,
                                   accum_out=st[:, 16 + b:17 + b]).then_inc(*sig["latent squares"].up(b))
                for n in range(2):
                    copy(("mq", n), QM[:, 2 * n:2 * n + 2, :])
                for n in range(2):
                    copy(("hq", n), QH[:, 2 * n:2 * n + 2, :], func=ACT.Silu)
                for n in range(2):
                    lab = ("hf", n)
                    act.wait_ge(*full(lab))
                    v = at(lab).rearrange("p (a b) -> p a b", a=2)
                    go(KH[:, 2 * n:2 * n + 2, :], v, ACT.Sigmoid, step(), scale=-1.0)
                    go(EB[0][:, 2 * n:2 * n + 2, :], v, ACT.Abs, sig["forget read"].up(n))
                for t in range(TT):
                    copy(("hi", t), VH[:, t, :])
                for t in range(TT):
                    copy(("hgate", t), GH[:, t, :], func=ACT.Silu)
                act.wait_ge(*sig["forget read"].after(1))
                go(EB[0], EB[0], ACT.Exp, step(), scale=-1.0)
                linked()
                go(EB[0], EB[0], ACT.Ln, sig["forget log"].up(0), bias=1.0)
                act.wait_ge(*sig["forget gap"].after(0))
                go(EB[1], EB[1], ACT.Exp, step())
                linked()
                go(EB[1], EB[1], ACT.Ln, sig["forget log"].up(1), bias=1.0)
                for n in range(12):
                    copy(("gate", n), G[:, 2 * n:2 * n + 2, :], func=ACT.Tanh, scale=0.5)
                for n in range(4):
                    copy(("uk", n), KT[0:64, 2 * n:2 * n + 2, :])
                for t in range(TT):
                    copy(("uv", t), VM[:, t, :])
                for n in range(2):
                    copy(("mk", n), KM[:, 2 * n:2 * n + 2, :])
                for t in range(TT):
                    copy(("mv", t), VX[:, t, :])
                for i in range(8):
                    act.wait_ge(*sig["gaps"].after((i, 1)))
                    go(EB[i % 2], EB[i % 2], ACT.Exp, sig["decays"].up(i))
                for t in range(TT):
                    act.wait_ge(*full(("ho", t)))
                    go(O[:, t, :], at(("ho", t)), ACT.Square, sig["out squares"].up(t))
                attention("mla", 2, True)
                turned("mla", 0)
                attention("mem", 1, False)
                turned("mem", 2)
                x_is_done(act, BEFORE[2])
                squares(2, x)
                hidden(1)

            with region(act, BETWEEN):
                x_is_done(act, None)
                squares("final", x)
                for n in range(8):
                    copy(("flip", n), BIAS[:, 2 * n:2 * n + 2, :])

            with region(act, BLOCK2):
                hidden(0)
                act.wait_ge(*sig["mean"].after(0))
                squares(0, x, st[:, 26:28])
                for n in range(2):
                    copy(("qa", n), QA[:, 2 * n:2 * n + 2, :])
                for n in range(2):
                    copy(("qb", n), QB[:, 2 * n:2 * n + 2, :])
                for t in range(TT):
                    copy(("vt", t), VT[:, t, :])
                for t in range(TT):
                    act.wait_ge(*taken(("vt", t)))
                    go(gg[:, t, :], VT[:, t, 384:408], ACT.Tanh, sig["small gates"].up(t), scale=0.5)
                fz = FS[0:8, 0, :]
                act.wait_ge(*sig["fox gap"].after(0))
                go(fz, fz, ACT.Exp, step())
                linked()
                go(fz, fz, ACT.Ln, sig["fox log"].up(0), bias=1.0)
                for n in range(2):
                    copy(("qf", n), QF[:, 2 * n:2 * n + 2, :])
                for t in range(TT):
                    copy(("vf", t), VF[:, t, :])
                for z in ("k", "v"):
                    if z == "v":
                        act.wait_ge(*full(("cmp out", "k")))
                    for m in range(2):
                        copy(("cmp", z, m), HC[:, m, :], func=ACT.Gelu_apprx_tanh)
                act.wait_ge(*sig["half gate bias"].after(0))
                for n in range(12):
                    lab = ("gate", n)
                    act.wait_ge(*full(lab))
                    for j in range(2):
                        i = 2 * n + j
                        go(G[:, i, :], at(lab)[:, j * S:(j + 1) * S], ACT.Tanh, read(lab) if j else step(),
                           bias=st[:, 96 + i:97 + i], scale=0.5)
                for qt in range(TT):
                    act.wait_ge(*sig["shifted"].after(("cmp", qt)))
                    sc = scf[:, qt * 1024:qt * 1024 + 120]
                    go(sc, sc, ACT.Exp, sig["weights"].up(("cmp", qt)))
                for qt in range(TT):
                    for b in range(2):
                        copy(("ptc", qt, b), PT[0:15, qt, b, :, :])
                attention("slc", 2, True)
                attention("win", 2, True)
                turned("nsa", 0)
                attention("swa", 2, True, sink=True)
                turned("swa", 1)
                attention("fox", 2, True)
                turned("fox", 2)
                act.wait_ge(*sig["mean"].after(1))
                squares(1, x, st[:, 26:28])
                hidden(1)
                act.wait_ge(*sig["mean"].after(2))
                squares(2, x, st[:, 26:28])

        for b in BANK:
            for r in range(len(ITERATIONS)):
                put, got = ({k[1] for k in sig[b + w].labels if k[0] == r} for w in (" full", " read"))
                assert put == got, (b, r, put ^ got)
        return sig.counts()


TWO_PI = 2.0 * float(np.pi)
ROUND = 1.5 * 2.0 ** 23
PERIOD = (6.28125, float(np.float32(2 * np.pi - 6.28125)) - float(np.float32(2 * np.pi - 6.28125)) % 2.0 ** -20,)
PERIOD += (float(np.float32(2 * np.pi - PERIOD[0] - PERIOD[1])),)
PI_IN = float(np.nextafter(np.float32(np.pi), np.float32(0)))
ALPHA = (2 * DEPTH) ** 0.25


def tiles(w, cols=None):
    w = w if cols is None else w[:, cols]
    return w.reshape(-1, P, w.shape[1]).transpose(1, 0, 2)


def stream(i):
    out = np.zeros((2 * DEPTH * SLOTS, P, SLOT), np.float32)
    at = [0]

    def put(*parts):
        c = 0
        for v in parts:
            n = v[0].size
            out[at[0], :, c:c + n].reshape(v.shape, copy=False)[...] = v
            c += n
        at[0] += 1

    def by_columns(w, width=256):
        t = tiles(w)
        for c in range(0, w.shape[1], width):
            put(t[:, :, c:c + width])

    def by_rows(w, n):
        t = tiles(w)
        for k in range(0, t.shape[1], n):
            put(t[:, k:k + n])

    def ffn(w1, w2):
        t1, t2 = tiles(w1), tiles(w2)
        for j in range(0, FT, 2):
            put(t1[:, :, j * P:(j + 2) * P])
            put(t1[:, :, F + j * P:F + (j + 2) * P])
            put(t2[:, j:j + 2])

    for l in range(DEPTH):
        ffn(i["w_ffn1_in"][l], i["w_ffn1_out"][l])
        w = i["w_in"][l]
        cuts = np.cumsum([0, 384, 256, 32, 512, 512, 512, 512, 512, 3072])
        lat, kr, hq, hf, hi, hg, mq, gate = (w[:, p:q] for p, q in zip(
            [0, *cuts[2:9]], [cuts[2], *cuts[3:]]))
        t = tiles(lat)
        for k in (0, 3, 6):
            put(t[:, k:k + 3])
        swap = np.concatenate([kr[:, 16:], kr[:, :16]], 1)
        zeros = np.zeros((D, 64), np.float32)
        put(tiles(np.concatenate([zeros, kr, kr], 1)), tiles(np.concatenate([zeros, swap, swap], 1)))
        by_columns(mq)
        by_columns(hq)
        by_columns(hf)
        by_rows(hi, 4)
        by_rows(hg, 4)
        by_columns(gate)
        q = i["w_uq"][l].reshape(384, 8, 96)
        q = np.concatenate([q, q[:, :, 80:96], q[:, :, 64:80]], 2).reshape(384, 1024)
        by_columns(q, 512)
        put(tiles(i["w_uk"][l]), tiles(i["w_uv"][l]))
        kv = i["w_mem_kv"][l]
        by_columns(kv[:, :512])
        by_rows(kv[:, 512:], 4)
        for n in ("w_o_mla", "w_o_hg", "w_o_mem"):
            by_columns(i[n][l], 512)
        by_rows(i["w_out"][l], 2)
        ffn(i["w_ffn2_in"][l], i["w_ffn2_out"][l])
        assert at[0] == (l + 1) * SLOTS
    for l in range(DEPTH):
        ffn(i["ffn1_w1_2"][l], i["ffn1_w2_2"][l])
        w = i["w_in_2"][l]
        cuts = np.cumsum([0, 512] + [128] * 6 + [24, 512, 128, 128, 512, 512, 512, 8])
        (qa, kc, vc, ks, vs, kw, vw, ga, qb, kb, vb, qc, kx, vx, f) = (w[:, p:q] for p, q in zip(cuts, cuts[1:]))
        twice = lambda v: np.concatenate([v[:, :64], v[:, :64], v[:, 64:], v[:, 64:]], 1)
        by_columns(qa)
        for v in (ks, kw, kc, vc):
            by_columns(twice(v))
        by_columns(qb)
        by_columns(twice(kb))
        by_rows(np.concatenate([vs, vw, vb, ga, f], 1), 4)
        by_columns(qc)
        by_columns(kx)
        by_rows(vx, 4)
        for n in ("cmp_k_w1_2", "cmp_v_w1_2"):
            by_columns(i[n][l], 128)
        by_columns(i["w_gate_2"][l])
        for n in ("w_br_a_2", "w_br_b_2", "w_br_c_2"):
            by_columns(i[n][l], 512)
        by_rows(i["w_out_2"][l], 2)
        ffn(i["ffn2_w1_2"][l], i["ffn2_w2_2"][l])
        assert at[0] == (l + 1 + DEPTH) * SLOTS
    return out


def params(i):
    out = np.zeros((2 * DEPTH, P, NP_COLS), np.float32)
    col = lambda v: v.reshape(-1, P).T
    for l in range(DEPTH):
        o = out[l]
        o[:, 0:8], o[:, 8:16], o[:, 16:24] = col(i["ffn1_norm"][l]), col(i["mix_norm"][l]), col(i["ffn2_norm"][l])
        o[:, 24:32], o[:, 32:35], o[:, 35:37] = col(i["mem_norm"][l]), col(i["q_lat_norm"][l]), col(i["kv_lat_norm"][l])
        o[:, 37:38], o[:, 38:42], o[:, 42:46] = (col(i["hg_out_norm"][l]), col(i["hg_lower_bounds"][0]),
                                                 col(i["hg_lower_bounds"][1]))
        o[:, 46] = float(l > 0)
        o = out[DEPTH + l]
        o[:, 0:24] = col(i["b_gate_2"][l])
        o[:, 24:40], o[:, 40:56] = col(i["cmp_pe_k_2"][l]), col(i["cmp_pe_v_2"][l])
        w = i["cmp_k_w2_2"][l]
        o[:, 56:312] = tiles(np.concatenate([w, w], 1)).reshape(P, 256)
        o[:, 312:440] = tiles(i["cmp_v_w2_2"][l]).reshape(P, 128)
        o[0:8, 440] = i["fox_b_f_2"][l]
        o[:, 441:449] = i["swa_sinks_2"][l][None, :]
    return out


def constants():
    c = np.zeros((P, NC_COLS), np.float32)
    q, j = np.arange(P)[:, None], np.arange(S)[None, :]
    c[:, 0:128] = np.eye(P)
    c[:, 128:384] = np.where(P + q - j >= 0, 0.0, NEG)
    c[:, 384:640] = 1.0
    freq = np.float32(10000.0) ** (-np.arange(0, 32, 2, dtype=np.float32) / np.float32(32))
    c[:, 640] = np.tile(freq, 8)
    c[:, 641] = np.tile(np.repeat([-1.0, 1.0], 16), 4)
    c[:, 642:650] = -0.5
    c[:, 712:840] = np.eye(P)[::-1]
    for qt in range(TT):
        c[:, 680 + 15 * qt:695 + 15 * qt] = np.where(qt * P + q >= 16 * np.arange(15)[None] + 31, 0.0, NEG)
    s, t = np.arange(P)[:, None], np.arange(P)[None, :]
    masks = np.stack([(s // (2 << i) == t // (2 << i)) & (s % (2 << i) < 1 << i) & (t % (2 << i) >= 1 << i)
                      for i in range(7)], 1).astype(np.int32).reshape(P, 7 * P)

    def bucket(dist):
        n = np.maximum(dist, 0)
        ratio = (np.log(np.maximum(n, 1).astype(np.float32) / np.float32(16)) / np.float32(np.log(128 / 16)))
        large = 16 + (ratio.astype(np.float32) * 16).astype(np.int32)
        return np.where(n < 16, n, np.minimum(large, 31))

    forward = np.arange(512) - 256
    hot = lambda d: (bucket(d)[None, :] == np.arange(32)[:, None]).astype(np.float32)
    onehots = np.concatenate([hot(forward), hot(-forward)], 1)
    d = -forward
    relmask = np.zeros((16, 512), np.float32)
    relmask[:, d < 0] = NEG
    relmask[8:, d >= 128] = NEG
    return {"consts": c, "masks": masks, "onehots": onehots, "relmask": relmask}


def kernel(**inputs):
    from concourse import bacc
    from concourse.bass_utils import run_bass_kernel_spmd

    i = {k: np.asarray(v) for k, v in inputs.items()}
    arrays = {
        "x": i["x"].reshape(S, D), "mem": i["mem"].reshape(S, D), "pos": i["positions"].reshape(1, S),
        "weights": stream(i), "params": params(i),
        "rows": np.concatenate([np.stack([i["final_norm"], i["final_norm"]])[None]] + [
            np.stack([i[f"ln{n}_{p}_2"][l] for p in "gb"])[None] for l in range(DEPTH) for n in (1, 2, 3)]),
        "relb": i["rel_bias_2"], **constants(),
    }
    new = lambda: bacc.Bacc("TRN2", target_bir_lowering=False, num_devices=1)
    nc = new()
    build(nc, declare(nc), new)
    r = run_bass_kernel_spmd(nc, [{"in_" + n: np.ascontiguousarray(v) for n, v in arrays.items()}], core_ids=[0])
    return r.results[0]["out_x"].reshape(1, S, D)
```

```python
from contextlib import ExitStack, contextmanager

import numpy as np

import concourse.bass as bass
from concourse import mybir

F32 = mybir.dt.float32
F32R = mybir.dt.float32r
I32 = mybir.dt.int32
ALU = mybir.AluOpType
ACT = mybir.ActivationFunctionType
AX = mybir.AxisListType.X
ALL = slice(None)

P = 128
S = 256
TT = S // P
D = 1024
KD = D // P
DEPTH = 2
F = 2816
FT = F // P
NEG = -1.0e30
LOW = -1.0e29

PIECE = 1024
R = 4
PIECES = 220
PASSES = PIECES // R
FFN_PIECES = 3 * FT
_FFN = [PIECE] * FFN_PIECES
WIDTHS = [_FFN + [0] * 8 + [640] * 8 + [PIECE] * 26 + [0] * 6 + [PIECE] * 20 + [0] * 12 + [PIECE] * 8 + _FFN,
          _FFN + [PIECE] * 18 + [832] * 4 + [PIECE] * 12 + [0, PIECE] * 8 + [PIECE] * 16 + [0] * 14 + [PIECE] * 8 + _FFN]
AFTER_MIX = PIECES - FFN_PIECES
FILL1 = {("level", i): [4 + i] for i in range(8)} | {
    ("ho", 0): [12, 13], ("mla", "start"): [14, 15, 16, 17], ("mla", 0): [18], ("mla", 1): [19], ("mla", 2): [20],
    ("mla", 3): [21], ("mem", 0): [22], ("mem", 1): [23]}
FILL2 = {("sc", 0): [8, 9]} | {(("slc", "win", "swa", "fox")[n // 4], n % 4): [10 + n] for n in range(14)}
assert sum(FILL1.values(), []) == list(range(4, 24)) and sum(FILL2.values(), []) == list(range(8, 24))
assert PIECES % R == 0 and all(len(w) == PIECES for w in WIDTHS)

NC_COLS = 128 + 256 + 256 + 40 + 32 + 128
NP_COLS = 512


class Signal:

    def __init__(self, name, sem, book, places):
        self.name, self.sem, self.book, self.places = name, sem, book, places
        self.count = [0] * len(ITERATIONS)
        self.labels = {}

    def up(self, label=None, by=1):
        r = self.places["made in"]
        self.count[r] += by
        if label is not None:
            assert (r, label) not in self.labels, (self.name, label)
            self.labels[r, label] = self.count[r]
        return self.sem, by

    def value(self, v):
        old = self.book.get(self.name)
        r, it = self.places["made in"], self.places["iteration"]
        if old is None:
            return self.sem, 1
        count = old[0]
        base = sum(n * c for n, c in zip(ITERATIONS[:r], count[:r])) + v
        if isinstance(it, int) or not count[r]:
            return self.sem, base
        return self.sem, it * count[r] + base

    def after(self, label):
        old = self.book.get(self.name)
        if old is None:
            return self.sem, 1
        return self.value(old[1][self.places["made in"], label])

    def value_at_end(self):
        old = self.book.get(self.name)
        return (self.sem, 1) if old is None else (self.sem, sum(n * c for n, c in zip(ITERATIONS, old[0])))

    def after_in(self, region, label):
        old = self.book.get(self.name)
        if old is None:
            return self.sem, 1
        assert ITERATIONS[region] == 1
        return self.sem, sum(n * c for n, c in zip(ITERATIONS[:region], old[0][:region])) + old[1][region, label]


PREP, BLOCK1, BETWEEN, BLOCK2, END = range(5)
ITERATIONS = [1, DEPTH, 1, DEPTH, 1]


class Signals(dict):
    def __init__(self, nc, ctx, book, places):
        super().__init__()
        self.nc, self.ctx, self.book, self.places = nc, ctx, book, places

    def __missing__(self, name):
        sem = self.ctx.enter_context(self.nc.semaphore("s_" + name.replace(" ", "_")))
        self[name] = Signal(name, sem, self.book, self.places)
        return self[name]

    def counts(self):
        return {n: (s.count, s.labels) for n, s in self.items()}


def build(nc, a, new):
    dry = new()
    emit(nc, a, emit(dry, declare(dry), {}))


INPUTS = {
    "x": ((S, D), F32), "mem": ((S, D), F32), "pos": ((1, S), I32),
    "weights": ((2 * DEPTH * PIECES + R, P, PIECE), F32), "params": ((2 * DEPTH, P, NP_COLS), F32),
    "rows": ((1 + 6 * DEPTH, 2, D), F32), "consts": ((P, NC_COLS), F32), "masks": ((P, 7 * P), I32),
    "onehots": ((32, 2 * 512), F32), "relb": ((32, 16), F32), "relmask": ((16, 512), F32),
}


def declare(nc):
    a = {n: nc.dram_tensor("in_" + n, s, t, kind="ExternalInput").ap() for n, (s, t) in INPUTS.items()}
    a["out"] = nc.dram_tensor("out_x", (S, D), F32, kind="ExternalOutput").ap()
    return a


def emit(nc, a, book):
    places = {"made in": PREP, "iteration": 0}
    nc.disable_value_cache = True
    rel_dram = nc.dram_tensor("rel_by_distance", (16, 512), F32).ap()
    mem_dram = nc.dram_tensor("memory_transposed", (P, KD * S), F32).ap()
    with ExitStack() as ctx:
        sig = Signals(nc, ctx, book, places)

        def sb(name, shape, dt=F32):
            return ctx.enter_context(nc.sbuf_tensor(name, shape, dt))

        psA = ctx.enter_context(nc.psum_tensor("psA", [P, 2, 512], F32))
        psY = ctx.enter_context(nc.psum_tensor("psY", [P, 4, 512], F32))
        psT = ctx.enter_context(nc.psum_tensor("psT", [P, 2, 512], F32))
        BANK = {f"A{i}": psA[:, i, :] for i in range(2)}
        BANK |= {f"Y{i}": psY[:, i, :] for i in range(4)}
        BANK |= {f"T{i}": psT[:, i, :] for i in range(2)}
        bank_of = {}

        ring = sb("ring", [P, R, PIECE])
        upper = sb("upper", [P, R, PIECE], F32R)
        rest = sb("rest", [P, R, PIECE], F32R)
        x = sb("x", [P, TT, D])
        xn = sb("xn", [P, TT, D])
        xT = (sb("xT_upper", [P, KD, S], F32R), sb("xT_rest", [P, KD, S], F32R))
        G = sb("G", [P, 24, S])
        Sc = sb("Sc", [P, 2, 4, S])
        PT = sb("PT", [P, 2, 2, 4, P])
        O = sb("O", [P, TT, 512])
        OT = sb("OT", [P, 3, 4, S])
        par = sb("par", [P, NP_COLS])
        sil = sb("sil", [P, 2, S])
        hT = (sb("hT_upper", [P, 2, S], F32R), sb("hT_rest", [P, 2, S], F32R))
        cst = sb("cst", [P, NC_COLS])
        st = sb("st", [P, 148])
        ident, CM, ones = cst[:, 0:128], cst[:, 128:384], cst[:, 384:640]
        invf, sgn, half = cst[:, 640:641], cst[:, 641:642], cst[:, 642:650]
        cmask, flip = cst[:, 680:710], cst[:, 712:840]
        lnr = G[:, 0:8, :].rearrange("p a b -> p (a b)").rearrange("p (a b) -> p a b", a=2)
        memraw = lnr
        xf = xn[:, :, :].rearrange("p a b -> p (a b)")
        memTg = OT[:, 0:2, :, :].rearrange("p a b c -> p (a b) c")
        cn = xf[:, 0:1280].rearrange("p (t n) -> p t n", t=2)
        ARENA = 15132
        arena = sb("arena", [P, ARENA])
        used = [0]

        def take(*shape):
            n = int(np.prod(shape))
            v = arena[:, used[0]:used[0] + n]
            used[0] += n
            assert used[0] <= ARENA, used[0]
            if len(shape) == 2:
                v = v.rearrange("p (a b) -> p a b", a=shape[0])
            if len(shape) == 3:
                v = v.rearrange("p (a b c) -> p a b c", a=shape[0], b=shape[1])
            return v

        KT = take(8, S)
        QT = take(8, S)
        QM = take(4, S)
        KM = take(4, S)
        QH, KH, GC = (OT[:, i, :, :] for i in range(3))
        Am = take(2, 4, P)
        Aoff = take(4, P)
        VM = take(TT, 512)
        VH = take(TT, 512)
        VX = take(TT, 512)
        GH = take(TT, 512)
        cT = take(5, S)
        MASK = take(7, P).bitcast(I32)
        CS = take(S)
        CK = take(2, S)
        lbt = take(64)
        posi = KT[:, 5, :].bitcast(I32)
        flatten = lambda t: t.rearrange("p a b -> p (a b)")
        mergedA = QT
        memT = QT
        EB = [Sc[:, i, :, :] for i in range(2)]
        TL = [PT[:, i, :, :, :].rearrange("p a b c -> p (a b c)").rearrange("p (h t) -> p h t", h=4)
              for i in range(2)]
        used[0] = 0
        BIAS = take(16, S)
        mergedB = take(KD, S)
        QA, QB = mergedB[:, 0:4, :], mergedB[:, 4:8, :]
        QF = take(4, S)
        KS = take(2, 2, S)
        KW = take(2, 2, S)
        KB = take(2, 2, S)
        KF = take(4, 2, S)
        KC = take(2, 30)
        VC = take(2, 64)
        VT = take(TT, 416)
        VF = take(TT, 512)
        CB = take(TT, 8, 15)
        CF = take(2, S)
        gg = take(TT, 24)

        scf = Sc[:, :, :, :].rearrange("p a b c -> p (a b c)")
        Z2 = scf[:, 0:512].rearrange("p (a b) -> p a b", a=2)
        ZB = scf[:, 512:992].rearrange("p (a b) -> p a b", a=16)
        HC = scf[:, 992:1052].rearrange("p (a b) -> p a b", a=2)
        FS = scf[:, 1052:1820].rearrange("p (a b) -> p a b", a=3)
        onehot_f, onehot_r, relb = scf[0:32, 0:512], scf[0:32, 512:1024], scf[0:32, 1024:1040]
        relmask = scf[0:16, 1040:1552]
        relsum = O[0:16, 0, :]
        BR = G[:, 8:24, :]
        BRANCH = {BLOCK1: ["mla", "hg", "mem"], BLOCK2: ["nsa", "swa", "fox"]}

        def spread(ap, shape):
            return ap.broadcast_to(shape)

        def fill(eng, bank, label):
            bank_of[places["made in"], label] = bank
            sem, v = sig[bank + " read"].value(sig[bank + " full"].count[places["made in"]])
            if not (isinstance(v, int) and v <= 0):
                eng.wait_ge(sem, v)
            return BANK[bank]

        def full(label):
            return sig[bank_of[places["made in"], label] + " full"].after(label)

        def filled(label):
            return sig[bank_of[places["made in"], label] + " full"].up(label)

        def at(label):
            return BANK[bank_of[places["made in"], label]]

        def read(label):
            return sig[bank_of[places["made in"], label] + " read"].up(label)

        def taken(label):
            bank, old = bank_of[places["made in"], label], book.get(bank_of[places["made in"], label] + " full")
            return sig[bank + " read"].value(old[1][places["made in"], label] if old else 1)

        @contextmanager
        def region(eng, r):
            places["made in"] = r
            if ITERATIONS[r] == 1:
                places["iteration"] = 0
                yield 0
            else:
                with eng.Fori(0, ITERATIONS[r]) as it:
                    places["iteration"] = it
                    yield it
            places["iteration"] = 0

        def number():
            return places["iteration"] + (DEPTH if places["made in"] == BLOCK2 else 0)

        def loaded(h):
            r = h % R
            return sig[f"place {r} loaded"].sem, number() * (16 * PASSES) + 16 * (h // R + 1)

        def emptied(h):
            r = h % R
            return sig[f"place {r} emptied"].sem, number() * PASSES + (h // R + 1)

        def gates(place):
            return (FILL1 if places["made in"] == BLOCK1 else FILL2).get(place, [])

        def gate_piece(n):
            if places["made in"] == BLOCK2:
                return 101 + 2 * n if n < 8 else 116 + n - 8
            return 104 + n if n < 4 else 114 + n - 4

        def width(h):
            return PIECE if h >= PIECES else WIDTHS[places["made in"] == BLOCK2][h]

        def parts_free(h):
            if h < R:
                return None
            if h == PIECES + R - 1:
                return full(("y", 1, 3))
            return sig["parts used"].after(max(i for i in range(h - R + 1) if width(i)))

        def ahead(eng, state, h, split):
            while state["split"] < h + R:
                if width(state["split"]):
                    split(state["split"])
                state["split"] += 1

        block = ctx.enter_context(nc.Block())

        @block.tensor
        def _(pe):
            state = {"piece": 0, "free": [], "A": 0}

            def mm(out, lhsT, rhs, start, stop, up=None):
                i = pe.matmul(out, lhsT, rhs, start=start, stop=stop)
                if up is not None:
                    i.then_inc(*up)
                elif state["free"]:
                    h = state["free"].pop(0)
                    i.then_inc(*(sig["parts used"].up(h) if width(h) else (sig[f"place {h % R} emptied"].sem, 1)))

            def product(out, lhsT, rhs, start, stop, up=None):
                which = [(0, 0)] if len(lhsT) == 1 else [(0, 0), (0, 1), (1, 0)]
                for n, (a_, b_) in enumerate(which):
                    last = n == len(which) - 1
                    mm(out, lhsT[a_], rhs[b_], start and n == 0, stop and last, up if last else None)

            def piece():
                h = state["piece"]
                state["piece"] += 1
                if width(h):
                    pe.wait_ge(*emptied(h))
                    return upper[:, h % R, :], rest[:, h % R, :]
                pe.wait_ge(*loaded(h))
                return (ring[:, h % R, :],)

            def free():
                state["free"].append(state["piece"] - 1)

            def cut(parts, *index):
                return tuple(p[index] for p in parts)

            def shaped(parts, n, pattern, **kw):
                return tuple(p[:, 0:n].rearrange(pattern, **kw) for p in parts)

            def leave_last():
                assert state["free"] == [PIECES - 1] and state["piece"] == PIECES
                state["free"] = []

            def next_a():
                state["A"] ^= 1
                return f"A{state['A'] ^ 1}"

            def turn(bank, label, tiles, src_ready=None):
                if src_ready is not None:
                    pe.wait_ge(*src_ready)
                out = fill(pe, bank, label)
                at_col = 0
                for n, t in enumerate(tiles):
                    i = pe.transpose(out[0:t.shape[1], at_col:at_col + P], t, ident)
                    at_col += P
                i.then_inc(*filled(label))

            def turn_x(src, label, ready):
                for tt in range(TT):
                    pe.wait_ge(*ready(tt))
                    for h in range(2):
                        turn(f"T{h}", label + (tt, h),
                             [src[:, tt, (4 * h + q) * P:(4 * h + q + 1) * P] for q in range(4)])

            def wait_xT(label):
                for h in range(2):
                    pe.wait_ge(*taken(label + (1, h)))

            def features(label, n_tiles, rhs, kt, w, m=P, ready=None):
                if ready is not None:
                    pe.wait_ge(*ready)
                for n in range(0, n_tiles, 2):
                    lab = (label, n // 2)
                    out = fill(pe, next_a(), lab)
                    for j in range(2):
                        for k in range(kt):
                            mm(out[0:m, j * S:(j + 1) * S], w(n + j, k), rhs(k), k == 0, k == kt - 1,
                               filled(lab) if j == 1 and k == kt - 1 else None)

            def by_features(label, banks, rhs=None):
                rhs = xT if rhs is None else rhs
                for n in range(banks):
                    lab = (label, n)
                    out = fill(pe, next_a(), lab)
                    for j in range(2):
                        s = shaped(piece(), PIECE, "p (k c) -> p k c", k=KD)
                        for k in range(KD):
                            product(out[:, j * S:(j + 1) * S], cut(s, ALL, k), cut(rhs, ALL, k), k == 0, k == KD - 1,
                                    filled(lab) if j == 1 and k == KD - 1 else None)
                        free()

            def gate(pieces):
                for n in pieces:
                    lab, j = ("gate", n // 2), n % 2
                    if j == 0:
                        state["gate bank"] = fill(pe, f"Y{2 + n // 2 % 2}", lab)
                    assert state["piece"] == gate_piece(n)
                    s = shaped(piece(), PIECE, "p (k c) -> p k c", k=KD)
                    for k in range(KD):
                        product(state["gate bank"][:, j * S:(j + 1) * S], cut(s, ALL, k), cut(xT, ALL, k),
                                k == 0, k == KD - 1, filled(lab) if j == 1 and k == KD - 1 else None)
                    free()

            def by_tokens(label, width, lhs=None, also=None):
                lhs = xT if lhs is None else lhs
                banks = [next_a(), next_a()]
                outs = [fill(pe, banks[t], (label, t)) for t in range(TT)]
                for h in range(4):
                    s = shaped(piece(), 2 * width, "p (k c) -> p k c", k=2)
                    for q in range(2):
                        k = 2 * h + q
                        for t in range(TT):
                            product(outs[t][:, 0:width], cut(lhs, ALL, k, slice(t * P, (t + 1) * P)), cut(s, ALL, q),
                                    k == 0, k == KD - 1, filled((label, t)) if k == KD - 1 else None)
                        if also is not None:
                            also(k, cut(s, ALL, q))
                    free()

            def ffn(f, xlabel):
                if xlabel is None:
                    for h in range(2):
                        pe.wait_ge(*sig[f"T{h} read"].value(0))
                else:
                    wait_xT(xlabel)

                def up(j):
                    lab = ("ab", f, j)
                    out = fill(pe, f"A{j % 2}", lab)
                    for v in range(2):
                        s = shaped(piece(), PIECE, "p (k c) -> p k c", k=KD)
                        for k in range(KD):
                            product(out[:, v * S:(v + 1) * S], cut(s, ALL, k), cut(xT, ALL, k),
                                    k == 0, k == KD - 1, filled(lab) if v == 1 and k == KD - 1 else None)
                        free()

                ys = []

                def down(j):
                    s = piece()
                    pe.wait_ge(*sig["hidden"].after((f, j)))
                    if j == 0:
                        ys.extend(fill(pe, f"Y{b}", ("y", f, b)) for b in range(4))
                    for t in range(TT):
                        for n in range(2):
                            product(ys[2 * t + n], cut(hT, ALL, j % 2, slice(t * P, (t + 1) * P)),
                                    cut(s, ALL, slice(n * 512, (n + 1) * 512)),
                                    j == 0, j == FT - 1, filled(("y", f, 2 * t + n)) if j == FT - 1 else None)
                    free()

                for j in range(FT):
                    up(j)
                    if j:
                        down(j - 1)
                down(FT - 1)
                state["A"] = 0

            def attention(name, hbs, q, k, v, dv, causal, extra=None, between=None):
                todo = [(hb, qt) for hb in range(hbs) for qt in range(TT)]
                keys = lambda qt: TT if (qt or not causal) else 1

                def scores(hb, qt):
                    w = keys(qt) * P
                    for b in range(2):
                        lab = ("s", name, hb, qt, b)
                        out = fill(pe, f"A{b}", lab)
                        for j in range(2):
                            h = 4 * hb + 2 * b + j
                            o = out[:, j * S:j * S + w]
                            last = filled(lab) if j == 1 else None
                            mm(o, q(h, qt), k(h, w), True, extra is None, None if extra else last)
                            if extra:
                                c1, c2 = extra(h, qt, w)
                                mm(o, *c1, False, False)
                                mm(o, *c2, False, True, last)

                def rest(n):
                    hb, qt = todo[n]
                    for kt in range(keys(qt)):
                        turn(f"T{kt}", ("pt", name, hb, qt, kt),
                             [Sc[:, n % 2, j, kt * P:(kt + 1) * P] for j in range(4)],
                             sig["weights"].after((name, hb, qt)))
                    gate(gates((name, n)))
                    lab = ("o", name, hb, qt)
                    out = fill(pe, f"Y{n % 2}", lab)
                    for kt in range(keys(qt)):
                        pe.wait_ge(*taken(("pt", name, hb, qt, kt)))
                    for j in range(4):
                        for kt in range(keys(qt)):
                            mm(out[:, j * dv:(j + 1) * dv], PT[:, n % 2, kt, j, :], v(4 * hb + j, kt),
                               kt == 0, kt == keys(qt) - 1,
                               filled(lab) if j == 3 and kt == keys(qt) - 1 else None)

                scores(*todo[0])
                for n in range(len(todo)):
                    if n + 1 < len(todo):
                        scores(*todo[n + 1])
                    if n == 0:
                        gate(gates((name, "start")))
                        if between is not None:
                            between()
                    rest(n)

            def turn_o(name, ready):
                for qt in range(TT):
                    turn(f"T{qt}", ("ot", name, qt), [O[:, qt, j * P:(j + 1) * P] for j in range(4)], ready(qt))

            def merge():
                for br in range(3):
                    for t in range(TT):
                        pe.wait_ge(*taken(("ot", BRANCH[places["made in"]][br], t)))
                    for n in range(4):
                        s, = shaped(piece(), PIECE, "p (k c) -> p k c", k=4)
                        lab = ("wo", br, n)
                        out = fill(pe, next_a(), lab)
                        for j in range(2):
                            for k in range(4):
                                mm(out[:, j * S:(j + 1) * S], s[:, k, j * P:(j + 1) * P], OT[:, br, k, :],
                                   k == 0, k == 3, filled(lab) if j == 1 and k == 3 else None)
                        free()
                ys = [fill(pe, f"Y{b}", ("y", "mix", b)) for b in range(4)]
                for k in range(KD):
                    if k % 2 == 0:
                        pe.wait_ge(*sig["merged parts"].after(k // 2))
                    s = piece()
                    for b in range(4):
                        product(ys[b], cut(xT, ALL, k, slice((b // 2) * P, (b // 2 + 1) * P)),
                                cut(s, ALL, slice((b % 2) * 512, (b % 2 + 1) * 512)),
                                k == 0, k == KD - 1, filled(("y", "mix", b)) if k == KD - 1 else None)
                    free()

            with region(pe, PREP):
                pe.wait_ge(sig["consts"].sem, 16)
                turn_x(xn, ("mem",), lambda tt: sig["scaled"].after(("mem", tt)))

            with region(pe, BLOCK1):
                state["piece"] = 0
                assert not state["free"]
                turn_x(xn, ("norm", 0), lambda tt: sig["scaled"].after((0, tt)))
                ffn(0, ("norm", 0))
                pe.wait_ge(*sig["memory scaled"].after(0))
                by_features("mk", 2, rhs=(memTg,))
                by_tokens("mv", 512, lhs=(memTg,))
                turn_x(xn, ("norm", 1), lambda tt: sig["scaled"].after((1, tt)))
                wait_xT(("norm", 1))
                outs = [fill(pe, f"Y{b}", ("c", b)) for b in range(4)]
                for k in range(KD):
                    s = piece()
                    for t in range(TT):
                        lhsT = cut(xT, ALL, k, slice(t * P, (t + 1) * P))
                        product(outs[t][:, 0:384], lhsT, cut(s, ALL, slice(0, 384)), k == 0, k == KD - 1,
                                filled(("c", t)) if k == KD - 1 else None)
                        product(outs[2 + t][:, 0:256], lhsT, cut(s, ALL, slice(384, 640)), k == 0, k == KD - 1,
                                filled(("c", 2 + t)) if k == KD - 1 else None)
                    free()
                by_features("kr", 1)
                by_features("mq", 2)
                by_features("hq", 2)
                by_features("hf", 2)
                by_tokens("hi", 512)
                by_tokens("hgate", 512)
                for t in range(TT):
                    pe.wait_ge(*taken(("c", t)))
                    pe.wait_ge(*taken(("c", 2 + t)))
                    turn("T0", ("cT", t, 0), [cn[:, t, j * P:(j + 1) * P] for j in range(3)])
                    turn("T1", ("cT", t, 1), [cn[:, t, j * P:(j + 1) * P] for j in range(3, 5)])
                gate(range(4))
                for h in range(2):
                    pe.wait_ge(*taken(("cT", 1, h)))
                for n in range(4):
                    s, = shaped(piece(), 3 * 256, "p (k c) -> p k c", k=3)
                    features(("uq", n), 2, lambda k: cT[:, k, :], 3, lambda n, k: s[:, k, n * P:(n + 1) * P])
                    free()
                s, = shaped(piece(), PIECE, "p (k c) -> p k c", k=2)
                features("uk", 8, lambda k: cT[:, 3 + k, :], 2, lambda n, k: s[:, k, n * 64:(n + 1) * 64], m=64)
                free()
                s, = shaped(piece(), PIECE, "p (k c) -> p k c", k=2)
                for t in range(TT):
                    out = fill(pe, next_a(), ("uv", t))
                    for k in range(2):
                        mm(out, cT[:, 3 + k, t * P:(t + 1) * P], s[:, k, :], k == 0, k == 1,
                           filled(("uv", t)) if k == 1 else None)
                free()
                pe.wait_ge(*sig["recurrence keys"].after(0))
                for i in range(2):
                    pe.wait_ge(*taken(("hq", i)))
                for t in range(TT):
                    lab = ("diag", t)
                    out = fill(pe, next_a(), lab)
                    for h in range(4):
                        c = slice(t * P, (t + 1) * P)
                        mm(out[:, h * P:(h + 1) * P], KH[:, h, c], QH[:, h, c], True, True,
                           filled(lab) if h == 3 else None)
                for i in range(8):
                    gate(gates(("level", i)))
                    pe.wait_ge(*sig["decayed"].after(i))
                    tl = TL[i % 2]
                    if i < 7:
                        for t in range(TT):
                            lab = ("level", i, t)
                            out = fill(pe, next_a(), lab)
                            for h in range(4):
                                c = tl[:, h, t * P:(t + 1) * P]
                                mm(out[:, h * P:(h + 1) * P], c, c, True, True, filled(lab) if h == 3 else None)
                    else:
                        lab = ("level", i, 0)
                        out = fill(pe, next_a(), lab)
                        for h in range(4):
                            mm(out[:, h * P:(h + 1) * P], tl[:, h, 0:P], tl[:, h, P:S], True, True,
                               filled(lab) if h == 3 else None)
                if state["A"]:
                    state["A"] = 0
                gate(gates(("ho", 0)))
                pe.wait_ge(*taken(("level", 7, 0)))
                for t in range(TT):
                    pe.wait_ge(*taken(("hi", t)))
                for t in range(TT):
                    lab = ("ho", t)
                    out = fill(pe, f"Y{2 + t}", lab)
                    for h in range(4):
                        o = out[:, h * P:(h + 1) * P]
                        v = lambda s: VH[:, s, h * P:(h + 1) * P]
                        last = filled(lab) if h == 3 else None
                        if t == 0:
                            mm(o, Am[:, 0, h, :], v(0), True, True, last)
                        else:
                            mm(o, Aoff[:, h, :], v(0), True, False)
                            mm(o, Am[:, 1, h, :], v(1), False, True, last)
                for n in range(4):
                    pe.wait_ge(*taken((("uq", n), 0)))
                for n in range(4):
                    pe.wait_ge(*taken(("uk", n)))
                for t in range(TT):
                    pe.wait_ge(*taken(("uv", t)))
                pe.wait_ge(*sig["rotary keys"].after(0))
                attention("mla", 2, lambda h, qt: QT[:, h, qt * P:(qt + 1) * P], lambda h, w: KT[:, h, 0:w],
                          lambda h, kt: VM[:, kt, h * 64:(h + 1) * 64], 64, True)

                def turn_both():
                    turn_o("mla", lambda qt: taken(("o", "mla", 1, qt)))
                    for t in range(TT):
                        turn(f"T{t}", ("ot", "hg", t), [GH[:, t, j * P:(j + 1) * P] for j in range(4)],
                             sig["recurrence out"].after(t))

                for n in range(2):
                    pe.wait_ge(*taken(("mq", n)))
                    pe.wait_ge(*taken(("mk", n)))
                    pe.wait_ge(*taken(("mv", n)))
                attention("mem", 1, lambda h, qt: QM[:, h, qt * P:(qt + 1) * P], lambda h, w: KM[:, h, 0:w],
                          lambda h, kt: VX[:, kt, h * P:(h + 1) * P], P, False, between=turn_both)
                turn_o("mem", lambda qt: taken(("o", "mem", 0, qt)))
                merge()
                turn_x(xn, ("norm", 2), lambda tt: sig["scaled"].after((2, tt)))
                ffn(1, ("norm", 2))
                leave_last()

            with region(pe, BETWEEN):
                pe.wait_ge(*sig["rel tables"].value(16 * 3))
                mm(fill(pe, "A0", "rel")[0:16, :], relb, onehot_r, True, True, filled("rel"))
                out = fill(pe, "A1", "rel cmp")
                for qt in range(TT):
                    for c in range(15):
                        i = 256 + qt * P - 31 - 16 * c
                        n = (qt * 15 + c) * 8
                        mm(out[:, n:n + 8], onehot_f[:, i:i + P], relb[:, 0:8], True, True,
                           filled("rel cmp") if (qt, c) == (1, 14) else None)
                turn_x(x, ("norm", "final"), lambda tt: sig["x normed"].after(("final", tt)))
                pe.wait_ge(*sig["bias"].value(16))
                for n in range(8):
                    mm(fill(pe, f"A{n % 2}", ("flip", n)), flip, BR[:, 2 * n:2 * n + 2, :], True, True, filled(("flip", n)))

            with region(pe, BLOCK2):
                state["piece"] = 0
                assert not state["free"]
                ffn(0, None)
                turn_x(x, ("norm", 0), lambda tt: sig["x normed"].after((0, tt)))
                wait_xT(("norm", 0))
                by_features("qa", 2)
                for n in ("ks", "kw", "kc", "vc"):
                    by_features(n, 1)
                by_features("qb", 2)
                by_features("kb", 1)
                fout = fill(pe, "Y0", "f")
                by_tokens("vt", 416, also=lambda k, s: product(
                    fout[0:8, 0:S], cut(s, ALL, slice(408, 416)), cut(xT, ALL, k), k == 0, k == KD - 1,
                    filled("f") if k == KD - 1 else None))
                by_features("qf", 2)
                by_features("kf", 2)
                by_tokens("vf", 512)
                for z in ("k", "v"):
                    pe.wait_ge(*sig["blocks"].after(z))
                    for m in range(2):
                        out = fill(pe, next_a(), ("cmp", z, m))
                        for q in range(2):
                            s, = shaped(piece(), PIECE, "p (l c) -> p l c", l=8)
                            for lp in range(8):
                                mm(out[:, 0:30], s[:, lp, :], ZB[:, 8 * q + lp, :], q == 0 and lp == 0, q == 1 and lp == 7,
                                   filled(("cmp", z, m)) if q == 1 and lp == 7 else None)
                            free()
                            gate([4 * (z == "v") + 2 * m + q])
                    for m in range(2):
                        pe.wait_ge(*taken(("cmp", z, m)))
                    out = fill(pe, "Y1", ("cmp out", z))
                    if z == "k":
                        for m in range(2):
                            mm(out[:, 0:30], par[:, 56 + m * P:56 + (m + 1) * P], HC[:, m, :], m == 0, m == 1,
                               filled(("cmp out", z)) if m == 1 else None)
                    else:
                        for g in range(2):
                            for m in range(2):
                                mm(out[0:15, g * 64:(g + 1) * 64], HC[:, m, g * 15:(g + 1) * 15],
                                   par[:, 312 + m * 64:312 + (m + 1) * 64], m == 0, m == 1,
                                   filled(("cmp out", z)) if g == 1 and m == 1 else None)
                state["A"] = 0
                for n in (("qa", 0), ("qa", 1), ("cmp out", "k"), ("cmp out", "v")):
                    pe.wait_ge(*taken(n))
                for qt in range(TT):
                    lab = ("sc", qt)
                    out = fill(pe, f"A{qt}", lab)
                    for h in range(8):
                        g = h // 4
                        mm(out[:, h * 15:(h + 1) * 15], QA[:, h // 2, qt * P:(qt + 1) * P],
                           KC[:, h % 2, g * 15:(g + 1) * 15], True, True, filled(lab) if h == 7 else None)
                gate(gates(("sc", 0)))
                for qt in range(TT):
                    pe.wait_ge(*sig["weights"].after(("cmp", qt)))
                    sc = scf[:, qt * 1024:qt * 1024 + 120]
                    for b in range(2):
                        turn(f"T{b}", ("ptc", qt, b), [sc[:, (4 * b + j) * 15:(4 * b + j + 1) * 15] for j in range(4)])
                    for b in range(2):
                        pe.wait_ge(*taken(("ptc", qt, b)))
                    lab = ("o", "cmp", 0, qt)
                    out = fill(pe, f"Y{qt}", lab)
                    for h in range(8):
                        mm(out[:, h * 64:(h + 1) * 64], PT[0:15, qt, h // 4, h % 4, :], VC[0:15, h // 4, :], True, True,
                           filled(lab) if h == 7 else None)
                for n in (("ks", 0), ("kw", 0), ("kb", 0), ("vt", 0), ("vt", 1), ("vf", 0), ("vf", 1),
                          ("qb", 0), ("qb", 1), ("qf", 0), ("qf", 1), ("kf", 0), ("kf", 1)):
                    pe.wait_ge(*taken(n))
                qa = lambda h, qt: QA[:, h // 2, qt * P:(qt + 1) * P]
                attention("slc", 2, qa, lambda h, w: KS[:, h // 4, h % 2, 0:w],
                          lambda h, kt: VT[:, kt, (h // 4) * 64:(h // 4 + 1) * 64], 64, True)
                attention("win", 2, qa, lambda h, w: KW[:, h // 4, h % 2, 0:w],
                          lambda h, kt: VT[:, kt, 128 + (h // 4) * 64:128 + (h // 4 + 1) * 64], 64, True)
                attention("swa", 2, lambda h, qt: QB[:, h // 2, qt * P:(qt + 1) * P],
                          lambda h, w: KB[:, h // 4, h % 2, 0:w],
                          lambda h, kt: VT[:, kt, 256 + (h // 4) * 64:256 + (h // 4 + 1) * 64], 64, True,
                          between=lambda: turn_o("nsa", lambda qt: taken(("o", "win", 1, qt))))
                pe.wait_ge(*sig["decay sums"].after(0))
                attention("fox", 2, lambda h, qt: QF[:, h // 2, qt * P:(qt + 1) * P],
                          lambda h, w: KF[:, h // 2, h % 2, 0:w],
                          lambda h, kt: VF[:, kt, h * 64:(h + 1) * 64], 64, True,
                          extra=lambda h, qt, w: ((CF[:, 0, qt * P:(qt + 1) * P], ident[:, h:h + 1].broadcast_to([P, w])),
                                                  (ident[:, h:h + 1].broadcast_to([P, P]), CF[:, 1, 0:w])),
                          between=lambda: turn_o("swa", lambda qt: taken(("o", "swa", 1, qt))))
                for _ in range(2):
                    piece()
                    free()
                turn_o("fox", lambda qt: taken(("o", "fox", 1, qt)))
                merge()
                turn_x(x, ("norm", 1), lambda tt: sig["x normed"].after((1, tt)))
                ffn(1, ("norm", 1))
                leave_last()
                turn_x(x, ("norm", 2), lambda tt: sig["x normed"].after((2, tt)))

        @block.sync
        def _(sp):
            sp.dma_start(memraw, a["mem"].rearrange("(t p) d -> p t d", p=P)).then_inc(sig["mem loaded"].sem, 16)
            sp.dma_start(cst[:, :], a["consts"]).then_inc(sig["consts"].sem, 16)
            sp.dma_start(x[:, :, :], a["x"].rearrange("(t p) d -> p t d", p=P)).then_inc(sig["x loaded"].sem, 16)

            def load(r, n):
                sp.dma_start(ring[:, r, :], a["weights"][bass.ds(n, 1), :, :].rearrange("a p n -> (a p) n"))\
                  .then_inc(sig[f"place {r} loaded"].sem, 16)

            for r in range(R):
                load(r, r)
            with sp.Fori(1, 2 * DEPTH * PASSES + 1) as go:
                for r in range(R):
                    sp.wait_ge(sig[f"place {r} emptied"].sem, go)
                    load(r, go * R + r)
            sp.wait_ge(*sig["x normed"].value_at_end())
            sp.dma_start(a["out"].rearrange("(t p) d -> p t d", p=P), x[:, :, :]).then_inc(sig["out stored"].sem, 16)
            sp.wait_ge(sig["out stored"].sem, 16)

        @block.gpsimd
        def _(pool):
            def power(label, n):
                pool.wait_ge(*sig["variance"].after(label))
                pool.tensor_tensor(st[:, 8:8 + n], st[:, 0:n], half[:, 0:n], ALU.pow).then_inc(*sig["rstd"].up(label))

            def norm_power(i):
                for tt in range(TT):
                    pool.wait_ge(*sig["variance"].after((i, tt)))
                    pool.tensor_tensor(st[:, 8 + tt:9 + tt], st[:, tt:tt + 1], half[:, 0:1], ALU.pow)\
                        .then_inc(*sig["rstd"].up((i, tt)))

            def load_params(layer):
                pool.dma_start(par[:, :], a["params"][bass.ds(layer, 1), :, :].rearrange("a p n -> (a p) n"))\
                    .then_inc(*sig["params"].up(by=16))

            def load_rows(q):
                pool.dma_start(lnr, rows_of(q)).then_inc(*sig["rows"].up(by=16))

            def rows_of(q):
                v = a["rows"][bass.ds(q, 1), :, :]
                return bass.AP(v.tensor, v.offset, [[0, P], [D, 2], [1, D]])

            state = {"split": 0}

            def split(h):
                free_ = parts_free(h)
                if free_ is not None:
                    pool.wait_ge(*free_)
                pool.wait_ge(*sig["upper parts"].after(h))
                r, n = h % R, width(h)
                pool.tensor_tensor(rest[:, r, 0:n], ring[:, r, 0:n], upper[:, r, 0:n], ALU.subtract)\
                    .then_inc(sig[f"place {r} emptied"].sem, 1)

            def until(h):
                ahead(pool, state, h, split)

            with region(pool, PREP):
                p = a["pos"]
                pool.dma_start(posi, bass.AP(p.tensor, p.offset, [[0, P], [1, S]])).then_inc(sig["positions"].sem, 16)
                pool.dma_start(flatten(MASK), a["masks"]).then_inc(sig["masks"].sem, 16)
                pool.wait_ge(sig["consts"].sem, 16)
                norm_power("mem")
                pool.wait_ge(*sig["scaled"].after(("mem", 1)))
                load_rows(0)
                until(0)
                for h in range(2):
                    pool.wait_ge(*taken(("mem", 1, h)))
                pool.dma_start(mem_dram, flatten(memT)).then_inc(*sig["memory stored"].up(by=16))
            with region(pool, BLOCK1) as l:
                for h in range(2):
                    pool.wait_ge(*sig[f"T{h} read"].value(0))
                load_params(l)
                pool.wait_ge(sig["memory stored"].sem, 16)
                pool.dma_start(OT[:, 0:2, :, :].rearrange("p a b c -> p (a b c)"), mem_dram)\
                    .then_inc(*sig["memory back"].up(by=16))
                state["split"] = R
                norm_power(0)
                pool.wait_ge(*sig["scaled"].after((0, 1)))
                load_rows(l * 3 + 1)
                until(FFN_PIECES - 1)
                norm_power(1)
                until(FFN_PIECES + 15)
                power("latent", 4)
                until(gate_piece(FILL1["ho", 0][-1]))
                power("recurrence", 8)
                until(AFTER_MIX - 8)
                pool.wait_ge(*sig["merged"].after("all"))
                load_rows(l * 3 + 2)
                until(AFTER_MIX - 2)
                norm_power(2)
                pool.wait_ge(*sig["scaled"].after((2, 1)))
                load_rows(l * 3 + 3)
                until(PIECES)
            with region(pool, BETWEEN):
                for h in range(2):
                    pool.wait_ge(*sig[f"T{h} read"].value(0))
                pool.dma_start(scf[0:32, 0:1024], a["onehots"]).then_inc(*sig["rel tables"].up(by=16))
                pool.dma_start(relb, a["relb"]).then_inc(*sig["rel tables"].up(by=16))
                pool.dma_start(relmask, a["relmask"]).then_inc(*sig["rel tables"].up(by=16))
                for z in (KS, KW, KB, KF):
                    v = z.rearrange("p a b c -> p (a b c)")
                    pool.memset(v, 0.0).then_inc(*sig["cleared"].up())
                for z in (KC, CF):
                    pool.memset(z.rearrange("p a b -> p (a b)"), 0.0).then_inc(*sig["cleared"].up())
                norm_power("final")
                pool.wait_ge(*sig["rel summed"].after(0))
                pool.dma_start(rel_dram, relsum).then_inc(*sig["rel stored"].up(by=16))
                pool.wait_ge(*sig["rel stored"].value(16))
                pool.dma_start(BR, bass.AP(rel_dram.tensor, rel_dram.offset + 1, [[1, P], [512, 16], [1, S]]))\
                    .then_inc(*sig["bias"].up(by=16))
            with region(pool, BLOCK2) as l:
                for h in range(2):
                    pool.wait_ge(*sig[f"T{h} read"].value(0))
                load_params(l + DEPTH)
                load_rows((l + DEPTH) * 3 + 1)
                state["split"] = R
                until(FFN_PIECES - 1)
                norm_power(0)
                until(AFTER_MIX - 8)
                pool.wait_ge(*sig["merged"].after("all"))
                load_rows((l + DEPTH) * 3 + 2)
                until(AFTER_MIX - 2)
                norm_power(1)
                for h in range(2):
                    pool.wait_ge(*taken(("norm", 1, 1, h)))
                load_rows((l + DEPTH) * 3 + 3)
                until(PIECES)
                norm_power(2)

        @block.vector
        def _(dve):
            def link(i):
                i.then_inc(*sig["vector step"].up())
                dve.wait_ge(*sig["vector step"].value(sig["vector step"].count[places["made in"]]))

            def own():
                dve.wait_ge(*sig["vector step"].value(sig["vector step"].count[places["made in"]]))

            tt_, ts_, stt_ = dve.tensor_tensor, dve.tensor_scalar, dve.scalar_tensor_tensor

            def variance(label, parts):
                for n, (src, dst, count) in enumerate(parts):
                    i = ts_(dst, src, 1.0 / count, 1e-6 if places["made in"] != BLOCK2 else 1e-5, ALU.mult, ALU.add)
                i.then_inc(*sig["variance"].up(label))
                dve.wait_ge(*sig["rstd"].after(label))

            def norm_variance(i):
                for tt in range(TT):
                    dve.wait_ge(*sig["square sum"].after((i, tt)))
                    ts_(st[:, tt:tt + 1], st[:, 16 + tt:17 + tt], 1.0 / D, 1e-6 if places["made in"] != BLOCK2 else 1e-5,
                        ALU.mult, ALU.add).then_inc(*sig["variance"].up((i, tt)))

            def rests(label):
                for tt in range(TT):
                    for h in range(2):
                        lab = label + (tt, h)
                        dve.wait_ge(*sig["residual's upper parts"].after(lab))
                        v = (ALL, slice(4 * h, 4 * h + 4), slice(tt * P, (tt + 1) * P))
                        tt_(xT[1][v], at(lab).rearrange("p (q c) -> p q c", q=4), xT[0][v], ALU.subtract)\
                            .then_inc(*read(lab))

            def rms(i):
                norm_variance(i)
                dve.wait_ge(*sig["rows"].value(16 * i))
                for tt in range(TT):
                    dve.wait_ge(*sig["rstd"].after((i, tt)))
                    stt_(xn[:, tt, :], x[:, tt, :], st[:, 8 + tt:9 + tt], lnr[:, 0, :], ALU.mult, ALU.mult)\
                        .then_inc(*sig["scaled"].up((i, tt)))
                rests(("norm", i))

            def add_sums(f):
                for b in range(4):
                    lab = ("y", f, b)
                    dve.wait_ge(*full(lab))
                    v = x[:, b // 2, (b % 2) * 512:(b % 2 + 1) * 512]
                    stt_(v, at(lab), 0.5, v, ALU.mult, ALU.add).then_inc(*read(lab))

            def layer_norm(i, f):
                for tt in range(TT):
                    for b in (2 * tt, 2 * tt + 1):
                        lab = ("y", f, b)
                        dve.wait_ge(*full(lab))
                        v = x[:, tt, (b % 2) * 512:(b % 2 + 1) * 512]
                        stt_(v, at(lab), 0.5, v, ALU.mult, ALU.add, accum_out=st[:, 20 + b:21 + b]).then_inc(*read(lab))
                    for b in (2 * tt, 2 * tt + 1):
                        dve.wait_ge(*taken(("y", f, b)))
                    link(tt_(st[:, 24 + tt:25 + tt], st[:, 20 + 2 * tt:21 + 2 * tt], st[:, 21 + 2 * tt:22 + 2 * tt], ALU.add))
                    ts_(st[:, 26 + tt:27 + tt], st[:, 24 + tt:25 + tt], -1.0 / D, None, ALU.mult)\
                        .then_inc(*sig["mean"].up((i, tt)))
                dve.wait_ge(*sig["rows"].value(16 * (i + 1)))
                for tt in range(TT):
                    dve.wait_ge(*sig["mean"].after((i, tt)))
                    stt_(xn[:, tt, :], x[:, tt, :], st[:, 26 + tt:27 + tt], lnr[:, 0, :], ALU.add, ALU.mult)\
                        .then_inc(*sig["vector step"].up())
                norm_variance(i)
                own()
                for tt in range(TT):
                    dve.wait_ge(*sig["rstd"].after((i, tt)))
                    stt_(x[:, tt, :], xn[:, tt, :], st[:, 8 + tt:9 + tt], lnr[:, 1, :], ALU.mult, ALU.add)\
                        .then_inc(*sig["x normed"].up((i, tt)))
                rests(("norm", i))

            def scale_x():
                link(ts_(x[:, :, :], x[:, :, :], ALPHA, None, ALU.mult))

            def hidden(f):
                for j in range(FT):
                    lab = ("ab", f, j)
                    dve.wait_ge(*sig["silu"].after((f, j)))
                    v = sil[:, j % 2, :]
                    tt_(v, v, at(lab)[:, S:2 * S], ALU.mult).then_inc(*read(lab))
                    dve.wait_ge(*taken(lab))
                    link(dve.tensor_copy(hT[0][:, j % 2, :], v))
                    tt_(hT[1][:, j % 2, :], v, hT[0][:, j % 2, :], ALU.subtract).then_inc(*sig["hidden"].up((f, j)))

            def soften(name, n, hb, qt, w, scale, bias, sink):
                sc = Sc[:, n % 2, :, 0:w]
                for b in range(2):
                    lab = ("s", name, hb, qt, b)
                    dve.wait_ge(*full(lab))
                    src = at(lab).rearrange("p (j c) -> p j c", j=2)[:, :, 0:w]
                    if bias is None:
                        ts_(sc[:, 2 * b:2 * b + 2, :], src, scale, None, ALU.mult).then_inc(*read(lab))
                    else:
                        stt_(sc[:, 2 * b:2 * b + 2, :], src, scale, bias(hb, b, S - w if qt == 0 else 0, w),
                             ALU.mult, ALU.add).then_inc(*read(lab))
                for b in range(2):
                    dve.wait_ge(*taken(("s", name, hb, qt, b)))
                m = st[:, 32 + 4 * (n % 2):36 + 4 * (n % 2)]
                link(dve.tensor_reduce(m, sc, AX, ALU.max))
                if sink is not None:
                    link(tt_(m, m, sink[:, 4 * hb:4 * hb + 4], ALU.max))
                    sk = st[:, 40 + 4 * (n % 2):44 + 4 * (n % 2)]
                    tt_(sk, sink[:, 4 * hb:4 * hb + 4], m, ALU.subtract).then_inc(*sig["sink shifted"].up((name, hb, qt)))
                tt_(sc, sc, m.unsqueeze(2).broadcast_to([P, 4, w]), ALU.subtract)\
                    .then_inc(*sig["shifted"].up((name, hb, qt)))

            def weigh(name, n, hb, qt, w, dv, sink, gate, first):
                dve.wait_ge(*sig["weights"].after((name, hb, qt)))
                sums, r = st[:, 48:52], st[:, 52:56]
                link(dve.tensor_reduce(sums, Sc[:, n % 2, :, 0:w], AX, ALU.add))
                if sink is not None:
                    link(tt_(sums, sums, st[:, 40 + 4 * (n % 2):44 + 4 * (n % 2)], ALU.add))
                link(dve.reciprocal(r, sums))
                if gate is not None:
                    link(tt_(r, r, gg[:, qt, :].rearrange("p (h b) -> p h b", b=3)[:, 4 * hb:4 * hb + 4, gate], ALU.mult))
                lab = ("o", name, hb, qt)
                dve.wait_ge(*full(lab))
                src = at(lab)[:, 0:4 * dv].rearrange("p (j c) -> p j c", j=4)
                o = O[:, qt, hb * 4 * dv:(hb + 1) * 4 * dv].rearrange("p (j c) -> p j c", j=4)
                rb = r.unsqueeze(2).broadcast_to([P, 4, dv])
                if first:
                    tt_(o, src, rb, ALU.mult).then_inc(*read(lab))
                else:
                    tmp = sil[:, 0, :].rearrange("p (j c) -> p j c", j=4)
                    link(tt_(tmp, src, rb, ALU.mult))
                    tt_(o, o, tmp, ALU.add).then_inc(*read(lab))

            def attention(name, hbs, dv, causal, scale, bias, before, sink=None, gate=None, first=True,
                          between=None):
                todo = [(hb, qt) for hb in range(hbs) for qt in range(TT)]
                width = lambda qt: S if (qt or not causal) else P
                for n, (hb, qt) in enumerate(todo):
                    soften(name, n, hb, qt, width(qt), scale, bias, sink)
                    if n == 1:
                        if before is not None:
                            for t in range(TT):
                                dve.wait_ge(*full(("ot", before, t)))
                        if between is not None:
                            between()
                    if n:
                        weigh(name, n - 1, *todo[n - 1], width(todo[n - 1][1]), dv, sink, gate, first)
                n = len(todo)
                weigh(name, n - 1, *todo[n - 1], width(todo[n - 1][1]), dv, sink, gate, first)

            def merge(merged):
                for br in range(3):
                    for n in range(4):
                        lab = ("wo", br, n)
                        dve.wait_ge(*full(lab))
                        src = at(lab).rearrange("p (j c) -> p j c", j=2)
                        g = G[:, 8 * br + 2 * n:8 * br + 2 * n + 2, :]
                        o = merged[:, 2 * n:2 * n + 2, :]
                        if br == 0:
                            stt_(o, g, 1.0, src, ALU.add, ALU.mult).then_inc(*read(lab))
                        else:
                            k = 4 * br + n
                            tmp = (sil[:, :, :], xn[:, 0, 0:512].rearrange("p (a b) -> p a b", a=2))[k % 2]
                            if k >= 6:
                                dve.wait_ge(*sig["merged"].after(k - 2))
                            if k >= 8:
                                dve.wait_ge(*sig["merged"].after(k - 4))
                            stt_(tmp, g, 1.0, src, ALU.add, ALU.mult).then_inc(*read(lab))
                            dve.wait_ge(*taken(lab))
                            tt_(o, o, tmp, ALU.add).then_inc(*sig["merged"].up("all" if k == 11 else k))
                            if br == 2:
                                dve.wait_ge(*sig["merged"].after("all" if k == 11 else k))
                                v = slice(2 * n, 2 * n + 2)
                                link(dve.tensor_copy(xT[0][:, v, :], o))
                                tt_(xT[1][:, v, :], o, xT[0][:, v, :], ALU.subtract).then_inc(*sig["merged parts"].up(n))

            causal_bias = lambda hb, b, c, w: CM[:, c:c + w].unsqueeze(1).broadcast_to([P, 2, w])

            with region(dve, PREP):
                dve.wait_ge(sig["consts"].sem, 16)
                dve.wait_ge(sig["positions"].sem, 16)
                an, kk, sn_, cs_, cm_ = (KT[:, i, :] for i in range(5))
                link(dve.tensor_copy(an, posi))
                link(ts_(an, an, invf, None, ALU.mult))
                link(ts_(kk, an, 1.0 / TWO_PI, ROUND, ALU.mult, ALU.add))
                link(ts_(kk, kk, ROUND, None, ALU.subtract))
                for c in PERIOD:
                    link(stt_(an, kk, -c, an, ALU.mult, ALU.add))
                link(ts_(cs_, an, TWO_PI / 4, None, ALU.add))
                link(ts_(cm_, cs_, TWO_PI / 2, -TWO_PI, ALU.is_gt, ALU.mult))
                link(tt_(cs_, cs_, cm_, ALU.add))
                link(ts_(cs_, cs_, PI_IN, -PI_IN, ALU.min, ALU.max))
                ts_(sn_, an, PI_IN, -PI_IN, ALU.min, ALU.max).then_inc(*sig["angles"].up(0))
                dve.wait_ge(*sig["sines"].after(0))
                link(ts_(sn_, sn_, sgn, None, ALU.mult))
                dve.memset(CS[0:64], 1.0).then_inc(*sig["vector step"].up())
                dve.tensor_copy(CS[64:96], cs_[64:96]).then_inc(*sig["vector step"].up())
                dve.tensor_copy(CS[96:128], sn_[96:128]).then_inc(*sig["vector step"].up())
                dve.tensor_copy(CK[:, 0, :], cs_).then_inc(*sig["vector step"].up())
                link(dve.tensor_copy(CK[:, 1, :], sn_))
                dve.wait_ge(sig["mem loaded"].sem, 16)
                norm_variance("mem")
                for tt in range(TT):
                    dve.wait_ge(*sig["rstd"].after(("mem", tt)))
                    ts_(xn[:, tt, :], memraw[:, tt, :], st[:, 8 + tt:9 + tt], None, ALU.mult)\
                        .then_inc(*sig["scaled"].up(("mem", tt)))
                for tt in range(TT):
                    for h in range(2):
                        lab = ("mem", tt, h)
                        dve.wait_ge(*full(lab))
                        dve.tensor_copy(memT[:, 4 * h:4 * h + 4, tt * P:(tt + 1) * P],
                                        at(lab).rearrange("p (q c) -> p q c", q=4)).then_inc(*read(lab))
                dve.wait_ge(sig["x loaded"].sem, 16)
                dve.wait_ge(sig["masks"].sem, 16)
                link(dve.memset(st[:, 125:126], 0.0))

            with region(dve, BLOCK1):
                rms(0)
                dve.wait_ge(*sig["params"].value(16))
                b2 = par[:, 38:46]
                m, e, s4, lb, oml = lbt[:, 0:4], lbt[:, 4:12], lbt[:, 12:16], lbt[:, 16:20], lbt[:, 20:24]
                lg, zero = lbt[:, 24:32], lbt[:, 32:40]
                link(tt_(m, b2[:, 0:4], b2[:, 4:8], ALU.max))
                link(tt_(e[:, 0:4], b2[:, 0:4], m, ALU.subtract))
                tt_(e[:, 4:8], b2[:, 4:8], m, ALU.subtract).then_inc(*sig["bounds"].up(0))
                dve.wait_ge(*sig["memory back"].value(16))
                tt_(memTg, memTg, par[:, 24:32].unsqueeze(2).broadcast_to([P, KD, S]), ALU.mult)\
                    .then_inc(*sig["memory scaled"].up(0))
                hidden(0)
                dve.wait_ge(*sig["bounds made"].after(0))
                link(tt_(s4, e[:, 0:4], e[:, 4:8], ALU.add))
                link(dve.reciprocal(s4, s4))
                link(tt_(e[:, 0:4], e[:, 0:4], s4, ALU.mult))
                link(tt_(e[:, 4:8], e[:, 4:8], s4, ALU.mult))
                link(tt_(lb, e[:, 0:4], e[:, 4:8], ALU.add))
                link(tt_(lb, lb, e[:, 0:4], ALU.subtract))
                link(ts_(lb, lb, par[:, 46:47], None, ALU.mult))
                link(ts_(oml, lb, -1.0, 1.0, ALU.mult, ALU.add))
                link(ts_(zero, lbt[:, 16:24], 0.0, NEG, ALU.is_equal, ALU.mult))
                ts_(lg, lbt[:, 16:24], 1e-18, None, ALU.max).then_inc(*sig["bounds"].up(1))
                dve.wait_ge(*sig["bounds made"].after(1))
                link(tt_(lg, lg, zero, ALU.add))
                add_sums(0)
                rms(1)
                dve.wait_ge(*sig["latent squares"].after(3))
                variance("latent", [(st[:, 16:18], st[:, 0:2], 384), (st[:, 18:20], st[:, 2:4], 256)])
                for b in range(4):
                    dve.wait_ge(*full(("c", b)))
                    t, lo, hi = b % 2, (0, 384)[b // 2], (384, 640)[b // 2]
                    ts_(cn[:, t, lo:hi], at(("c", b))[:, 0:hi - lo], st[:, 8 + b:9 + b], None, ALU.mult)\
                        .then_inc(*read(("c", b)))
                lab = ("kr", 0)
                dve.wait_ge(*full(lab))
                tt_(sil[64:128, :, :], at(lab)[64:128].rearrange("p (a b) -> p a b", a=2), CK[64:128], ALU.mult)\
                    .then_inc(*read(lab))
                dve.wait_ge(*taken(lab))
                tt_(KT[64:128, :, :], sil[64:128, 0:1, :].broadcast_to([64, 8, S]),
                    sil[64:128, 1:2, :].broadcast_to([64, 8, S]), ALU.add).then_inc(*sig["rotary keys"].up(0))
                for i in range(2):
                    lab = ("hf", i)
                    dve.wait_ge(*sig["forget read"].after(i))
                    ts_(GC[:, 2 * i:2 * i + 2, :], at(lab).rearrange("p (a b) -> p a b", a=2), 0.0, None, ALU.min)\
                        .then_inc(*read(lab))
                for i in range(2):
                    dve.wait_ge(*taken(("hf", i)))
                wide = lambda v: v.unsqueeze(2).broadcast_to([P, 4, S])
                tt_(KH, KH, wide(oml), ALU.mult).then_inc(*sig["recurrence keys"].up(0))
                for t in range(TT):
                    for h, (lo, n) in enumerate(((0, 3), (3, 2))):
                        lab = ("cT", t, h)
                        dve.wait_ge(*full(lab))
                        tt_(cT[:, lo:lo + n, t * P:(t + 1) * P], at(lab)[:, 0:n * P].rearrange("p (q c) -> p q c", q=n),
                            par[:, 32 + lo:32 + lo + n].unsqueeze(2).broadcast_to([P, n, P]), ALU.mult)\
                            .then_inc(*read(lab))
                dve.wait_ge(*sig["forget log"].after(0))
                link(tt_(GC, GC, EB[0], ALU.subtract))
                link(tt_(GC, GC, wide(lg[:, 4:8]), ALU.add))
                link(tt_(EB[1], GC, wide(lg[:, 0:4]), ALU.subtract))
                link(tt_(GC, GC, wide(lg[:, 0:4]), ALU.max))
                stt_(EB[1], EB[1], -1.0, EB[1], ALU.mult, ALU.min).then_inc(*sig["forget gap"].up(0))
                dve.wait_ge(*sig["forget log"].after(1))
                link(tt_(EB[0], GC, EB[1], ALU.add))
                for h in range(4):
                    i = dve.tensor_tensor_scan(GC[:, h, :], ones, EB[0][:, h, :], 0.0, ALU.mult, ALU.add)
                    i.then_inc(*sig["vector step"].up())
                dve.wait_ge(*sig["vector step"].value(sig["vector step"].count[places["made in"]]))
                for n in range(4):
                    lab = (("uq", n), 0)
                    dve.wait_ge(*full(lab))
                    tt_(QT[:, 2 * n:2 * n + 2, :], at(lab).rearrange("p (a b) -> p a b", a=2),
                        CS.unsqueeze(1).broadcast_to([P, 2, S]), ALU.mult).then_inc(*read(lab))

                def halves(t, i):
                    v = t.rearrange("p h t -> p (h t)").rearrange("p (n w) -> p n w", w=2 << i)
                    return v[:, :, 0:1 << i], v[:, :, 1 << i:2 << i]

                def gaps(i):
                    g0, g1 = halves(GC, i)
                    e0, e1 = halves(EB[i % 2], i)
                    if i >= 2:
                        dve.wait_ge(*sig["decayed"].after(i - 2))
                        own()
                    mid = g0[:, :, (1 << i) - 1:1 << i].broadcast_to(list(g0.shape))
                    tt_(e0, mid, g0, ALU.subtract).then_inc(*sig["gaps"].up((i, 0)))
                    tt_(e1, g1, mid, ALU.subtract).then_inc(*sig["gaps"].up((i, 1)))

                def decayed(i):
                    dve.wait_ge(*sig["decays"].after(i))
                    if i >= 2:
                        dve.wait_ge(*full(("level", i - 2, 1)))
                    e0, e1 = halves(EB[i % 2], i)
                    t0, t1 = halves(TL[i % 2], i)
                    tt_(t0, e0, halves(KH, i)[0], ALU.mult).then_inc(*sig["vector step"].up())
                    tt_(t1, e1, halves(QH, i)[1], ALU.mult).then_inc(*sig["decayed"].up(i))

                def chosen(i):
                    for t in range(2 if i < 7 else 1):
                        lab = ("level", i, t)
                        dve.wait_ge(*full(lab))
                        src = at(lab).rearrange("p (h c) -> p h c", h=4)
                        if i < 7:
                            dve.wait_ge(*taken(("diag", t) if i == 0 else ("level", i - 1, t)))
                            c = 128 + 2 * i + t
                            dve.tensor_copy(st[:, c:c + 1], st[:, 125:126])
                            dve.copy_predicated(Am[:, t], MASK[:, i:i + 1, :].broadcast_to([P, 4, P]), src)\
                                .then_inc(*read(lab))
                        else:
                            dve.tensor_copy(Aoff, src).then_inc(*read(lab))

                dve.wait_ge(*sig["recurrence keys"].after(0))
                for i in range(2):
                    dve.wait_ge(*taken(("hq", i)))
                gaps(0)
                for t in range(TT):
                    lab = ("diag", t)
                    dve.wait_ge(*full(lab))
                    tt_(Am[:, t], at(lab).rearrange("p (h c) -> p h c", h=4),
                        ident.unsqueeze(1).broadcast_to([P, 4, P]), ALU.mult).then_inc(*read(lab))
                    dve.wait_ge(*taken(lab))
                for i in range(1, 10):
                    if i < 8:
                        gaps(i)
                    if i <= 8:
                        decayed(i - 1)
                    if i >= 2:
                        chosen(i - 2)
                for t in range(TT):
                    dve.wait_ge(*sig["out squares"].after(t))
                    link(dve.tensor_reduce(st[:, 64 + 4 * t:68 + 4 * t], O[:, t, :].rearrange("p (h c) -> p h c", h=4),
                                           AX, ALU.add))
                variance("recurrence", [(st[:, 64:72], st[:, 0:8], P)])
                for t in range(TT):
                    lab = ("ho", t)
                    tt_(O[:, t, :].rearrange("p (h c) -> p h c", h=4), at(lab).rearrange("p (h c) -> p h c", h=4),
                        st[:, 8 + 4 * t:12 + 4 * t].unsqueeze(2).broadcast_to([P, 4, P]), ALU.mult).then_inc(*read(lab))
                    dve.wait_ge(*taken(lab))
                    dve.wait_ge(*taken(("hgate", t)))
                    tt_(GH[:, t, :], O[:, t, :], GH[:, t, :], ALU.mult).then_inc(*sig["recurrence out"].up(t))
                attention("mla", 2, 64, True, 96.0 ** -0.5, causal_bias, None)

                def recurrence_turned():
                    for t in range(TT):
                        lab = ("ot", "hg", t)
                        dve.wait_ge(*full(lab))
                        ts_(OT[:, 1, :, t * P:(t + 1) * P], at(lab).rearrange("p (q c) -> p q c", q=4), par[:, 37:38],
                            None, ALU.mult).then_inc(*read(lab))

                attention("mem", 1, P, False, 128.0 ** -0.5, None, "mla", between=recurrence_turned)
                merge(mergedA)
                add_sums("mix")
                rms(2)
                hidden(1)
                add_sums(1)

            with region(dve, BETWEEN):
                norm_variance("final")
                dve.wait_ge(*sig["rows"].value(0))
                for tt in range(TT):
                    dve.wait_ge(*sig["rstd"].after(("final", tt)))
                    stt_(x[:, tt, :], x[:, tt, :], st[:, 8 + tt:9 + tt], lnr[:, 0, :], ALU.mult, ALU.mult)\
                        .then_inc(*sig["x normed"].up(("final", tt)))
                dve.wait_ge(*sig["rel tables"].value(48))
                dve.wait_ge(*full("rel"))
                tt_(relsum, at("rel")[0:16, :], relmask, ALU.add).then_inc(*read("rel"))
                dve.wait_ge(*taken("rel"))
                ts_(relsum, relsum, 0.0, None, ALU.add).then_inc(*sig["rel summed"].up(0))
                dve.wait_ge(*full("rel cmp"))
                src = at("rel cmp")[:, 0:240].rearrange("p (q c h) -> p q h c", q=2, c=15)
                for qt in range(TT):
                    i = tt_(CB[:, qt], src[:, qt], cmask[:, 15 * qt:15 * qt + 15].unsqueeze(1).broadcast_to([P, 8, 15]),
                            ALU.add)
                    i.then_inc(*(read("rel cmp") if qt else sig["vector step"].up()))
                rests(("norm", "final"))

            with region(dve, BLOCK2):
                dve.wait_ge(*sig["params"].value(16))
                dve.wait_ge(*sig["x normed"].value(0))
                for b in range(2):
                    dve.wait_ge(*sig[f"A{b} read"].value(0))
                for h in range(2):
                    dve.wait_ge(*sig[f"T{h} read"].value(0))
                scale_x()
                hidden(0)
                layer_norm(0, 0)
                scale_x()
                hb = st[:, 96:120]
                ts_(hb, par[:, 0:24], 0.5, None, ALU.mult).then_inc(*sig["half gate bias"].up(0))
                dve.wait_ge(sig["cleared"].sem, 6)
                two = lambda lab: at(lab).rearrange("p (a b) -> p a b", a=2)

                def both_halves(lab, lo, hi):
                    dve.wait_ge(*full(lab))
                    dve.tensor_copy(lo[0:64], two(lab)[0:64]).then_inc(*sig["vector step"].up())
                    dve.tensor_copy(hi[64:128], two(lab)[64:128]).then_inc(*read(lab))

                def compress_blocks(z, lab, pe_cols):
                    dve.wait_ge(*full(lab))
                    link(dve.tensor_copy(Z2[0:64, :, :], two(lab)[0:64]))
                    dve.tensor_copy(Z2[64:128, :, 0:S - 1], two(lab)[64:128, :, 1:S]).then_inc(*read(lab))
                    dve.wait_ge(*taken(lab))
                    if z == "v":
                        dve.wait_ge(*full(("cmp", "k", 1)))
                    for g in range(2):
                        zz = Z2[:, g, :]
                        src = bass.AP(zz.tensor, zz.offset, [zz.ap[0], (2, 16), (16, 15)])
                        i = tt_(ZB[:, :, 15 * g:15 * g + 15], src, pe_cols.unsqueeze(2).broadcast_to([P, 16, 15]), ALU.add)
                        i.then_inc(*(sig["blocks"].up(z) if g else sig["vector step"].up()))

                both_halves(("ks", 0), KS[:, :, 0, :], KS[:, :, 1, :])
                both_halves(("kw", 0), KW[:, :, 0, :], KW[:, :, 1, :])
                compress_blocks("k", ("kc", 0), par[:, 24:40])
                lab = ("vc", 0)
                dve.wait_ge(*full(lab))
                dve.wait_ge(*sig["blocks"].after("k"))
                link(dve.tensor_copy(Z2[0:64, :, :], two(lab)[0:64]))
                dve.tensor_copy(Z2[64:128, :, 0:S - 1], two(lab)[64:128, :, 1:S]).then_inc(*read(lab))
                dve.wait_ge(*taken(lab))
                both_halves(("kb", 0), KB[:, :, 0, :], KB[:, :, 1, :])
                fz, fm, fc = (FS[0:8, i, :] for i in range(3))
                dve.wait_ge(*full("f"))
                ts_(fz, at("f")[0:8, 0:S], par[0:8, 440:441], None, ALU.add).then_inc(*read("f"))
                dve.wait_ge(*taken("f"))
                link(ts_(fm, fz, 0.0, None, ALU.min))
                stt_(fz, fz, -1.0, fz, ALU.mult, ALU.min).then_inc(*sig["fox gap"].up(0))
                dve.wait_ge(*sig["fox log"].after(0))
                link(tt_(fm, fm, fz, ALU.subtract))
                link(dve.tensor_tensor_scan(fc, ones[0:8], fm, 0.0, ALU.mult, ALU.add))
                link(ts_(CF[0:8, 0, :], fc, 8.0, None, ALU.mult))
                ts_(CF[0:8, 1, :], fc, -8.0, None, ALU.mult).then_inc(*sig["decay sums"].up(0))
                for n in range(2):
                    both_halves(("kf", n), KF[:, 2 * n:2 * n + 2, 0, :], KF[:, 2 * n:2 * n + 2, 1, :])
                dve.wait_ge(*full(("cmp", "k", 1)))
                for g in range(2):
                    zz = Z2[:, g, :]
                    src = bass.AP(zz.tensor, zz.offset, [zz.ap[0], (2, 16), (16, 15)])
                    i = tt_(ZB[:, :, 15 * g:15 * g + 15], src, par[:, 40:56].unsqueeze(2).broadcast_to([P, 16, 15]), ALU.add)
                    i.then_inc(*(sig["blocks"].up("v") if g else sig["vector step"].up()))
                lab = ("cmp out", "k")
                dve.wait_ge(*full(lab))
                dve.tensor_copy(KC[0:64, 0, :], at(lab)[0:64, 0:30]).then_inc(*sig["vector step"].up())
                dve.tensor_copy(KC[64:128, 1, :], at(lab)[64:128, 0:30]).then_inc(*read(lab))
                lab = ("cmp out", "v")
                dve.wait_ge(*full(lab))
                dve.tensor_copy(VC[0:15, :, :], at(lab)[0:15, 0:128].rearrange("p (g c) -> p g c", g=2))\
                    .then_inc(*read(lab))
                dve.wait_ge(*sig["small gates"].after(1))
                link(ts_(gg, gg, 0.5, 0.5, ALU.mult, ALU.add))
                for qt in range(TT):
                    lab = ("sc", qt)
                    sc = scf[:, qt * 1024:qt * 1024 + 120].rearrange("p (h c) -> p h c", h=8)
                    dve.wait_ge(*full(lab))
                    stt_(sc, at(lab)[:, 0:120].rearrange("p (h c) -> p h c", h=8), 0.125, CB[:, qt], ALU.mult, ALU.add)\
                        .then_inc(*read(lab))
                    dve.wait_ge(*taken(lab))
                    m = st[:, 56 + 32 * qt:64 + 32 * qt]
                    link(dve.tensor_reduce(m, sc, AX, ALU.max))
                    link(ts_(m, m, LOW, None, ALU.max))
                    tt_(sc, sc, m.unsqueeze(2).broadcast_to([P, 8, 15]), ALU.subtract)\
                        .then_inc(*sig["shifted"].up(("cmp", qt)))
                for qt in range(TT):
                    dve.wait_ge(*sig["weights"].after(("cmp", qt)))
                    sc = scf[:, qt * 1024:qt * 1024 + 120].rearrange("p (h c) -> p h c", h=8)
                    r = st[:, 72 + 8 * qt:80 + 8 * qt]
                    link(dve.tensor_reduce(r, sc, AX, ALU.add))
                    link(ts_(r, r, 1e-30, None, ALU.max))
                    link(dve.reciprocal(r, r))
                    link(tt_(r, r, gg[:, qt, :].rearrange("p (h b) -> p h b", b=3)[:, :, 0], ALU.mult))
                    lab = ("o", "cmp", 0, qt)
                    dve.wait_ge(*full(lab))
                    tt_(O[:, qt, :].rearrange("p (h c) -> p h c", h=8), at(lab).rearrange("p (h c) -> p h c", h=8),
                        r.unsqueeze(2).broadcast_to([P, 8, 64]), ALU.mult).then_inc(*read(lab))
                    dve.wait_ge(*taken(lab))
                dve.wait_ge(*sig["A1 read"].value(0))
                table = lambda h0: (lambda hb, b, c, w: BIAS[:, h0 + 4 * hb + 2 * b:h0 + 4 * hb + 2 * b + 2, c:c + w])
                attention("slc", 2, 64, True, 0.125, table(0), None, gate=1, first=False)
                attention("win", 2, 64, True, 0.125, table(0), None, gate=2, first=False)
                attention("swa", 2, 64, True, 0.125, table(8), "nsa", sink=par[:, 441:449])
                attention("fox", 2, 64, True, 0.125, causal_bias, "swa")
                merge(mergedB)
                layer_norm(1, "mix")
                scale_x()
                hidden(1)
                layer_norm(2, 1)

        @block.scalar
        def _(act):
            def go(out, in_, func, up, **kw):
                act.activation(out, in_, func, **kw).then_inc(*up)

            def step():
                return sig["scalar step"].up()

            def linked():
                act.wait_ge(*sig["scalar step"].value(sig["scalar step"].count[places["made in"]]))

            def squares(i, src, bias=None, after=None):
                junk = xn if bias is None else G[:, 16:24, :].rearrange("p a b -> p (a b)")\
                    .rearrange("p (t d) -> p t d", t=TT)
                for tt in range(TT):
                    if bias is not None:
                        act.wait_ge(*sig["mean"].after((i, tt)))
                    if after is not None:
                        for b in (2 * tt, 2 * tt + 1):
                            act.wait_ge(*(sig[f"Y{b} read"].value(0) if after == () else taken(after + (b,))))
                    kw = {} if bias is None else {"bias": bias[:, tt:tt + 1]}
                    act.activation(junk[:, tt, :], src[:, tt, :], ACT.Square, accum_out=st[:, 16 + tt:17 + tt], **kw)\
                        .then_inc(*sig["square sum"].up((i, tt)))

            state = {"split": 0}

            def split(h):
                free_ = parts_free(h)
                if free_ is not None:
                    act.wait_ge(*free_)
                act.wait_ge(*loaded(h))
                r, n = h % R, width(h)
                go(upper[:, r, 0:n], ring[:, r, 0:n], ACT.Copy, sig["upper parts"].up(h))

            def until(h):
                ahead(act, state, h, split)

            def uppers(label):
                for tt in range(TT):
                    for h in range(2):
                        lab = label + (tt, h)
                        act.wait_ge(*full(lab))
                        go(xT[0][:, 4 * h:4 * h + 4, tt * P:(tt + 1) * P], at(lab).rearrange("p (q c) -> p q c", q=4),
                           ACT.Copy, sig["residual's upper parts"].up(lab))

            def hidden(f):
                for j in range(FT):
                    lab = ("ab", f, j)
                    until((0, AFTER_MIX)[f] + max(1, 3 * j))
                    act.wait_ge(*full(lab))
                    if j >= 2:
                        act.wait_ge(*sig["hidden"].after((f, j - 2)))
                    go(sil[:, j % 2, :], at(lab)[:, 0:S], ACT.Silu, sig["silu"].up((f, j)))
                until((FFN_PIECES - 1, PIECES - 1)[f])

            def copy(lab, out, n=None, func=ACT.Copy, piece=None, **kw):
                if piece is not None:
                    until(piece)
                act.wait_ge(*full(lab))
                src = at(lab)
                if len(out.shape) == 3:
                    src = src[0:out.shape[0], 0:out.shape[1] * out.shape[2]].rearrange("p (a b) -> p a b", a=out.shape[1])
                else:
                    src = src[0:out.shape[0], 0:out.shape[1]]
                go(out, src, func, read(lab), **kw)

            def gate_out(pieces):
                for n in pieces:
                    until(gate_piece(n))
                    if n % 2 == 0:
                        continue
                    n = n // 2
                    lab = ("gate", n)
                    if places["made in"] == BLOCK1:
                        copy(lab, G[:, 2 * n:2 * n + 2, :], func=ACT.Tanh, scale=0.5)
                        continue
                    if n == 0:
                        act.wait_ge(*sig["half gate bias"].after(0))
                    act.wait_ge(*full(lab))
                    for j in range(2):
                        i = 2 * n + j
                        go(G[:, i, :], at(lab)[:, j * S:(j + 1) * S], ACT.Tanh, read(lab) if j else step(),
                           bias=st[:, 96 + i:97 + i], scale=0.5)

            def attention(name, hbs, causal, sink=False, between=None):
                start = gates((name, "start"))
                gate_out(start[:-2])
                todo = [(hb, qt) for hb in range(hbs) for qt in range(TT)]
                for n, (hb, qt) in enumerate(todo):
                    kts = TT if (qt or not causal) else 1
                    if sink:
                        act.wait_ge(*sig["sink shifted"].after((name, hb, qt)))
                        sk = st[:, 40 + 4 * (n % 2):44 + 4 * (n % 2)]
                        go(sk, sk, ACT.Exp, step())
                    act.wait_ge(*sig["shifted"].after((name, hb, qt)))
                    sc = Sc[:, n % 2, :, 0:kts * P]
                    if sink:
                        linked()
                    go(sc, sc, ACT.Exp, sig["weights"].up((name, hb, qt)))
                    if n == 0:
                        gate_out(start[-2:])
                        if between is not None:
                            between()
                    for kt in range(kts):
                        copy(("pt", name, hb, qt, kt), PT[:, n % 2, kt, :, :])
                    gate_out(gates((name, n)))

            def turned(name, br):
                for qt in range(TT):
                    copy(("ot", name, qt), OT[:, br, :, qt * P:(qt + 1) * P])

            with region(act, PREP):
                act.wait_ge(sig["mem loaded"].sem, 16)
                squares("mem", memraw)
                act.wait_ge(*sig["angles"].after(0))
                go(KT[:, 2, :], KT[:, 2, :], ACT.Sin, step())
                go(KT[:, 3, :], KT[:, 3, :], ACT.Sin, sig["sines"].up(0))
                until(0)
                act.wait_ge(sig["x loaded"].sem, 16)
                for h in range(2):
                    act.wait_ge(*full(("mem", 1, h)))

            with region(act, BLOCK1):
                squares(0, x, after=())
                state["split"] = R
                uppers(("norm", 0))
                lb_e, lb_g = lbt[:, 4:12], lbt[:, 24:32]
                act.wait_ge(*sig["bounds"].after(0))
                go(lb_e, lb_e, ACT.Exp, sig["bounds made"].up(0))
                hidden(0)
                act.wait_ge(*sig["bounds"].after(1))
                go(lb_g, lb_g, ACT.Ln, sig["bounds made"].up(1))
                squares(1, x, after=("y", 0))
                for n in range(2):
                    copy(("mk", n), KM[:, 2 * n:2 * n + 2, :], piece=67 + 2 * n)
                for t in range(TT):
                    copy(("mv", t), VX[:, t, :], piece=73)
                uppers(("norm", 1))
                until(FFN_PIECES + 15)
                for b in range(4):
                    act.wait_ge(*full(("c", b)))
                    t, lo, hi = b % 2, (0, 384)[b // 2], (384, 640)[b // 2]
                    if b == 0:
                        for h in range(2):
                            act.wait_ge(*taken(("norm", 1, 1, h)))
                    act.activation(cn[:, t, lo:hi], at(("c", b))[:, 0:hi - lo], ACT.Square,
                                   accum_out=st[:, 16 + b:17 + b]).then_inc(*sig["latent squares"].up(b))
                for n in range(2):
                    copy(("mq", n), QM[:, 2 * n:2 * n + 2, :], piece=85 + 2 * n)
                for n in range(2):
                    copy(("hq", n), QH[:, 2 * n:2 * n + 2, :], func=ACT.Silu, piece=FFN_PIECES + 23 + 2 * n)
                for n in range(2):
                    lab = ("hf", n)
                    until(93 + 2 * n)
                    act.wait_ge(*full(lab))
                    v = at(lab).rearrange("p (a b) -> p a b", a=2)
                    go(KH[:, 2 * n:2 * n + 2, :], v, ACT.Sigmoid, step(), scale=-1.0)
                    go(EB[0][:, 2 * n:2 * n + 2, :], v, ACT.Abs, sig["forget read"].up(n))
                for t in range(TT):
                    copy(("hi", t), VH[:, t, :], piece=FFN_PIECES + 33)
                for t in range(TT):
                    copy(("hgate", t), GH[:, t, :], func=ACT.Silu, piece=103)
                act.wait_ge(*sig["forget read"].after(1))
                go(EB[0], EB[0], ACT.Exp, step(), scale=-1.0)
                linked()
                go(EB[0], EB[0], ACT.Ln, sig["forget log"].up(0), bias=1.0)
                gate_out([0, 1])
                act.wait_ge(*sig["forget gap"].after(0))
                go(EB[1], EB[1], ACT.Exp, step())
                linked()
                go(EB[1], EB[1], ACT.Ln, sig["forget log"].up(1), bias=1.0)
                gate_out([2, 3])
                for n in range(4):
                    copy(("uk", n), KT[0:64, 2 * n:2 * n + 2, :])
                for t in range(TT):
                    copy(("uv", t), VM[:, t, :])
                for i in range(8):
                    act.wait_ge(*sig["gaps"].after((i, 1)))
                    go(EB[i % 2], EB[i % 2], ACT.Exp, sig["decays"].up(i))
                    gate_out(gates(("level", i)))
                gate_out(gates(("ho", 0)))
                for t in range(TT):
                    act.wait_ge(*full(("ho", t)))
                    go(O[:, t, :], at(("ho", t)), ACT.Square, sig["out squares"].up(t))
                attention("mla", 2, True)
                attention("mem", 1, False, between=lambda: turned("mla", 0))
                turned("mem", 2)
                until(AFTER_MIX - 2)
                squares(2, x, after=("y", "mix"))
                uppers(("norm", 2))
                hidden(1)
                until(PIECES)

            with region(act, BETWEEN):
                squares("final", x, after=())
                uppers(("norm", "final"))
                for n in range(8):
                    copy(("flip", n), BIAS[:, 2 * n:2 * n + 2, :])

            with region(act, BLOCK2):
                state["split"] = R
                hidden(0)
                squares(0, x, st[:, 26:28])
                uppers(("norm", 0))
                for n in range(2):
                    copy(("qa", n), QA[:, 2 * n:2 * n + 2, :], piece=67 + 2 * n)
                for n in range(2):
                    copy(("qb", n), QB[:, 2 * n:2 * n + 2, :], piece=79 + 2 * n)
                for t in range(TT):
                    copy(("vt", t), VT[:, t, :], piece=87)
                for t in range(TT):
                    act.wait_ge(*taken(("vt", t)))
                    go(gg[:, t, :], VT[:, t, 384:408], ACT.Tanh, sig["small gates"].up(t), scale=0.5)
                fz = FS[0:8, 0, :]
                act.wait_ge(*sig["fox gap"].after(0))
                go(fz, fz, ACT.Exp, step())
                linked()
                go(fz, fz, ACT.Ln, sig["fox log"].up(0), bias=1.0)
                for n in range(2):
                    copy(("qf", n), QF[:, 2 * n:2 * n + 2, :], piece=89 + 2 * n)
                for t in range(TT):
                    copy(("vf", t), VF[:, t, :], piece=99)
                for z in ("k", "v"):
                    if z == "v":
                        act.wait_ge(*full(("cmp out", "k")))
                    for m in range(2):
                        n = 4 * (z == "v") + 2 * m
                        copy(("cmp", z, m), HC[:, m, :], func=ACT.Gelu_apprx_tanh, piece=gate_piece(n + 1) - 1)
                        gate_out([n, n + 1])
                for qt in range(TT):
                    act.wait_ge(*sig["shifted"].after(("cmp", qt)))
                    sc = scf[:, qt * 1024:qt * 1024 + 120]
                    go(sc, sc, ACT.Exp, sig["weights"].up(("cmp", qt)))
                gate_out(gates(("sc", 0)))
                for qt in range(TT):
                    for b in range(2):
                        copy(("ptc", qt, b), PT[0:15, qt, b, :, :])
                attention("slc", 2, True)
                attention("win", 2, True)
                attention("swa", 2, True, sink=True, between=lambda: turned("nsa", 0))
                attention("fox", 2, True, between=lambda: turned("swa", 1))
                turned("fox", 2)
                until(AFTER_MIX - 2)
                squares(1, x, st[:, 26:28])
                uppers(("norm", 1))
                hidden(1)
                until(PIECES)
                squares(2, x, st[:, 26:28])
                uppers(("norm", 2))

        for b in BANK:
            for r in range(len(ITERATIONS)):
                put, got = ({k[1] for k in sig[b + w].labels if k[0] == r} for w in (" full", " read"))
                assert put == got, (b, r, put ^ got)
        return sig.counts()


TWO_PI = 2.0 * float(np.pi)
ROUND = 1.5 * 2.0 ** 23
PERIOD = (6.28125, float(np.float32(2 * np.pi - 6.28125)) - float(np.float32(2 * np.pi - 6.28125)) % 2.0 ** -20,)
PERIOD += (float(np.float32(2 * np.pi - PERIOD[0] - PERIOD[1])),)
PI_IN = float(np.nextafter(np.float32(np.pi), np.float32(0)))
ALPHA = (2 * DEPTH) ** 0.25


def tiles(w, cols=None):
    w = w if cols is None else w[:, cols]
    return w.reshape(-1, P, w.shape[1]).transpose(1, 0, 2)


def stream(i):
    out = np.zeros((2 * DEPTH * PIECES + R, P, PIECE), np.float32)
    at = [0]

    def put(*parts):
        c = 0
        for v in parts:
            n = v[0].size
            out[at[0], :, c:c + n].reshape(v.shape, copy=False)[...] = v
            c += n
        at[0] += 1

    def by_columns(w, width=P):
        t = tiles(w)
        for c in range(0, w.shape[1], width):
            put(t[:, :, c:c + width])

    def by_rows(w, n):
        t = tiles(w)
        for k in range(0, t.shape[1], n):
            put(t[:, k:k + n])

    def ffn(w1, w2):
        t1, t2 = tiles(w1), tiles(w2)
        for j in range(FT):
            put(t1[:, :, j * P:(j + 1) * P])
            put(t1[:, :, F + j * P:F + (j + 1) * P])
            if j:
                put(t2[:, j - 1])
        put(t2[:, FT - 1])

    for l in range(DEPTH):
        ffn(i["w_ffn1_in"][l], i["w_ffn1_out"][l])
        kv = i["w_mem_kv"][l]
        by_columns(kv[:, :512])
        by_rows(kv[:, 512:], 2)
        w = i["w_in"][l]
        cuts = np.cumsum([0, 384, 256, 32, 512, 512, 512, 512, 512, 3072])
        lat, kr, hq, hf, hi, hg, mq, gate = (w[:, p:q] for p, q in zip(
            [0, *cuts[2:9]], [cuts[2], *cuts[3:]]))
        by_rows(lat, 1)
        swap = np.concatenate([kr[:, 16:], kr[:, :16]], 1)
        zeros = np.zeros((D, 64), np.float32)
        put(tiles(np.concatenate([zeros, kr, kr], 1)))
        put(tiles(np.concatenate([zeros, swap, swap], 1)))
        by_columns(mq)
        by_columns(hq)
        by_columns(hf)
        by_rows(hi, 2)
        by_rows(hg, 2)
        by_columns(gate[:, 0:4 * P])
        q = i["w_uq"][l].reshape(384, 8, 96)
        q = np.concatenate([q, q[:, :, 80:96], q[:, :, 64:80]], 2).reshape(384, 1024)
        by_columns(q, 256)
        put(tiles(i["w_uk"][l]))
        put(tiles(i["w_uv"][l]))
        by_columns(gate[:, 4 * P:])
        for n in ("w_o_mla", "w_o_hg", "w_o_mem"):
            by_columns(i[n][l], 256)
        by_rows(i["w_out"][l], 1)
        ffn(i["w_ffn2_in"][l], i["w_ffn2_out"][l])
        assert at[0] == (l + 1) * PIECES
    for l in range(DEPTH):
        ffn(i["ffn1_w1_2"][l], i["ffn1_w2_2"][l])
        w = i["w_in_2"][l]
        cuts = np.cumsum([0, 512] + [128] * 6 + [24, 512, 128, 128, 512, 512, 512, 8])
        (qa, kc, vc, ks, vs, kw, vw, ga, qb, kb, vb, qc, kx, vx, f) = (w[:, p:q] for p, q in zip(cuts, cuts[1:]))
        twice = lambda v: np.concatenate([v[:, :64], v[:, :64], v[:, 64:], v[:, 64:]], 1)
        by_columns(qa)
        for v in (ks, kw, kc, vc):
            by_columns(twice(v))
        by_columns(qb)
        by_columns(twice(kb))
        by_rows(np.concatenate([vs, vw, vb, ga, f], 1), 2)
        by_columns(qc)
        by_columns(kx)
        by_rows(vx, 2)
        gate, g = tiles(i["w_gate_2"][l]), 0
        for n in ("cmp_k_w1_2", "cmp_v_w1_2"):
            t = tiles(i[n][l])
            for c in range(0, 256, P):
                for k in range(0, 16, 8):
                    put(t[:, k:k + 8, c:c + P])
                    put(gate[:, :, g:g + P])
                    g += P
        by_columns(i["w_gate_2"][l][:, g:])
        at[0] += 2
        for n in ("w_br_a_2", "w_br_b_2", "w_br_c_2"):
            by_columns(i[n][l], 256)
        by_rows(i["w_out_2"][l], 1)
        ffn(i["ffn2_w1_2"][l], i["ffn2_w2_2"][l])
        assert at[0] == (l + 1 + DEPTH) * PIECES
    return out


def params(i):
    out = np.zeros((2 * DEPTH, P, NP_COLS), np.float32)
    col = lambda v: v.reshape(-1, P).T
    for l in range(DEPTH):
        o = out[l]
        o[:, 0:8], o[:, 8:16], o[:, 16:24] = col(i["ffn1_norm"][l]), col(i["mix_norm"][l]), col(i["ffn2_norm"][l])
        o[:, 24:32], o[:, 32:35], o[:, 35:37] = col(i["mem_norm"][l]), col(i["q_lat_norm"][l]), col(i["kv_lat_norm"][l])
        o[:, 37:38], o[:, 38:42], o[:, 42:46] = (col(i["hg_out_norm"][l]), col(i["hg_lower_bounds"][0]),
                                                 col(i["hg_lower_bounds"][1]))
        o[:, 46] = float(l > 0)
        o = out[DEPTH + l]
        o[:, 0:24] = col(i["b_gate_2"][l])
        o[:, 24:40], o[:, 40:56] = col(i["cmp_pe_k_2"][l]), col(i["cmp_pe_v_2"][l])
        w = i["cmp_k_w2_2"][l]
        o[:, 56:312] = tiles(np.concatenate([w, w], 1)).reshape(P, 256)
        o[:, 312:440] = tiles(i["cmp_v_w2_2"][l]).reshape(P, 128)
        o[0:8, 440] = i["fox_b_f_2"][l]
        o[:, 441:449] = i["swa_sinks_2"][l][None, :]
    return out


def constants():
    c = np.zeros((P, NC_COLS), np.float32)
    q, j = np.arange(P)[:, None], np.arange(S)[None, :]
    c[:, 0:128] = np.eye(P)
    c[:, 128:384] = np.where(P + q - j >= 0, 0.0, NEG)
    c[:, 384:640] = 1.0
    freq = np.float32(10000.0) ** (-np.arange(0, 32, 2, dtype=np.float32) / np.float32(32))
    c[:, 640] = np.tile(freq, 8)
    c[:, 641] = np.tile(np.repeat([-1.0, 1.0], 16), 4)
    c[:, 642:650] = -0.5
    c[:, 712:840] = np.eye(P)[::-1]
    for qt in range(TT):
        c[:, 680 + 15 * qt:695 + 15 * qt] = np.where(qt * P + q >= 16 * np.arange(15)[None] + 31, 0.0, NEG)
    s, t = np.arange(P)[:, None], np.arange(P)[None, :]
    masks = np.stack([(s // (2 << i) == t // (2 << i)) & (s % (2 << i) < 1 << i) & (t % (2 << i) >= 1 << i)
                      for i in range(7)], 1).astype(np.int32).reshape(P, 7 * P)

    def bucket(dist):
        n = np.maximum(dist, 0)
        ratio = (np.log(np.maximum(n, 1).astype(np.float32) / np.float32(16)) / np.float32(np.log(128 / 16)))
        large = 16 + (ratio.astype(np.float32) * 16).astype(np.int32)
        return np.where(n < 16, n, np.minimum(large, 31))

    forward = np.arange(512) - 256
    hot = lambda d: (bucket(d)[None, :] == np.arange(32)[:, None]).astype(np.float32)
    onehots = np.concatenate([hot(forward), hot(-forward)], 1)
    d = -forward
    relmask = np.zeros((16, 512), np.float32)
    relmask[:, d < 0] = NEG
    relmask[8:, d >= 128] = NEG
    return {"consts": c, "masks": masks, "onehots": onehots, "relmask": relmask}


def kernel(**inputs):
    from concourse import bacc
    from concourse.bass_utils import run_bass_kernel_spmd

    i = {k: np.asarray(v) for k, v in inputs.items()}
    arrays = {
        "x": i["x"].reshape(S, D), "mem": i["mem"].reshape(S, D), "pos": i["positions"].reshape(1, S),
        "weights": stream(i), "params": params(i),
        "rows": np.concatenate([
            np.stack([i[n][l], i[n][l]])[None] for l in range(DEPTH) for n in ("ffn1_norm", "mix_norm", "ffn2_norm")] + [
            np.stack([i["final_norm"], i["final_norm"]])[None]] + [
            np.stack([i[f"ln{n}_{p}_2"][l] for p in "gb"])[None] for l in range(DEPTH) for n in (1, 2, 3)]),
        "relb": i["rel_bias_2"], **constants(),
    }
    new = lambda: bacc.Bacc("TRN2", target_bir_lowering=False, num_devices=1)
    nc = new()
    build(nc, declare(nc), new)
    r = run_bass_kernel_spmd(nc, [{"in_" + n: np.ascontiguousarray(v) for n, v in arrays.items()}], core_ids=[0])
    return r.results[0]["out_x"].reshape(1, S, D)
```
